# Optimizing a Trainium2 kernel written in Bass

```python
import jax, jax.numpy as jnp
from jax import lax
import numpy as np

D_MODEL = 1024
BATCH = 1
SEQ = 1024
DEPTH = 1
DEC_BATCH = 8
DEC_SEQ = 1
PAST_LEN = 1024
PAGE_SIZE = 128

M_HEADS = 4
M_DQK = 64
M_DV = 128
M_CHUNK = 64
GATE_CAP = 15.0
N_HEADS = 8
N_KV = 2
HEAD_DIM = 64
HPG = N_HEADS // N_KV
CMP_BLOCK = 32
SEL_BLOCK = 64
TOP_K = 16
WINDOW = 512
Q_BLOCK = 128
ROPE_DIM = HEAD_DIM // 4
ROPE_THETA = 500000.0
D_FF = ((8 * D_MODEL // 3 + 255) // 256) * 256
EPS = 1e-6
NEG = -1e30

MQK = M_HEADS * M_DQK
MV = M_HEADS * M_DV
NQ = N_HEADS * HEAD_DIM
NKV = N_KV * HEAD_DIM
SPLITS = (('mq', MQK), ('mk', MQK), ('mv', MV), ('mo', MV), ('mi', M_HEADS), ('mf', M_HEADS),
          ('nq', NQ), ('nkv', 6 * NKV), ('ng', 3 * N_HEADS), ('ga', D_MODEL), ('gb', D_MODEL))
D_IN = sum(n for _, n in SPLITS)

kernel_name = 'hybrid_mlstm_nsa_decode_step'

def rms_norm(x, g):
    xf = x.astype(jnp.float32)
    y = xf * lax.rsqrt(jnp.mean(xf * xf, axis=-1, keepdims=True) + EPS)
    return (y * g.astype(jnp.float32)).astype(x.dtype)

def rope(x, pos):
    half = ROPE_DIM // 2
    inv = ROPE_THETA ** (-jnp.arange(half, dtype=jnp.float32) * 2.0 / ROPE_DIM)
    ang = pos.astype(jnp.float32)[:, None] * inv[None, :]
    cos = jnp.cos(ang)[:, None, :]
    sin = jnp.sin(ang)[:, None, :]
    xr = x[..., :ROPE_DIM].astype(jnp.float32)
    x1, x2 = xr[..., :half], xr[..., half:]
    rot = jnp.concatenate([x1 * cos - x2 * sin, x2 * cos + x1 * sin], axis=-1)
    return jnp.concatenate([rot.astype(x.dtype), x[..., ROPE_DIM:]], axis=-1)

def masked_softmax(s, mask):
    s = jnp.where(mask, s.astype(jnp.float32), NEG)
    p = jax.nn.softmax(s, axis=-1)
    return jnp.where(mask, p, 0.0)

def project(h, w_in, b_in):
    proj = h @ w_in + b_in
    offs = [int(o) for o in np.cumsum([n for _, n in SPLITS])[:-1]]
    return dict(zip([nm for nm, _ in SPLITS], jnp.split(proj, offs, axis=-1)))

def mlstm_chunkwise(q, k, v, i_pre, log_f, C0, n0, m0):
    B, L = q.shape[0], q.shape[1]
    T = min(M_CHUNK, L)
    NC = -(-L // T)
    pad = NC * T - L

    def prep(a, fill):
        a = a.astype(jnp.float32)
        if pad:
            a = jnp.pad(a, [(0, 0), (0, pad)] + [(0, 0)] * (a.ndim - 2), constant_values=fill)
        a = jnp.moveaxis(a.reshape((B, NC, T) + a.shape[2:]), 1, 0)
        return jnp.swapaxes(a, 2, 3)

    qc, kc, vc = prep(q, 0.0), prep(k, 0.0), prep(v, 0.0)
    ic, fc = prep(i_pre, NEG), prep(log_f, 0.0)
    causal = jnp.tril(jnp.ones((T, T), dtype=bool))

    def step(carry, xs):
        C, n, m = carry
        qb, kb, vb, ib, fb = xs
        b = jnp.cumsum(fb, axis=-1)
        d = jnp.where(causal, b[..., :, None] - b[..., None, :] + ib[..., None, :], NEG)
        m_inter = b + m[..., None]
        m_t = jnp.maximum(m_inter, jnp.max(d, axis=-1))
        w = jnp.einsum('bhtd,bhsd->bhts', qb, kb) * jnp.exp(d - m_t[..., None])
        a_inter = jnp.exp(m_inter - m_t)
        num = jnp.einsum('bhts,bhsv->bhtv', w, vb) + a_inter[..., None] * jnp.einsum('bhtd,bhdv->bhtv', qb, C)
        den = jnp.sum(w, axis=-1) + a_inter * jnp.einsum('bhtd,bhd->bht', qb, n)
        h = num / jnp.maximum(jnp.abs(den), jnp.exp(-m_t))[..., None]
        b_T = b[..., -1]
        g = b_T[..., None] - b + ib
        m_new = jnp.maximum(b_T + m, jnp.max(g, axis=-1))
        a_in = jnp.exp(g - m_new[..., None])
        a_st = jnp.exp(b_T + m - m_new)
        C_new = a_st[..., None, None] * C + jnp.einsum('bhs,bhsd,bhsv->bhdv', a_in, kb, vb)
        n_new = a_st[..., None] * n + jnp.einsum('bhs,bhsd->bhd', a_in, kb)
        return (C_new, n_new, m_new), h

    init = (C0.astype(jnp.float32), n0.astype(jnp.float32), m0.astype(jnp.float32))
    (C, n, m), h = lax.scan(step, init, (qc, kc, vc, ic, fc))
    h = jnp.transpose(h, (1, 0, 3, 2, 4)).reshape(B, NC * T, M_HEADS, M_DV)[:, :L]
    return h, C, n, m

def mlstm_branch(parts, C0, n0, m0, norm_w):
    B, L = parts['mq'].shape[:2]
    q = parts['mq'].reshape(B, L, M_HEADS, M_DQK) * (M_DQK ** -0.5)
    k = parts['mk'].reshape(B, L, M_HEADS, M_DQK)
    v = parts['mv'].reshape(B, L, M_HEADS, M_DV)
    i_pre = GATE_CAP * jnp.tanh(parts['mi'].astype(jnp.float32) / GATE_CAP)
    log_f = jax.nn.log_sigmoid(GATE_CAP * jnp.tanh(parts['mf'].astype(jnp.float32) / GATE_CAP))
    h, C, n, m = mlstm_chunkwise(q, k, v, i_pre, log_f, C0, n0, m0)
    h = rms_norm(h, norm_w.reshape(M_HEADS, M_DV)).reshape(B, L, MV)
    y = (jax.nn.sigmoid(parts['mo'].astype(jnp.float32)) * h).astype(parts['mo'].dtype)
    return y, C, n, m

def nsa_inputs(parts, pos):
    B, T = parts['nq'].shape[:2]
    q = rope(parts['nq'].reshape(B, T, N_HEADS, HEAD_DIM), pos)
    kv = parts['nkv'].reshape(B, T, 6, N_KV, HEAD_DIM)
    k_c, v_c = rope(kv[:, :, 0], pos), kv[:, :, 1]
    k_s, v_s = rope(kv[:, :, 2], pos), kv[:, :, 3]
    k_w, v_w = rope(kv[:, :, 4], pos), kv[:, :, 5]
    gates = jax.nn.sigmoid(parts['ng'].astype(jnp.float32)).reshape(B, T, N_HEADS, 3)
    return q, gates, k_c, v_c, k_s, v_s, k_w, v_w

def compress(rows, w):
    B, L = rows.shape[:2]
    ncmp = L // CMP_BLOCK
    blocks = rows[:, :ncmp * CMP_BLOCK].reshape(B, ncmp, CMP_BLOCK, N_KV, HEAD_DIM)
    return jnp.einsum('bjigd,id->bjgd', blocks, w)

def to_blocks(rows):
    B, L = rows.shape[:2]
    nsel = -(-L // SEL_BLOCK)
    rows = jnp.pad(rows, ((0, 0), (0, nsel * SEL_BLOCK - L), (0, 0), (0, 0)))
    return jnp.transpose(rows.reshape(B, nsel, SEL_BLOCK, N_KV, HEAD_DIM), (0, 3, 1, 2, 4))

def nsa_attend(q, q_pos, kc, vc, k_blk, v_blk, k_win, v_win, win_pos, gates):
    B, T = q.shape[:2]
    qg = q.astype(jnp.float32).reshape(B, T, N_KV, HPG, HEAD_DIM) * (HEAD_DIM ** -0.5)
    ncmp = kc.shape[1]
    valid_c = ((jnp.arange(ncmp) + 1) * CMP_BLOCK - 1)[None, :] <= q_pos[:, None]
    p_c = masked_softmax(jnp.einsum('btghd,bjgd->btghj', qg, kc), valid_c[None, :, None, None, :])
    o_c = jnp.einsum('btghj,bjgd->btghd', p_c, vc)
    nsel = k_blk.shape[2]
    ratio = SEL_BLOCK // CMP_BLOCK
    imp = jnp.sum(p_c, axis=3)
    imp = jnp.pad(imp, ((0, 0), (0, 0), (0, 0), (0, nsel * ratio - ncmp)))
    imp = imp.reshape(B, T, N_KV, nsel, ratio).sum(-1)
    blk = jnp.arange(nsel)
    forced = (blk[None, :] == (q_pos // SEL_BLOCK)[:, None]) | (blk[None, :] == 0)
    future = blk[None, :] * SEL_BLOCK > q_pos[:, None]
    imp = jnp.where(forced[None, :, None, :], jnp.inf, jnp.where(future[None, :, None, :], -jnp.inf, imp))
    k_eff = min(TOP_K, nsel)
    _, idx = lax.top_k(imp, k_eff)
    bi = jnp.arange(B)[:, None, None, None]
    gi = jnp.arange(N_KV)[None, None, :, None]
    ks = k_blk[bi, gi, idx].reshape(B, T, N_KV, k_eff * SEL_BLOCK, HEAD_DIM)
    vs = v_blk[bi, gi, idx].reshape(B, T, N_KV, k_eff * SEL_BLOCK, HEAD_DIM)
    kpos = (idx[..., None] * SEL_BLOCK + jnp.arange(SEL_BLOCK)).reshape(B, T, N_KV, 1, k_eff * SEL_BLOCK)
    p_s = masked_softmax(jnp.einsum('btghd,btgnd->btghn', qg, ks), kpos <= q_pos[None, :, None, None, None])
    o_s = jnp.einsum('btghn,btgnd->btghd', p_s, vs)
    dpos = q_pos[:, None] - win_pos[None, :]
    valid_w = (dpos >= 0) & (dpos < WINDOW) & (win_pos >= 0)[None, :]
    p_w = masked_softmax(jnp.einsum('btghd,blgd->btghl', qg, k_win), valid_w[None, :, None, None, :])
    o_w = jnp.einsum('btghl,blgd->btghd', p_w, v_win)
    g = gates.reshape(B, T, N_KV, HPG, 3)
    out = g[..., 0:1] * o_c + g[..., 1:2] * o_s + g[..., 2:3] * o_w
    return out.reshape(B, T, NQ).astype(q.dtype)

def nsa_prompt(parts, pos, w_cmp_k, w_cmp_v):
    q, gates, k_c, v_c, k_s, v_s, k_w, v_w = nsa_inputs(parts, pos)
    B, S = q.shape[:2]
    kc, vc = compress(k_c, w_cmp_k), compress(v_c, w_cmp_v)
    k_blk, v_blk = to_blocks(k_s), to_blocks(v_s)
    k_wp = jnp.pad(k_w, ((0, 0), (WINDOW, 0), (0, 0), (0, 0)))
    v_wp = jnp.pad(v_w, ((0, 0), (WINDOW, 0), (0, 0), (0, 0)))
    qb = min(Q_BLOCK, S)
    nqb = S // qb

    def one_block(i):
        start = i * qb
        qpos = start + jnp.arange(qb, dtype=jnp.int32)
        wpos = start - WINDOW + jnp.arange(qb + WINDOW, dtype=jnp.int32)
        return nsa_attend(lax.dynamic_slice_in_dim(q, start, qb, axis=1), qpos, kc, vc, k_blk, v_blk,
                          lax.dynamic_slice_in_dim(k_wp, start, qb + WINDOW, axis=1),
                          lax.dynamic_slice_in_dim(v_wp, start, qb + WINDOW, axis=1), wpos,
                          lax.dynamic_slice_in_dim(gates, start, qb, axis=1))

    out = lax.map(one_block, jnp.arange(nqb, dtype=jnp.int32))
    out = jnp.moveaxis(out, 0, 1).reshape(B, S, NQ)
    win = jnp.stack([k_w, v_w], axis=2)[:, -min(WINDOW, S):]
    return out, jnp.stack([k_c, v_c], axis=2), jnp.stack([k_s, v_s], axis=2), win

def nsa_sample(parts, pos, cache_cmp, cache_slc, cache_win, page_table, w_cmp_k, w_cmp_v):
    q, gates, k_c, v_c, k_s, v_s, k_w, v_w = nsa_inputs(parts, pos)
    B, T = q.shape[:2]
    past_len = page_table.shape[1] * PAGE_SIZE
    cmp_past = cache_cmp[page_table].reshape(B, past_len, 2, N_KV, HEAD_DIM)
    slc_past = cache_slc[page_table].reshape(B, past_len, 2, N_KV, HEAD_DIM)
    kc = compress(jnp.concatenate([cmp_past[:, :, 0], k_c], axis=1), w_cmp_k)
    vc = compress(jnp.concatenate([cmp_past[:, :, 1], v_c], axis=1), w_cmp_v)
    k_blk = to_blocks(jnp.concatenate([slc_past[:, :, 0], k_s], axis=1))
    v_blk = to_blocks(jnp.concatenate([slc_past[:, :, 1], v_s], axis=1))
    wb = cache_win.shape[1]
    k_win = jnp.concatenate([cache_win[:, :, 0], k_w], axis=1)
    v_win = jnp.concatenate([cache_win[:, :, 1], v_w], axis=1)
    wpos = past_len - wb + jnp.arange(wb + T, dtype=jnp.int32)
    out = nsa_attend(q, pos, kc, vc, k_blk, v_blk, k_win, v_win, wpos, gates)
    new_win = jnp.concatenate([cache_win, jnp.stack([k_w, v_w], axis=2)], axis=1)[:, -min(WINDOW, past_len + T):]
    return out, jnp.stack([k_c, v_c], axis=2), jnp.stack([k_s, v_s], axis=2), new_win

def layer(x, c, mix_fn, g_pre_mix, g_post_mix, g_pre_ffn, g_post_ffn, w_ada, b_ada, w_in, b_in,
          w_proj_a, w_proj_b, w_out, w_up, w_down):
    mod = jax.nn.silu(c) @ w_ada + b_ada
    sh1, sc1, ga1, sh2, sc2, ga2 = jnp.split(mod[:, None, :], 6, axis=-1)
    h = rms_norm(x, g_pre_mix) * (1.0 + sc1) + sh1
    parts = project(h, w_in, b_in)
    y_a, y_b, state = mix_fn(parts)
    merged = jax.nn.sigmoid(parts['ga']) * (y_a @ w_proj_a) + jax.nn.sigmoid(parts['gb']) * (y_b @ w_proj_b)
    x = x + ga1 * rms_norm(merged @ w_out, g_post_mix)
    h = rms_norm(x, g_pre_ffn) * (1.0 + sc2) + sh2
    gate, up = jnp.split(h @ w_up, 2, axis=-1)
    x = x + ga2 * rms_norm((jax.nn.silu(gate) * up) @ w_down, g_post_ffn)
    return x, state

def setup_inputs(seed: int = 0) -> dict:
    key = jax.random.key(seed)
    ks = jax.random.split(key, 32)
    n_pages = PAST_LEN // PAGE_SIZE
    n_used = DEC_BATCH * n_pages
    n_pool = (n_used * 5 + 3) // 4
    wb = min(WINDOW, PAST_LEN)

    def nrm(k, shape, s):
        return jax.random.normal(k, shape, jnp.float32) * s

    f_lo = 0
    off = 0
    for name, n in SPLITS:
        if name == 'mf':
            f_lo = off
        off += n
    b_in = nrm(ks[17], (DEPTH, D_IN), 0.02).at[:, f_lo:f_lo + M_HEADS].add(3.0)
    page_table = jax.random.permutation(ks[10], n_pool)[:n_used].reshape(DEC_BATCH, n_pages).astype(jnp.int32)
    return {
        'x_prompt': nrm(ks[0], (BATCH, SEQ, D_MODEL), 1.0),
        'x_sample': nrm(ks[1], (DEC_BATCH, DEC_SEQ, D_MODEL), 1.0),
        'c_prompt': nrm(ks[2], (BATCH, D_MODEL), 1.0),
        'c_sample': nrm(ks[3], (DEC_BATCH, D_MODEL), 1.0),
        'cache_cmp_kv': nrm(ks[4], (DEPTH, n_pool, PAGE_SIZE, 2, N_KV, HEAD_DIM), 1.0),
        'cache_slc_kv': nrm(ks[5], (DEPTH, n_pool, PAGE_SIZE, 2, N_KV, HEAD_DIM), 1.0),
        'cache_win_kv': nrm(ks[6], (DEPTH, DEC_BATCH, wb, 2, N_KV, HEAD_DIM), 1.0),
        'state_mlstm_C': nrm(ks[7], (DEPTH, DEC_BATCH, M_HEADS, M_DQK, M_DV), 1.0),
        'state_mlstm_n': nrm(ks[8], (DEPTH, DEC_BATCH, M_HEADS, M_DQK), 1.0),
        'state_mlstm_m': nrm(ks[9], (DEPTH, DEC_BATCH, M_HEADS), 1.0),
        'page_table': page_table,
        'g_pre_mix': 1.0 + nrm(ks[11], (DEPTH, D_MODEL), 0.05),
        'g_post_mix': 1.0 + nrm(ks[12], (DEPTH, D_MODEL), 0.05),
        'g_pre_ffn': 1.0 + nrm(ks[13], (DEPTH, D_MODEL), 0.05),
        'g_post_ffn': 1.0 + nrm(ks[14], (DEPTH, D_MODEL), 0.05),
        'w_ada': nrm(ks[15], (DEPTH, D_MODEL, 6 * D_MODEL), 0.5 * D_MODEL ** -0.5),
        'b_ada': nrm(ks[16], (DEPTH, 6 * D_MODEL), 0.02),
        'w_in': nrm(ks[18], (DEPTH, D_MODEL, D_IN), D_MODEL ** -0.5),
        'b_in': b_in,
        'mlstm_norm_w': 1.0 + nrm(ks[19], (DEPTH, MV), 0.05),
        'w_cmp_k': (1.0 + nrm(ks[20], (DEPTH, CMP_BLOCK, HEAD_DIM), 0.1)) / CMP_BLOCK,
        'w_cmp_v': (1.0 + nrm(ks[21], (DEPTH, CMP_BLOCK, HEAD_DIM), 0.1)) / CMP_BLOCK,
        'w_proj_a': nrm(ks[22], (DEPTH, MV, D_MODEL), MV ** -0.5),
        'w_proj_b': nrm(ks[23], (DEPTH, NQ, D_MODEL), NQ ** -0.5),
        'w_out': nrm(ks[24], (DEPTH, D_MODEL, D_MODEL), D_MODEL ** -0.5),
        'w_up': nrm(ks[25], (DEPTH, D_MODEL, 2 * D_FF), D_MODEL ** -0.5),
        'w_down': nrm(ks[26], (DEPTH, D_FF, D_MODEL), D_FF ** -0.5),
    }

def reference(x_prompt, x_sample, c_prompt, c_sample, cache_cmp_kv, cache_slc_kv, cache_win_kv,
              state_mlstm_C, state_mlstm_n, state_mlstm_m, page_table,
              g_pre_mix, g_post_mix, g_pre_ffn, g_post_ffn, w_ada, b_ada, w_in, b_in, mlstm_norm_w,
              w_cmp_k, w_cmp_v, w_proj_a, w_proj_b, w_out, w_up, w_down):
    Bp, S = x_prompt.shape[:2]
    Bs, Ts = x_sample.shape[:2]
    past_len = page_table.shape[1] * PAGE_SIZE
    pos_p = jnp.arange(S, dtype=jnp.int32)
    pos_s = past_len + jnp.arange(Ts, dtype=jnp.int32)
    xp, xs = x_prompt, x_sample
    st_p = [[] for _ in range(6)]
    st_s = [[] for _ in range(6)]
    for l in range(DEPTH):
        def mix_prompt(parts, l=l):
            zC = jnp.zeros((Bp, M_HEADS, M_DQK, M_DV), jnp.float32)
            zn = jnp.zeros((Bp, M_HEADS, M_DQK), jnp.float32)
            zm = jnp.zeros((Bp, M_HEADS), jnp.float32)
            y_a, C, n, m = mlstm_branch(parts, zC, zn, zm, mlstm_norm_w[l])
            y_b, cmp_rows, slc_rows, win = nsa_prompt(parts, pos_p, w_cmp_k[l], w_cmp_v[l])
            return y_a, y_b, (cmp_rows, slc_rows, win, C, n, m)

        def mix_sample(parts, l=l):
            y_a, C, n, m = mlstm_branch(parts, state_mlstm_C[l], state_mlstm_n[l], state_mlstm_m[l], mlstm_norm_w[l])
            y_b, cmp_rows, slc_rows, win = nsa_sample(parts, pos_s, cache_cmp_kv[l], cache_slc_kv[l], cache_win_kv[l],
                                                      page_table, w_cmp_k[l], w_cmp_v[l])
            return y_a, y_b, (cmp_rows, slc_rows, win, C, n, m)

        weights = (g_pre_mix[l], g_post_mix[l], g_pre_ffn[l], g_post_ffn[l], w_ada[l], b_ada[l], w_in[l], b_in[l],
                   w_proj_a[l], w_proj_b[l], w_out[l], w_up[l], w_down[l])
        xp, sp = layer(xp, c_prompt, mix_prompt, *weights)
        xs, ss = layer(xs, c_sample, mix_sample, *weights)
        for j in range(6):
            st_p[j].append(sp[j])
            st_s[j].append(ss[j])
    cmp_p, slc_p, win_p, C_p, n_p, m_p = [jnp.stack(a, axis=0) for a in st_p]
    cmp_s, slc_s, win_s, C_s, n_s, m_s = [jnp.stack(a, axis=0) for a in st_s]
    return (xp, xs, cmp_p, slc_p, win_p, C_p, n_p, m_p, cmp_s, slc_s, win_s, C_s, n_s, m_s)


_drawn_inputs = setup_inputs


def setup_inputs(seed=0):
    import zlib

    import numpy as np

    out = dict(_drawn_inputs(seed))
    spreads = {}
    factors = {'cache_cmp_kv': 5.467,
     'cache_slc_kv': 3.087,
     'g_post_mix': 3.623,
     'g_pre_ffn': 2.771,
     'g_post_ffn': 3.895,
     'mlstm_norm_w': 4.068,
     'w_cmp_k': 8.0,
     'w_cmp_v': 8.0}
    for name, (base, spread) in spreads.items():
        noise = np.random.default_rng([zlib.crc32(name.encode()), seed]).standard_normal(out[name].shape)
        drawn = base * np.exp(spread * noise) if base else spread * noise
        out[name] = __import__('jax').numpy.asarray(drawn.astype(out[name].dtype))
    for name, factor in factors.items():
        out[name] = (out[name] * factor).astype(out[name].dtype)
    return out
```

```python
from contextlib import ExitStack

import numpy as np
import concourse.bass as bass
from concourse import mybir

ALU = mybir.AluOpType
ACT = mybir.ActivationFunctionType
AX = mybir.AxisListType
F32 = mybir.dt.float32
I32 = mybir.dt.int32

P = 128
D = 1024
KD = D // P
SEQ = 1024
NT = SEQ // P
NS = 8
TOK = SEQ + NS
TG = TOK // 3
MH, DQK, DV = 4, 64, 128
NH, NKV, HD = 8, 2, 64
HPG = NH // NKV
CAP = 15.0
CMP, SEL, WIN = 32, 64, 512
PAST, PAGE = 1024, 128
NPAGE = PAST // PAGE
NCMP = SEQ // CMP
DFF = 2816
KF = DFF // P
EPS = 1e-6
NEG = -1e30

C_MQ, C_MK, C_MV, C_MO, C_MI, C_MF = 0, 256, 512, 1024, 1536, 1540
C_NQ, C_KV, C_NG, C_GA, C_GB, D_IN = 1544, 2056, 2824, 2848, 3872, 4896
MIX = C_GA
PB = 356
NPB = MIX // PB
ARENA = 38500


def constants():
    p = np.arange(P)
    parts = {}
    parts["ident"] = np.eye(P)
    parts["causal_st"] = np.where(p[:, None] <= p[None, :], 0.0, NEG)
    parts["causal_ts"] = np.where(p[None, :] <= p[:, None], 0.0, NEG)
    parts["window_ts"] = np.where(p[None, :] > p[:, None], 0.0, NEG)
    pos = (np.arange(NT)[None, :, None] * P + p[:, None, None])
    ends = (np.arange(NCMP) + 1)[None, None, :] * CMP - 1
    parts["cmp_add"] = np.where(ends <= pos, 0.0, NEG).reshape(P, NT * NCMP)
    parts["cmp_one"] = np.where(ends <= pos, 1.0, 0.0).reshape(P, NT * NCMP)
    parts["block"] = (np.arange(60)[None, :] - 28 == p[:, None] // CMP) * 1.0
    half = HD // 8
    inv = (np.float32(500000.0) ** (-np.arange(half, dtype=np.float32) * np.float32(2.0) / np.float32(HD // 4)))
    ang = (pos.astype(np.float32) * inv.astype(np.float32)[None, None, :]).astype(np.float32)
    parts["cos"] = np.cos(ang.astype(np.float64)).reshape(P, NT * half)
    parts["sin"] = np.sin(ang.astype(np.float64)).reshape(P, NT * half)
    sang = (np.float32(PAST) * inv).astype(np.float32).astype(np.float64)
    parts["scos"] = np.broadcast_to(np.cos(sang), (P, half))
    parts["ssin"] = np.broadcast_to(np.sin(sang), (P, half))
    r = np.arange(P)
    parts["own_new"] = np.where((r[:, None] // NH) == np.arange(NS)[None, :], 0.0, NEG)
    parts["same_group"] = ((r[:, None] // HPG) == (r[None, :] // HPG))[:, :64] * 1.0
    parts["blk"] = np.broadcast_to(np.arange(16.0), (P, 16))
    parts["quarter"] = ((r[:, None] // 4) == np.arange(32)[None, :]) * 1.0
    parts["onehot"] = np.broadcast_to(np.eye(NS).reshape(1, NS * NS), (P, NS * NS))
    at, n = {}, 0
    for k, v in parts.items():
        at[k] = (n, n + v.shape[1])
        n += v.shape[1]
    return np.concatenate([v.astype(np.float32) for v in parts.values()], axis=1), at


CONST, CAT = constants()


class Tally:

    def __init__(self, sem):
        self.sem, self.base, self.n, self.trip, self.per = sem, 0, 0, None, 0

    def loop(self, trip, per):
        self.base += self.n
        self.n, self.trip, self.per = 0, trip, per

    def end(self, trips):
        assert self.n == self.per, f"{self.sem.name}: per trip {self.n}, not {self.per}"
        self.base += trips * self.per
        self.n, self.trip, self.per = 0, None, 0

    def value(self, back=0):
        v = self.base + self.n - back
        return v if self.trip is None else self.trip * self.per + v


def build(nc, t, outs):
    (y_prompt, y_sample, cmp_prompt, slc_prompt, win_prompt, C_prompt, n_prompt, m_prompt,
     cmp_sample, slc_sample, win_sample, C_sample, n_sample, m_sample) = outs
    with ExitStack() as ctx:
        def sb(name, shape, dt=F32):
            return ctx.enter_context(nc.sbuf_tensor(name, shape, dt))

        def sem(name):
            return ctx.enter_context(nc.semaphore(name))

        ps = ctx.enter_context(nc.psum_tensor("ps", [P, 8, 512], F32))

        const = sb("const", [P, CONST.shape[1]])

        def cst(name, rows=P):
            return const[0:rows, CAT[name][0]:CAT[name][1]]

        ident = cst("ident")
        vecT = sb("vecT", [P, 96])
        modT = sb("modT", [P, 48, 9])
        sc1 = sb("sc1", [P, KD, 9])
        sc2 = sb("sc2", [P, KD, 9])
        gg1 = sb("gg1", [P, KD, 9])
        gg2 = sb("gg2", [P, KD, 9])
        ones = sb("ones", [P, P])
        mnormB = sb("mnormB", [P, MH * DV])
        ss = sb("ss", [P, 9])
        rstd = sb("rstd", [P, 9])
        cT = sb("cT", [P, KD, 9])
        xn = sb("xn", [P, 2, D])
        hT = sb("hT", [P, KD, TOK])
        arena = sb("arena", [P, ARENA])

        def room(at, *shape, rows=P):
            n = int(np.prod(shape))
            assert at + n <= ARENA, (at, shape)
            v = arena[0:rows, at:at + n]
            if len(shape) == 2:
                v = v.rearrange("p (a b) -> p a b", a=shape[0])
            if len(shape) == 3:
                v = v.rearrange("p (a b c) -> p a b c", a=shape[0], b=shape[1])
            return v

        xin = room(0, NT, D)
        xs = room(NT * D, D, rows=NS)
        cin = room(NT * D + D, D, rows=9)
        vrows = room(NT * D + 2 * D, P, rows=96)
        wada = [room(NT * D + 2 * D + P + s * KD * 512, KD, 512) for s in range(3)]
        Pm = room(0, NT, MIX)
        Ps = room(NT * MIX, MIX, rows=NS)
        bmix = room(NT * MIX + MIX, MIX)
        wmix = [room(NT * MIX + 2 * MIX + s * KD * PB, KD, PB) for s in range(2)]

        at = NT * MIX + MIX
        yaT = room(at, MH, TOK)
        at += MH * TOK
        ybT = room(at, NH * HD // P, TOK)
        at_nsa = at + NH * HD // P * TOK

        def take(rows, *shape):
            nonlocal at
            v = room(at, *shape, rows=rows)
            at += int(np.prod(shape))
            return v
        gate = take(P, 9, 8)
        gi, lf, gtmp = take(P, 36), take(P, 36), take(P, 36)
        iR, fR, bR, aR, AR, nmxR, eiR, emR, ainR = (take(32, P) for _ in range(9))
        row = sb("row", [1, 6, 32])
        colR = take(32, 4)
        tok = take(P, 4, 32)
        astB = take(P, 32)
        nmxM = take(32, MH, P)
        qk, vone, qe, ke = take(P, 2 * MH, DQK), take(P, MH, DV + 1), take(P, MH, DQK), take(P, MH, DQK)
        qT, qeT, kT = take(DQK, MH, P), take(DQK, MH, P), take(DQK, MH, P)
        wexp, wgt = take(P, MH, P), take(P, MH, P)
        Cst = sb("Cst", [DQK, MH, DV + 1])
        dn = take(P, MH)
        hn = take(P, 32)

        at = at_nsa
        ksT, kwT = take(P, SEQ), take(P, SEQ)
        kcT = take(P, NCMP)
        vc = take(NCMP, NKV * HD)
        gts = take(P, NT, 3 * NH)
        wck, wcv = take(P, HD), take(P, HD)
        qst = Pm[:, 5, 0:SEQ].rearrange("p (t c) -> p t c", c=P)
        ost = take(HD, SEQ)
        nmx = take(P, 3 * NT)
        rsum = take(P, NT, 3)
        gsc = take(P, NT, 3)
        pbuf = [Pm[:, u, 0:SEQ] for u in range(2)]
        ptbuf = [Pm[:, 2 + u, 0:SEQ] for u in range(2)]
        qTh = Pm[:, 4, 0:SEQ]
        kcw, vcw = (Pm[:, 6 + j, 0:SEQ].rearrange("p (t c) -> p t c", t=NT) for j in range(2))
        units = []
        for i in range(NT):
            for kind in "ws":
                lo = max(0, i - WIN // P) if kind == "w" else 0
                blocks = [((b - lo) * P, P, b) for b in range(lo, i + 1)]
                if kind == "w":
                    blocks.append((5 * P, NCMP, None))
                units.append((kind, i, lo, blocks, [blocks[j:j + 4] for j in range(0, len(blocks), 4)]))
        NU = len(units)
        groups, g_no = [], 2
        for u in units:
            groups.append([g_no + j for j in range(len(u[4]))])
            g_no += len(u[4])
        GA, GB = (g_no + 1) // 2, g_no // 2

        at = 0
        CB, SB_, WB = NPAGE * 2 * NKV * HD, NPAGE * NKV * HD, WIN // P * NKV * HD
        slot_at = [at, at + CB + SB_ + WB]
        pg_cmp = [room(x, NPAGE, 2 * NKV * HD) for x in slot_at]
        pg_slc = [room(x + CB, NPAGE, NKV * HD) for x in slot_at]
        pg_win = [room(x + CB + SB_, WIN // P, NKV * HD) for x in slot_at]
        at = slot_at[1] + CB + SB_ + WB
        pT, wT = take(P, PAST), take(P, WIN)
        ckT = take(P, NCMP)
        vcs = take(NCMP, NS, NKV * HD)
        Qall, Qpad = take(P, NS, NH), take(P, NS, NH)
        knT = take(P, 2, NS)
        SR = NS * NH
        Ssl, Swn, Scm = take(SR, PAST + NS), take(SR, WIN + NS), take(SR, NCMP)
        pcm = take(SR, NCMP)
        imp, msk, small, sgt = take(SR, 16), take(SR, 16), take(SR, 16), take(SR, 3)
        zrow = take(1, 512)
        PTs = take(P, 1, 512)
        PTw = take(P, 512)
        DQ = DQK // 4
        sC, sT_ = take(P, DQ, DV), take(P, DQ, DV)
        sv = take(P, DV)
        sq, sk, sn = take(P, DQ), take(P, DQ), take(P, DQ)
        sW = take(P, DV + 2)
        hsum = take(P, 2, DQ)
        sg = take(P, 8)
        hv, hmo, hw = take(32, DV), take(32, DV), take(32, DV)
        hg = take(32, 10)
        hs = take(32, DV + 2)
        hsq = take(32, DV)
        assert at <= NT * MIX, at
        scr = {n: nc.dram_tensor(f"scratch_{n}", [NS, w], F32, kind="Internal").ap()
               for n, w in (("q", 256), ("k", 256), ("v", 512), ("o", 512), ("i", MH), ("f", MH), ("g", 3 * NH))}
        ptab = sb("ptab", [1, NS * NPAGE], I32)

        merT = room(0, KD, TOK)
        wmg = [room(8256 + s * 6144, 24, 256) for s in range(2)]
        wot = [room(20608 + s * 2048, KD, 256) for s in range(2)]
        yT1 = room(9216, KD, TOK)
        yt, yts = room(0, NT, D), room(NT * D, D, rows=NS)
        xres, xress = room(25632, NT, D), room(25632 + NT * D, D, rows=NS)
        G, Gs = room(34848, D), room(35872, D, rows=NS)
        sgm = [room(36896 + j * TG, TG) for j in range(4)]
        aT = room(0, KF, TOK)
        wup = [room(22704, 2 * KD, P), room(34848, 2 * KD, P)]
        sil = [room(24752, TG), room(24752 + TG, TG)]
        wdn = [room(22704, KF, P), room(34848, KF, P)]
        G2, G2s = xn[:, 0, :], xn[0:NS, 1, :]
        bnow = room(38300, 8)

        def flat(x):
            return x[:, :, :].rearrange("p a b -> p (a b)")
        junk = room(9216 + KD * TOK + D, D)
        diag = [room(9216 + KD * TOK, D), room(9216, D)]

        s_const, s_c, s_vrow, s_x, s_bmix = (sem(n) for n in ("const", "c", "vrow", "x", "bmix"))
        s_ada = [sem(f"ada{s}") for s in range(3)]
        s_ada_used = sem("ada_used")
        s_cT, s_vT, s_cS = sem("cT_ps"), sem("vT_ps"), sem("cT_silu")
        s_modps, s_mod, s_ss, s_ms, s_sd, s_rstd = (sem(n) for n in ("mod_ps", "mod", "ss", "meansq", "std", "rstd"))
        s_xn, s_xT, s_xT_act, s_xT_dve = (sem(n) for n in ("xn", "xT", "xT_act", "xT_dve"))
        s_sT, s_sh = sem("sampleT"), sem("sample_h")
        s_wmix = [sem(f"wmix{s}") for s in range(2)]
        s_wmix_used, s_mixps, s_mix = sem("wmix_used"), sem("mix_ps"), sem("mix")
        s_rope, s_rows = sem("rope"), sem("rows_out")
        s_gate, s_tanh, s_gabs, s_gln, s_gRps, s_gR, s_rowps, s_rowsb, s_colps, s_colsb, s_bR = (
            sem(n) for n in ("gate", "tanh", "gabs", "gln", "gR_ps", "gR", "row_ps", "row_sb", "col_ps", "col_sb", "bR"))
        s_gexp, s_tokps, s_tok = sem("gexp"), sem("tok_ps"), sem("tok")
        s_ones, s_stage, s_qkps, s_qTs, s_kTs, s_zps, s_arg, s_we, s_Sps, s_w, s_num, s_st, s_h, s_C = (
            sem(n) for n in ("ones", "stage", "qk_ps", "qT", "kT", "z_ps", "w_arg", "w_exp", "S_ps", "w", "num_ps", "state_ps", "h", "C"))
        s_kv, s_kvps, s_kvT, s_wc, s_cw, s_cps, s_cT2, s_gts = (
            sem(n) for n in ("kv_go", "kv_ps", "kvT", "w_cmp", "cmp_weighted", "cmp_ps", "cmpT", "gates"))
        s_qst, s_qseen, s_S, s_max, s_exp, s_one, s_pv, s_comb = (
            sem(n) for n in ("q_staged", "q_seen", "att_S", "att_max", "att_exp", "att_scaled", "att_pv", "att_O_taken"))
        s_pt, s_ev = [sem("pt_A"), sem("pt_B")], [sem("ev_A"), sem("ev_B")]
        s_yb, s_ybd = sem("ybT_sample"), sem("ybT_rows")
        s_scr, s_scrg, s_smp, s_pt64, s_newwin = sem("scratch"), sem("scratch_gates"), sem("sample_in"), sem("page_table"), sem("new_win")
        s_ldk, s_ldv = [sem("pages_k0"), sem("pages_k1")], [sem("pages_v0"), sem("pages_v1")]
        s_free, s_cmul, s_pgps, s_pga, s_pgd, s_qp = (
            sem(n) for n in ("pages_used", "pages_weighted", "pages_T", "pages_act", "pages_dve", "q_padded"))
        s_Qps, s_Qall, s_kn, s_zero, s_newS, s_soft, s_softm, s_softe, s_impps, s_sPT, s_sPTe, s_pvs, s_Osum = (
            sem(n) for n in ("Q_ps", "Q_all", "knT", "zero", "new_S", "soft", "soft_max", "soft_exp", "imp_ps", "sPT_ps", "sPT", "sample_pv", "sample_O"))
        s_cg, s_cge, s_sWd, s_sWp, s_sh2, s_shd, s_sCn, s_syT, s_sya = (
            sem(n) for n in ("sm_gate", "sm_exp", "sm_W", "sm_W_ps", "sm_h", "sm_std", "sm_C", "sm_yT", "sm_ya"))
        s_wmg, s_wl = ([sem(f"{n}{j}") for j in range(2)] for n in ("wmerge", "wlate"))
        UP0, DN0 = 2 * 16, 2 * 16 + KF // 2 * 32
        s_mgps, s_mgact, s_mgdve, s_mgused, s_mgadd = sem("merge_ps"), sem("merge_sig"), sem("merge_dve"), sem("merge_used"), sem("merge_add")
        s_wops, s_woact, s_wodve, s_woused = sem("wout_ps"), sem("wout_act"), sem("wout_dve"), sem("wout_used")
        s_upps, s_upact, s_updve, s_upused = sem("up_ps"), sem("up_act"), sem("up_dve"), sem("up_used")
        s_out2, s_ss2 = sem("x1_ready"), sem("ss_x1")
        s_x1in, s_diag, s_Gps, s_G, s_ytps, s_ytsq, s_ytdve, s_out = (
            sem(n) for n in ("x_again", "diag", "G_ps", "G", "yt_ps", "yt_sq", "yt_dve", "y_out"))
        s_mo, s_y, s_yT, s_ya, s_hsd = sem("mo_sig"), sem("y"), sem("yT_ps"), sem("yaT"), sem("h_std")
        s_dve, s_act, s_pool = sem("dve_steps"), sem("act_steps"), sem("pool_steps")

        block = ctx.enter_context(nc.Block())

        @block.sync
        def _(sp):
            sp.dma_start(ptab[:, :], t["page_table"].rearrange("b j -> (b j)").unsqueeze(0)).then_inc(s_pt64, 16)
            sp.dma_start(const[:, :], t["const"]).then_inc(s_const, 16)
            sp.dma_start(mnormB[:, :], t["mlstm_norm_w"].partition_broadcast(P)).then_inc(s_const, 16)
            sp.dma_start(cin[0:1, :], t["c_prompt"]).then_inc(s_c, 16)
            sp.dma_start(cin[1:9, :], t["c_sample"]).then_inc(s_c, 16)
            line = 0
            for name, lo, n in (("b_ada", 0, 48), ("b_in", C_GA, 16), ("g_pre_mix", 0, 8), ("g_pre_ffn", 0, 8),
                                ("g_post_mix", 0, 8), ("g_post_ffn", 0, 8)):
                sp.dma_start(vrows[line:line + n, :], t[name][0, lo:lo + n * P].rearrange("(r f) -> r f", f=P))\
                  .then_inc(s_vrow, 16)
                line += n
            w_ada = t["w_ada"][0].rearrange("(k p) n -> p k n", p=P)
            for s in range(3):
                sp.dma_start(wada[s], w_ada[:, :, s * 512:(s + 1) * 512]).then_inc(s_ada[s], 16)
            with sp.Fori(1, 4) as i:
                for s in range(3):
                    sp.wait_ge(s_ada_used, i * 3 + (s - 2))
                    sp.dma_start(wada[s], w_ada[:, :, bass.ds(i * 1536 + s * 512, 512)]).then_inc(s_ada[s], 16)
            w_in = t["w_in"][0].rearrange("(k p) n -> p k n", p=P)
            sp.wait_ge(s_modps, 1)
            sp.wait_ge(s_sh, 1)
            sp.wait_ge(s_xn, 8)
            sp.dma_start(bmix, t["b_in"][:, 0:MIX].partition_broadcast(P)).then_inc(s_bmix, 16)
            for s in range(2):
                sp.dma_start(wmix[s], w_in[:, :, s * PB:(s + 1) * PB]).then_inc(s_wmix[s], 16)
            with sp.Fori(1, MIX // PB // 2) as i:
                for s in range(2):
                    sp.wait_ge(s_wmix_used, i * 2 + (s - 1))
                    sp.dma_start(wmix[s], w_in[:, :, bass.ds(i * 2 * PB + s * PB, PB)]).then_inc(s_wmix[s], 16)
            sp.wait_ge(s_rope, 1)
            for n, lo, w in (("q", C_MQ, 256), ("k", C_MK, 256), ("v", C_MV, 512), ("o", C_MO, 512), ("g", C_NG, 24)):
                sp.dma_start(scr[n], Ps[:, lo:lo + w]).then_inc(s_scr, 16)
            sp.wait_ge(s_gate, 2)
            sp.dma_start(scr["i"], gi[0:NS, 32:36]).then_inc(s_scrg, 16)
            sp.dma_start(scr["f"], lf[0:NS, 32:36]).then_inc(s_scrg, 16)
            sp.dma_start(win_sample[0, :, 0:WIN - 1].rearrange("b r a g d -> b (r a g d)"),
                         t["cache_win_kv"][0, :, 1:WIN].rearrange("b r a g d -> b (r a g d)")).then_inc(s_newwin, 16)
            sp.wait_ge(s_ya, NT)
            for r in range(4):
                sp.dma_start(wck[r * CMP:(r + 1) * CMP, :], t["w_cmp_k"][0]).then_inc(s_wc, 16)
                sp.dma_start(wcv[r * CMP:(r + 1) * CMP, :], t["w_cmp_v"][0]).then_inc(s_wc, 16)
            with sp.Fori(0, NH // 2) as j:
                for odd in range(2):
                    sp.wait_ge(s_comb, j * 2 * NT + (odd * NT + NT + 1))
                    sp.dma_start(ybT[odd * HD:(odd + 1) * HD, bass.ds(j, 1), 0:SEQ], ost.unsqueeze(1)).then_inc(s_ybd, 16)
            sp.wait_ge(s_rope, 1)

            def rows(dst, src, slow=False):
                sp.dma_start(dst, src, allow_slow_non_contiguous=slow).then_inc(s_rows, 16)
            rows(cmp_prompt[0, 0].rearrange("(t p) a g d -> p t (a g d)", p=P), Pm[:, :, C_KV:C_KV + 256])
            rows(slc_prompt[0, 0].rearrange("(t p) a g d -> p t (a g d)", p=P), Pm[:, :, C_KV + 256:C_KV + 512])
            rows(win_prompt[0, 0].rearrange("(t p) a g d -> p t (a g d)", p=P), Pm[:, NT - WIN // P:, C_KV + 512:C_KV + 768])
            rows(cmp_sample[0, :, 0].rearrange("b a g d -> b (a g d)"), Ps[:, C_KV:C_KV + 256])
            rows(slc_sample[0, :, 0].rearrange("b a g d -> b (a g d)"), Ps[:, C_KV + 256:C_KV + 512])
            sp.wait_ge(s_C, NT + 1)
            rows(C_prompt[0, 0].rearrange("h d v -> d h v"), Cst[:, :, 0:DV])
            rows(n_prompt[0, 0].rearrange("h d -> d h").unsqueeze(2), Cst[:, :, DV:DV + 1], True)
            rows(m_prompt[0], row[:, 2, 32 - MH:32])
            rows(win_sample[0, :, WIN - 1].rearrange("b a g d -> b (a g d)"), Ps[:, C_KV + 512:C_KV + 768])
            sp.wait_ge(s_scr, 80)
            sp.wait_ge(s_scrg, 32)
            sp.wait_ge(s_ybd, 16 * (NH + 1))

            def give(dst, src, slow=False):
                sp.dma_start(dst, src, allow_slow_non_contiguous=slow).then_inc(s_smp, 16)

            def flat_rows(x, w):
                names = "abcdef"[:len(x.shape)]
                return x.rearrange(f"{' '.join(names)} -> ({' '.join(names)})").rearrange("(r w) -> r w", w=w)
            sC2 = sC.rearrange("p a b -> p (a b)")
            give(sC2, flat_rows(t["state_mlstm_C"], DQ * DV))
            give(sn, flat_rows(t["state_mlstm_n"], DQ))
            give(sq, flat_rows(scr["q"], DQ))
            give(sk, flat_rows(scr["k"], DQ))
            for j in range(4):
                give(sv[j::4, :], flat_rows(scr["v"], DV))
                give(sg[j::4, 0:1], flat_rows(scr["i"], 1))
                give(sg[j::4, 1:2], flat_rows(scr["f"], 1))
                give(sg[j::4, 2:3], flat_rows(t["state_mlstm_m"], 1))
            give(hv, flat_rows(scr["v"], DV))
            give(hmo, flat_rows(scr["o"], DV))
            give(hg[:, 0:1], flat_rows(scr["i"], 1))
            give(hg[:, 1:2], flat_rows(scr["f"], 1))
            give(hg[:, 2:3], flat_rows(t["state_mlstm_m"], 1))
            for b in range(NS):
                give(hw[b * MH:(b + 1) * MH, :], flat_rows(t["mlstm_norm_w"], DV))
            give(sgt, flat_rows(scr["g"], 3))
            sp.wait_ge(s_pt64, 16)

            def win_rows(b, a):
                return t["cache_win_kv"][0, bass.ds(b, 1), :, a].rearrange("o (q p) g d -> p (o q) (g d)", p=P)

            def load_keys(b, s):
                for j in range(NPAGE):
                    page = sp.value_load(ptab[0:1, bass.ds(b * NPAGE + j, 1)], min_val=0,
                                         max_val=t["cache_cmp_kv"].shape[1] - 1)
                    sp.dma_start(pg_cmp[s][:, j:j + 1, :],
                                 t["cache_cmp_kv"][0, bass.ds(page, 1)].rearrange("o p a g d -> p o (a g d)")).then_inc(s_ldk[s], 16)
                    sp.dma_start(pg_slc[s][:, j:j + 1, :],
                                 t["cache_slc_kv"][0, bass.ds(page, 1), :, 0].rearrange("o p g d -> p o (g d)")).then_inc(s_ldk[s], 16)
                sp.dma_start(pg_win[s], win_rows(b, 0)).then_inc(s_ldk[s], 16)

            def load_values(b, s):
                for j in range(NPAGE):
                    page = sp.value_load(ptab[0:1, bass.ds(b * NPAGE + j, 1)], min_val=0,
                                         max_val=t["cache_slc_kv"].shape[1] - 1)
                    sp.dma_start(pg_slc[s][:, j:j + 1, :],
                                 t["cache_slc_kv"][0, bass.ds(page, 1), :, 1].rearrange("o p g d -> p o (g d)")).then_inc(s_ldv[s], 16)
                sp.dma_start(pg_win[s], win_rows(b, 1)).then_inc(s_ldv[s], 16)
            with sp.Fori(0, NS // 2) as i:
                for s in range(2):
                    sp.wait_ge(s_free, i * 2 + (s + 1))
                    load_keys(i * 2 + s, s)
            with sp.Fori(0, NS // 2) as i:
                for s in range(2):
                    sp.wait_ge(s_free, i * 2 + (NS + s + 1))
                    load_values(i * 2 + s, s)
            sp.wait_ge(s_sCn, 1)
            rows(flat_rows(C_sample, DQ * DV), sC2)
            rows(flat_rows(n_sample, DQ), sn)
            rows(flat_rows(m_sample, 1), hg[:, 3:4])
            sp.wait_ge(s_newwin, 16)
            sp.wait_ge(s_rows, 16 * 12)

            sp.wait_ge(s_yb, 1)
            wpa = t["w_proj_a"][0].rearrange("(k p) n -> p k n", p=P)
            wpb = t["w_proj_b"][0].rearrange("(k p) n -> p k n", p=P)
            w_out = t["w_out"][0].rearrange("(k p) n -> p k n", p=P)
            w_up = t["w_up"][0].rearrange("(k p) n -> p k n", p=P)
            w_down = t["w_down"][0].rearrange("(k p) n -> p k n", p=P)

            def load_merge(col, s):
                sp.dma_start(wmg[s][:, 0:8, :], w_in[:, :, bass.ds(col + C_GA, 256)]).then_inc(s_wmg[s], 16)
                sp.dma_start(wmg[s][:, 8:16, :], w_in[:, :, bass.ds(col + C_GB, 256)]).then_inc(s_wmg[s], 16)
                sp.dma_start(wmg[s][:, 16:20, :], wpa[:, :, bass.ds(col, 256)]).then_inc(s_wmg[s], 16)
                sp.dma_start(wmg[s][:, 20:24, :], wpb[:, :, bass.ds(col, 256)]).then_inc(s_wmg[s], 16)
            for s in range(2):
                load_merge(s * 256, s)
            for s in range(2):
                sp.dma_start(wot[s], w_out[:, :, s * 256:(s + 1) * 256]).then_inc(s_wl[s], 16)
            for s in range(2):
                sp.wait_ge(s_mgused, s + 1)
                load_merge(512 + s * 256, s)
            sp.wait_ge(s_mgused, 4)
            sp.dma_start(xres, t["x_prompt"][0].rearrange("(t p) d -> p t d", p=P)).then_inc(s_x1in, 16)
            sp.dma_start(xress, t["x_sample"][:, 0, :]).then_inc(s_x1in, 16)
            for s in range(2):
                sp.wait_ge(s_woused, s + 1)
                sp.dma_start(wot[s], w_out[:, :, 512 + s * 256:768 + s * 256]).then_inc(s_wl[s], 16)

            def load_up(col, s):
                sp.dma_start(wup[s][:, 0:8, :], w_up[:, :, bass.ds(col, P)]).then_inc(s_wl[s], 16)
                sp.dma_start(wup[s][:, 8:16, :], w_up[:, :, bass.ds(col + DFF, P)]).then_inc(s_wl[s], 16)
            sp.wait_ge(s_woused, 4)
            load_up(0, 0)
            sp.wait_ge(s_ytdve, NT + 1)
            load_up(P, 1)
            with sp.Fori(1, KF // 2) as i:
                for s in range(2):
                    sp.wait_ge(s_upused, i * 2 + (s - 1))
                    load_up(i * 2 * P + s * P, s)
            sp.wait_ge(s_upused, KF)
            sp.wait_ge(s_updve, 3 * KF + 2)
            for s in range(2):
                sp.dma_start(wdn[s], w_down[:, :, s * P:(s + 1) * P]).then_inc(s_wl[s], 16)
            with sp.Fori(1, KD // 2) as i:
                for s in range(2):
                    sp.wait_ge(s_woused, i * 2 + (4 + s - 1))
                    sp.dma_start(wdn[s], w_down[:, :, bass.ds(i * 2 * P + s * P, P)]).then_inc(s_wl[s], 16)
            for n in range(NT):
                sp.wait_ge(s_out, n + 1)
                sp.dma_start(y_prompt[0, n * P:(n + 1) * P, :], xres[:, n, :]).then_inc(s_rows, 16)
            sp.wait_ge(s_out, NT + 1)
            sp.dma_start(y_sample[:, 0, :], xress).then_inc(s_rows, 16)
            sp.wait_ge(s_rows, 16 * 21)

        @block.gpsimd
        def _(pool):
            nc.gpsimd.memset(ones[:, :], 1.0).then_inc(s_ones, 1)
            pool.wait_ge(s_ones, 1)
            pool.wait_ge(s_mix, 4 + 72)
            nc.gpsimd.memset(vone, 1.0).then_inc(s_ones, 1)
            pool.wait_ge(s_ones, 2)
            pool.wait_ge(s_tok, 1)
            with pool.Fori(0, NT) as c:
                pool.wait_ge(s_st, c + 1)
                pm = Pm[:, bass.ds(c, 1), :]
                q3 = pm[:, :, 0:256].rearrange("p a (h d) -> p (a h) d", d=DQK)
                k3 = pm[:, :, 256:512].rearrange("p a (h d) -> p (a h) d", d=DQK)

                def per_head(j):
                    return tok[:, j, bass.ds(c * MH, MH)].unsqueeze(2).to_broadcast([P, MH, DQK])
                nc.gpsimd.tensor_copy(qk, pm[:, :, 0:512].rearrange("p a (h d) -> p (a h) d", d=DQK))
                nc.gpsimd.tensor_tensor(qe, q3, per_head(1), ALU.mult)
                nc.gpsimd.tensor_tensor(nmxM, nmxR.unsqueeze(1).to_broadcast([32, MH, P]),
                                        ident[0:32, bass.ds(c * MH, MH)].unsqueeze(2).to_broadcast([32, MH, P]), ALU.mult)\
                  .then_inc(s_stage, 1)
                nc.gpsimd.tensor_tensor(ke, k3, per_head(3), ALU.mult)
                nc.gpsimd.tensor_copy(vone[:, :, 0:DV], pm[:, :, 512:1024].rearrange("p a (h v) -> p (a h) v", v=DV))\
                  .then_inc(s_stage, 1)

            pool.wait_ge(s_wc, 128)
            for src, w, lo in ((kcw, wck, C_KV), (vcw, wcv, C_KV + 128)):
                for g in range(NKV):
                    ins = nc.gpsimd.tensor_tensor(src[:, :, g * HD:(g + 1) * HD], Pm[:, :, lo + g * HD:lo + (g + 1) * HD],
                                                  w.unsqueeze(1).to_broadcast([P, NT, HD]), ALU.mult)
            ins.then_inc(s_cw, 1)
            for g in range(NKV):
                pool.wait_ge(s_qseen, g * HPG + 1)
                nc.gpsimd.memset(qst, 0.0).then_inc(s_pool, 1)
                pool.wait_ge(s_pool, g + 1)
                with pool.Fori(g * HPG, (g + 1) * HPG) as h:
                    pool.wait_ge(s_qseen, h + 1)
                    nc.gpsimd.tensor_copy(qst[:, :, g * HD:(g + 1) * HD], Pm[:, :, bass.ds(h * HD + C_NQ, HD)]).then_inc(s_qst, 1)

            with pool.Fori(0, NS // 2) as i:
                for s in range(2):
                    pool.wait_ge(s_ldk[s], i * 272 + 272)
                    for a, w in ((0, wck), (1, wcv)):
                        v = pg_cmp[s][:, :, a * NKV * HD:(a + 1) * NKV * HD].rearrange("p j (g d) -> p j g d", g=NKV)
                        ins = nc.gpsimd.tensor_tensor(v, v, w.unsqueeze(1).unsqueeze(1).to_broadcast([P, NPAGE, NKV, HD]), ALU.mult)
                    ins.then_inc(s_cmul, 1)

        @block.scalar
        def _(act):
            act.dma_start(xin, t["x_prompt"][0].rearrange("(t p) d -> p t d", p=P)).then_inc(s_x, 16)
            act.dma_start(xs, t["x_sample"][:, 0, :]).then_inc(s_x, 16)
            act.sem_inc(s_xT_act, 2)
            act.wait_ge(s_cT, 1)
            nc.scalar.activation(cT[:, :, :], ps[:, 7, 0:72].rearrange("p (k c) -> p k c", c=9), ACT.Silu).then_inc(s_cS, 1)
            act.wait_ge(s_x, 32)
            act.wait_ge(s_ss, 1)
            with act.Fori(0, NT) as i:
                nc.scalar.activation(hT[:, 0, 0:D], xin[:, bass.ds(i, 1), :].rearrange("p a b -> p (a b)"), ACT.Square,
                                     accum_out=ss[:, bass.ds(i, 1)]).then_inc(s_ss, 1)
                act.wait_ge(s_ss, i + 2)
            nc.scalar.activation(hT[0:NS, 0, 0:D], xs, ACT.Square, accum_out=ss[0:NS, 8:9]).then_inc(s_ss, 1)
            act.wait_ge(s_ms, 1)
            nc.scalar.activation(rstd[:, :], rstd[:, :], ACT.Sqrt).then_inc(s_sd, 1)
            act.wait_ge(s_mod, 1)

            def h_act(rnd):
                sc, sh = (sc1, sc2)[rnd], 24 * rnd
                with act.Fori(0, NT // 2) as i:
                    for s in range(2):
                        act.wait_ge(s_xT, 2 * i + (NT * rnd + s + 1))
                        for k in range(KD // 2):
                            ins = nc.scalar.activation(hT[:, k, bass.ds(i * 256 + s * P, P)],
                                                       ps[:, 2 * s + k // 4, (k % 4) * P:(k % 4 + 1) * P], ACT.Identity,
                                                       scale=sc[:, k, 0:1], bias=modT[:, sh + k, 0:1])
                        ins.then_inc(s_xT_act, 1)
            h_act(0)

            act.wait_ge(s_gate, 1)
            nc.scalar.activation(gate, gate, ACT.Tanh, scale=1.0 / CAP).then_inc(s_tanh, 1)
            act.wait_ge(s_gabs, 1)
            nc.scalar.activation(gtmp, gtmp, ACT.Exp, scale=-1.0).then_inc(s_gln, 1)
            act.wait_ge(s_gln, 1)
            nc.scalar.activation(gtmp, gtmp, ACT.Ln, bias=1.0).then_inc(s_gln, 1)
            act.wait_ge(s_bR, 1)
            nc.scalar.activation(eiR, nmxR, ACT.Exp, bias=colR[:, 0:1])
            nc.scalar.activation(emR, emR, ACT.Exp, scale=-1.0)
            nc.scalar.activation(ainR, aR, ACT.Exp, bias=colR[:, 2:3])
            nc.scalar.activation(row[:, 5, :], row[:, 5, :], ACT.Exp).then_inc(s_gexp, 1)
            with act.Fori(0, NT) as c:
                act.wait_ge(s_qkps, c + 1)
                nc.scalar.activation(qT, ps[0:DQK, 0, :].rearrange("p (h t) -> p h t", h=MH), ACT.Copy, scale=DQK ** -0.5)
                nc.scalar.activation(qeT, ps[0:DQK, 2, :].rearrange("p (h t) -> p h t", h=MH), ACT.Copy, scale=DQK ** -0.5)\
                  .then_inc(s_qTs, 1)
                act.wait_ge(s_arg, c + 1)
                nc.scalar.activation(wexp, wexp, ACT.Exp).then_inc(s_we, 1)
            for c in range(NT):
                ins = nc.scalar.activation(Pm[:, c, C_MO:C_MO + 512], Pm[:, c, C_MO:C_MO + 512], ACT.Sigmoid)
            ins.then_inc(s_mo, 1)
            act.wait_ge(s_h, NT + 2)
            nc.scalar.activation(hn, hn, ACT.Sqrt).then_inc(s_hsd, 1)

            act.wait_ge(s_ya, NT)
            nc.scalar.activation(gts, Pm[:, :, C_NG:C_NG + 24], ACT.Sigmoid).then_inc(s_gts, 1)
            for j in range(1, 4, 2):
                act.wait_ge(s_kvps, j + 1)
                nc.scalar.activation((ksT, kwT)[j // 2][:, 512:1024], ps[:, j, :], ACT.Copy).then_inc(s_kvT, 1)
            act.sem_inc(s_ev[1], 1)
            act.sem_inc(s_comb, 1)
            act.sem_inc(s_ybd, 16)

            def att_exp(u, h):
                kind, i, lo, blocks, _ = units[u]
                act.wait_ge(s_max, h * NU + (u + 1))
                for b in range(2):
                    n = sum(1 for x in range(u - 1) for q in groups[x] if q % 2 == b) + 1
                    if u >= 2:
                        act.wait_ge(s_pt[b], h * (GA, GB)[b] + n)
                span = ps[:, 2 * (u % 2):2 * (u % 2) + 2, :].rearrange("p b c -> p (b c)")
                n = (i + 1 - lo) * P
                j = 1 if kind == "s" else 2
                ins = nc.scalar.activation(pbuf[u % 2][:, 0:n], span[:, 0:n], ACT.Exp, bias=nmx[:, 3 * i + j:3 * i + j + 1],
                                           accum_out=rsum[:, i, j:j + 1])
                if kind == "w":
                    ins = nc.scalar.activation(pbuf[u % 2][:, 5 * P:5 * P + NCMP], span[:, 5 * P:5 * P + NCMP], ACT.Exp,
                                               bias=nmx[:, 3 * i:3 * i + 1], accum_out=rsum[:, i, 0:1])
                ins.then_inc(s_exp, 1)

            with act.Fori(0, NH) as h:
                act.wait_ge(s_pt[1], h * GB + 1)
                nc.scalar.activation(qTh[:, 512:1024], ps[:, 5, :], ACT.Copy, scale=HD ** -0.5).then_inc(s_ev[1], 1)
                att_exp(0, h)
                att_exp(1, h)
                nb = 1
                for u in range(NU):
                    for q, g in zip(groups[u], units[u][4]):
                        if q % 2 == 1:
                            nb += 1
                            act.wait_ge(s_pt[1], h * GB + nb)
                            if u >= 2:
                                act.wait_ge(s_pv, h * NU + (u - 1))
                            j = units[u][4].index(g)
                            full = sum(1 for c, w, b in g if w == P)
                            if full:
                                ins = nc.scalar.activation(ptbuf[u % 2][:, j * 512:j * 512 + full * P], ps[:, 5, 0:full * P], ACT.Copy)
                            if full < len(g):
                                ins = nc.scalar.activation(ptbuf[u % 2][0:NCMP, j * 512 + full * P:j * 512 + (full + 1) * P],
                                                           ps[0:NCMP, 5, full * P:(full + 1) * P], ACT.Copy)
                            ins.then_inc(s_ev[1], 1)
                    if u + 2 < NU:
                        att_exp(u + 2, h)
                    if u % 2 == 1:
                        i = u // 2
                        act.wait_ge(s_pv, h * NU + (u + 1))
                        if i == 0:
                            act.wait_ge(s_ybd, h * 16 + 16)
                        nc.scalar.activation(ost[:, i * P:(i + 1) * P], ps[0:HD, 6 + i % 2, 0:P], ACT.Copy).then_inc(s_comb, 1)

            act.wait_ge(s_cg, 1)
            for x in (sg, hg):
                nc.scalar.activation(x[:, 4:7], x[:, 4:7], ACT.Exp)
            act.wait_ge(s_smp, 16 * 34)
            nc.scalar.activation(hg[:, 7:8], hg[:, 7:8], ACT.Exp, scale=-1.0).then_inc(s_cge, 1)
            act.wait_ge(s_sh2, 1)
            nc.scalar.activation(hg[:, 9:10], hg[:, 9:10], ACT.Sqrt).then_inc(s_shd, 1)
            nc.scalar.activation(hmo, hmo, ACT.Sigmoid)
            nc.scalar.activation(sgt, sgt, ACT.Sigmoid).then_inc(s_shd, 1)
            with act.Fori(0, NS) as b:
                act.wait_ge(s_pgps, 2 * b + 1)
                nc.scalar.activation(pT[:, 0:512], ps[:, 4, :], ACT.Copy)
                act.wait_ge(s_pgps, 2 * b + 2)
                nc.scalar.activation(wT, ps[:, 6, :], ACT.Copy).then_inc(s_pga, 1)
            for n, x, j in ((1, Scm, 0), (2, Swn, 2), (3, Ssl, 1)):
                act.wait_ge(s_softm, n)
                nc.scalar.activation(x, x, ACT.Exp, bias=small[:, j:j + 1], accum_out=small[:, 4 + j:5 + j]).then_inc(s_softe, 1)
            act.wait_ge(s_sPT, 1)
            nc.scalar.activation(PTs[:, 0, :], ps[:, 4, :], ACT.Copy).then_inc(s_sPTe, 1)

            with act.Fori(0, 2) as i:
                for j in range(2):
                    ins = nc.scalar.activation(bnow[:, 4 * j:4 * j + 4], vecT[:, bass.ds(i * 4 + (48 + 8 * j), 4)], ACT.Copy)
                ins.then_inc(s_act, 1)
                act.wait_ge(s_act, i + 1)
                for s in range(2):
                    for m in range(2):
                        for q in range(3):
                            u = (s * 2 + m) * 3 + q
                            act.wait_ge(s_mgps, i * 12 + (u + 1))
                            act.wait_ge(s_mgdve, i * 12 + (u + 1))
                            for j in range(2):
                                ins = nc.scalar.activation(sgm[2 * (u % 2) + j], ps[:, 4 * (u % 2) + j, 0:TG], ACT.Sigmoid,
                                                           bias=bnow[:, 4 * j + 2 * s + m:4 * j + 2 * s + m + 1])
                            ins.then_inc(s_mgact, 1)
                act.wait_ge(s_mgact, i * 12 + 12)

            act.sem_inc(s_woact, 3)
            with act.Fori(0, 2) as i:
                for s in range(2):
                    for u in range(0, 6, 2):
                        act.wait_ge(s_wops, i * 12 + (s * 6 + u + 1))
                        nc.scalar.activation(flat(yT1)[:, bass.ds(i * 4 * TOK + (s * 6 + u) * TG, TG)], ps[:, u, 0:TG], ACT.Copy).then_inc(s_woact, 1)
            def post_act(rnd):
                for n in range(NT + 1):
                    r = P if n < NT else NS
                    act.wait_ge(s_ytps, (NT + 1) * rnd + n + 1)
                    b = 2 * (n % 2)
                    nc.scalar.activation(junk[0:r, :], ps[0:r, b:b + 2, :].rearrange("p b c -> p (b c)"), ACT.Square,
                                         accum_out=ss[0:r, n:n + 1]).then_inc(s_ytsq, 1)
                    act.wait_ge(s_ytsq, (NT + 1) * rnd + n + 1)
                act.wait_ge(s_ms, 2 * rnd + 2)
                nc.scalar.activation(rstd[:, :], rstd[:, :], ACT.Sqrt).then_inc(s_sd, 1)
            post_act(0)
            for n in range(NT + 1):
                act.wait_ge(s_out2, n + 1)
                r, src = (P, xres[:, n, :]) if n < NT else (NS, xress)
                nc.scalar.activation(junk[0:r, :], src, ACT.Square, accum_out=ss[0:r, n:n + 1]).then_inc(s_ss2, 1)
                act.wait_ge(s_ss2, n + 1)
            act.wait_ge(s_ms, 3)
            nc.scalar.activation(rstd[:, :], rstd[:, :], ACT.Sqrt).then_inc(s_sd, 1)
            h_act(1)
            with act.Fori(0, KF // 2) as i:
                for s in range(2):
                    for q in range(3):
                        u = s * 3 + q
                        act.wait_ge(s_upps, i * 6 + (u + 1))
                        act.wait_ge(s_updve, i * 6 + (u + 1))
                        nc.scalar.activation(sil[u % 2], ps[:, 2 * q, 0:TG], ACT.Silu).then_inc(s_upact, 1)
            with act.Fori(0, KD // 2) as i:
                for u in range(0, 6, 2):
                    act.wait_ge(s_wops, i * 6 + (24 + u + 1))
                    nc.scalar.activation(flat(hT)[:, bass.ds(i * 2 * TOK + u * TG, TG)], ps[:, u, 0:TG], ACT.Copy).then_inc(s_woact, 1)
            post_act(1)

        @block.vector
        def _(dve):
            own = Tally(s_dve)

            def step(ins):
                ins.then_inc(s_dve, 1)
                own.n += 1
                dve.wait_ge(s_dve, own.value())

            nc.vector.memset(ss[:, :], 1.0).then_inc(s_ss, 1)
            dve.sem_inc(s_xT_dve, 2)
            dve.wait_ge(s_vT, 1)
            step(nc.vector.tensor_copy(vecT[:, :], ps[:, 6, 0:96]))
            dve.wait_ge(s_ss, 10)
            nc.vector.tensor_scalar(rstd[:, :], ss[:, :], 1.0 / D, EPS, ALU.mult, ALU.add).then_inc(s_ms, 1)
            dve.wait_ge(s_sd, 1)
            step(nc.vector.reciprocal(rstd[:, :], rstd[:, :]))
            dve.wait_ge(s_modps, 1)
            step(nc.vector.tensor_tensor(modT[:, :, :], ps[:, 0, 0:432].rearrange("p (m c) -> p m c", c=9),
                                         vecT[:, 0:48].unsqueeze(2).to_broadcast([P, 48, 9]), ALU.add))

            def feat(lo):
                return vecT[:, lo:lo + 8].unsqueeze(2).to_broadcast([P, KD, 9])
            nc.vector.scalar_tensor_tensor(sc1[:, :, :], modT[:, 8:16, :], 1.0, feat(64), ALU.add, ALU.mult)
            nc.vector.scalar_tensor_tensor(sc2[:, :, :], modT[:, 32:40, :], 1.0, feat(72), ALU.add, ALU.mult)
            nc.vector.tensor_tensor(gg1[:, :, :], modT[:, 16:24, :], feat(80), ALU.mult)
            step(nc.vector.tensor_tensor(gg2[:, :, :], modT[:, 40:48, :], feat(88), ALU.mult))
            dve.sem_inc(s_mod, 1)
            def h_dve(rnd, rows_p, rows_s):
                sc, sh = (sc1, sc2)[rnd], 24 * rnd
                with dve.Fori(0, NT // 2) as i:
                    for s in range(2):
                        dve.wait_ge(s_xT_dve, 2 * i + (NT * rnd + s + 1))
                        tile = i * 2 + s
                        nc.vector.tensor_scalar(xn[:, s, :], rows_p[:, bass.ds(tile, 1), :].rearrange("p a b -> p (a b)"),
                                                rstd[:, bass.ds(tile, 1)], None, ALU.mult).then_inc(s_xn, 1)
                        dve.wait_ge(s_xT, 2 * i + (NT * rnd + s + 1))
                        for k in range(KD // 2, KD):
                            ins = nc.vector.tensor_scalar(hT[:, k, bass.ds(i * 256 + s * P, P)],
                                                          ps[:, 2 * s + k // 4, (k % 4) * P:(k % 4 + 1) * P],
                                                          sc[:, k, 0:1], modT[:, sh + k, 0:1], ALU.mult, ALU.add)
                        ins.then_inc(s_xT_dve, 1)
                dve.wait_ge(s_xT_dve, NT * rnd + NT + 2)
                nc.vector.tensor_scalar(xn[0:NS, 0, :], rows_s, rstd[0:NS, 8:9], None, ALU.mult).then_inc(s_xn, 1)
                dve.wait_ge(s_sT, rnd + 1)
                sT = ps[:, 4, 0:64].rearrange("p (k c) -> p k c", c=NS)
                step(nc.vector.tensor_tensor(hT[:, :, SEQ:TOK], sT, sc[:, :, 1:9], ALU.mult))
                nc.vector.tensor_tensor(hT[:, :, SEQ:TOK], hT[:, :, SEQ:TOK], modT[:, sh:sh + 8, 1:9], ALU.add).then_inc(s_sh, 1)
            h_dve(0, xin, xs)

            dve.sem_inc(s_mix, 4)
            dve.wait_ge(s_bmix, 16)
            with dve.Fori(0, MIX // PB // 2) as i:
                for s in range(2):
                    for n in range(9):
                        dve.wait_ge(s_mixps, i * 18 + (s * 9 + n + 1))
                        cols = bass.ds(i * 2 * PB + s * PB, PB)
                        rows, dst = (P, Pm[:, n, cols]) if n < NT else (NS, Ps[:, cols])
                        nc.vector.tensor_tensor(dst, ps[0:rows, n % 4 if n < NT else 4, 0:PB], bmix[0:rows, cols],
                                                ALU.add).then_inc(s_mix, 1)
            dve.wait_ge(s_mix, 4 + 72)
            for rows, pm, lead in ((P, Pm, [NT]), (NS, Ps, [])):
                for lo, heads in ((C_NQ, NH), (C_KV, NKV), (C_KV + 256, NKV), (C_KV + 512, NKV)):
                    h8 = heads * 8
                    if lead:
                        v = pm[:, :, lo:lo + heads * HD].rearrange("p t (h d) -> p t h d", d=HD)
                        x1, x2 = v[:, :, :, 0:8], v[:, :, :, 8:16]
                        tmp = [xn[:, j // 2, (j % 2) * 512:(j % 2) * 512 + NT * h8].rearrange("p (t h d) -> p t h d", t=NT, d=8)
                               for j in range(4)]
                        co, si = (cst(c).rearrange("p (t d) -> p t d", t=NT).unsqueeze(2).to_broadcast([P, NT, heads, 8])
                                  for c in ("cos", "sin"))
                    else:
                        v = pm[:, lo:lo + heads * HD].rearrange("p (h d) -> p h d", d=HD)
                        x1, x2 = v[:, :, 0:8], v[:, :, 8:16]
                        tmp = [xn[0:NS, j // 2, (j % 2) * 512:(j % 2) * 512 + h8].rearrange("p (h d) -> p h d", d=8)
                               for j in range(4)]
                        co, si = (cst(c, NS).unsqueeze(1).to_broadcast([NS, heads, 8]) for c in ("scos", "ssin"))
                    nc.vector.tensor_tensor(tmp[0], x1, co, ALU.mult)
                    nc.vector.tensor_tensor(tmp[1], x2, si, ALU.mult)
                    nc.vector.tensor_tensor(tmp[2], x2, co, ALU.mult)
                    step(nc.vector.tensor_tensor(tmp[3], x1, si, ALU.mult))
                    nc.vector.tensor_tensor(x1, tmp[0], tmp[1], ALU.subtract)
                    step(nc.vector.tensor_tensor(x2, tmp[2], tmp[3], ALU.add))
            dve.sem_inc(s_rope, 1)

            step(nc.vector.memset(gate, 0.0))
            dve.wait_ge(s_rope, 1)
            step(nc.vector.tensor_copy(gate[:, 0:NT, :], Pm[:, :, C_MI:C_MI + 8]))
            nc.vector.tensor_copy(gate[0:NS, NT, :], Ps[:, C_MI:C_MI + 8]).then_inc(s_gate, 1)
            dve.wait_ge(s_tanh, 1)
            g4 = gate.rearrange("p t (a h) -> p t a h", a=2)
            lf3, gi3, gt3 = (x.rearrange("p (t h) -> p t h", h=MH) for x in (lf, gi, gtmp))
            nc.vector.tensor_scalar(gi3, g4[:, :, 0, :], CAP, None, ALU.mult)
            step(nc.vector.tensor_scalar(lf3, g4[:, :, 1, :], CAP, None, ALU.mult))
            nc.vector.scalar_tensor_tensor(gtmp, lf, -1.0, lf, ALU.mult, ALU.max).then_inc(s_gabs, 1)
            dve.wait_ge(s_gln, 2)
            nc.vector.scalar_tensor_tensor(lf, lf, 0.0, gtmp, ALU.min, ALU.subtract).then_inc(s_gate, 1)
            dve.wait_ge(s_gRps, 1)
            nc.vector.tensor_copy(iR, ps[0:32, 5, 0:P])
            step(nc.vector.tensor_copy(fR, ps[0:32, 5, P:2 * P]))
            dve.wait_ge(s_ones, 1)
            step(nc.vector.tensor_tensor_scan(bR, ones[0:32, :], fR, 0.0, ALU.mult, ALU.add))
            step(nc.vector.tensor_tensor(aR, iR, bR, ALU.subtract))
            step(nc.vector.tensor_tensor_scan(AR, ones[0:32, :], aR, -3e38, ALU.mult, ALU.max))
            dve.sem_inc(s_gR, 1)
            dve.wait_ge(s_rowps, 1)
            step(nc.vector.tensor_copy(row[:, 0:2, :], ps[0:1, 5, 0:64].rearrange("p (a b) -> p a b", a=2)))
            for h in range(MH):
                ins = nc.vector.tensor_tensor_scan(row[:, 2, h::MH], row[:, 0, h::MH], row[:, 1, h::MH], 0.0, ALU.max, ALU.add)
            nc.vector.memset(row[:, 3, 0:MH], 0.0)
            step(nc.vector.memset(row[:, 4, :], 0.0))
            step(nc.vector.tensor_copy(row[:, 3, MH:32], row[:, 2, 0:32 - MH]))
            step(nc.vector.tensor_tensor(row[:, 4, :], row[:, 0, :], row[:, 3, :], ALU.max))
            nc.vector.tensor_tensor(row[:, 5, :], row[:, 3, :], row[:, 4, :], ALU.subtract).then_inc(s_rowsb, 1)
            dve.wait_ge(s_colps, 1)
            step(nc.vector.tensor_copy(colR[:, 0:2], ps[0:32, 6, 0:2]))
            step(nc.vector.tensor_scalar(colR[:, 2:3], colR[:, 1:2], -1.0, None, ALU.mult))
            step(nc.vector.tensor_scalar(nmxR, AR, colR[:, 0:1], -1.0, ALU.max, ALU.mult))
            nc.vector.tensor_tensor(emR, bR, nmxR, ALU.subtract).then_inc(s_bR, 1)
            dve.wait_ge(s_tokps, 1)
            nc.vector.tensor_copy(tok, ps[:, 5, 0:P].rearrange("p (a b) -> p a b", a=4))
            step(nc.vector.tensor_copy(astB, ps[:, 5, P:P + 32]))
            nc.vector.memset(Cst[:, :, :], 0.0).then_inc(s_tok, 1)
            dve.wait_ge(s_tok, 1)
            dve.sem_inc(s_C, 1)
            dve.sem_inc(s_h, 1)
            with dve.Fori(0, NT) as c:
                own.loop(c, 4)
                dve.wait_ge(s_qkps, c + 1)
                nc.vector.tensor_copy(kT, ps[0:DQK, 1, :].rearrange("p (h t) -> p h t", h=MH)).then_inc(s_kTs, 1)
                dve.wait_ge(s_zps, c + 1)
                for h in range(MH):
                    ins = nc.vector.scalar_tensor_tensor(wexp[:, h, :], ps[:, 3, h * P:(h + 1) * P],
                                                         tok[:, 0, bass.ds(c * MH + h, 1)], cst("causal_st"),
                                                         ALU.add, ALU.min)
                ins.then_inc(s_arg, 1)
                dve.wait_ge(s_we, c + 1)
                dve.wait_ge(s_Sps, c + 1)
                nc.vector.tensor_tensor(wgt, wexp, ps[:, 4, :].rearrange("p (h t) -> p h t", h=MH), ALU.mult).then_inc(s_w, 1)
                dve.wait_ge(s_st, c + 2)
                for h in range(MH):
                    src = ps[0:DQK, 7 if h < 2 else 0, (h % 2) * (DV + 1):(h % 2 + 1) * (DV + 1)]
                    ins = nc.vector.scalar_tensor_tensor(Cst[:, h, :], Cst[:, h, :], astB[0:DQK, bass.ds(c * MH + h, 1)],
                                                         src, ALU.mult, ALU.add)
                ins.then_inc(s_C, 1)
                num = ps[:, 5:7, 0:2 * (DV + 1)].rearrange("p b (j e) -> p b j e", e=DV + 1)
                step(nc.vector.tensor_copy(dn.rearrange("p (b j) -> p b j", b=2), num[:, :, :, DV]))
                step(nc.vector.scalar_tensor_tensor(dn, dn, -1.0, dn, ALU.mult, ALU.max))
                step(nc.vector.tensor_tensor(dn, dn, tok[:, 2, bass.ds(c * MH, MH)], ALU.max))
                step(nc.vector.reciprocal(dn, dn))
                pm = Pm[:, bass.ds(c, 1), 512:1024].rearrange("p a (b j v) -> p (a b) j v", b=2, v=DV)
                for b in range(2):
                    ins = nc.vector.tensor_tensor(pm[:, b, :, :], num[:, b, :, 0:DV],
                                                  dn[:, 2 * b:2 * b + 2].unsqueeze(2).to_broadcast([P, 2, DV]), ALU.mult)
                ins.then_inc(s_h, 1)
            own.end(NT)
            dve.wait_ge(s_h, NT + 1)
            H4 = Pm[:, :, 512:1024].rearrange("p t (h v) -> p t h v", v=DV)
            for c in range(NT):
                step(nc.vector.tensor_tensor(wexp, H4[:, c], H4[:, c], ALU.mult))
                step(nc.vector.tensor_reduce(hn[:, c * MH:(c + 1) * MH], wexp, AX.X, ALU.add))
            nc.vector.tensor_scalar(hn, hn, 1.0 / DV, EPS, ALU.mult, ALU.add).then_inc(s_h, 1)
            dve.wait_ge(s_hsd, 1)
            step(nc.vector.reciprocal(hn, hn))
            dve.wait_ge(s_mo, 1)
            for c in range(NT):
                sl = H4[:, c]
                step(nc.vector.tensor_tensor(sl, sl, hn[:, c * MH:(c + 1) * MH].unsqueeze(2).to_broadcast([P, MH, DV]), ALU.mult))
                step(nc.vector.tensor_tensor(Pm[:, c, 512:1024], Pm[:, c, 512:1024], mnormB[:, :], ALU.mult))
                nc.vector.tensor_tensor(Pm[:, c, 512:1024], Pm[:, c, 512:1024], Pm[:, c, C_MO:C_MO + 512], ALU.mult).then_inc(s_y, 1)
            for c in range(NT):
                dve.wait_ge(s_yT, c + 1)
                nc.vector.tensor_copy(yaT[:, :, c * P:(c + 1) * P], ps[:, c % 4, :].rearrange("p (h t) -> p h t", h=MH)).then_inc(s_ya, 1)

            for j in range(0, 4, 2):
                dve.wait_ge(s_kvps, j + 1)
                nc.vector.tensor_copy((ksT, kwT)[j // 2][:, 0:512], ps[:, j, :]).then_inc(s_kvT, 1)
            dve.wait_ge(s_cps, 1)
            nc.vector.tensor_copy(kcT, ps[:, 0, 0:NCMP]).then_inc(s_cT2, 1)
            nc.vector.tensor_copy(vc, ps[0:NCMP, 0, 64:64 + NKV * HD]).then_inc(s_cT2, 1)
            dve.sem_inc(s_ev[0], 1)
            dve.wait_ge(s_gts, 1)

            def att_max(u, h):
                kind, i, lo, blocks, _ = units[u]
                span = ps[:, 2 * (u % 2):2 * (u % 2) + 2, :].rearrange("p b c -> p (b c)")
                n = (i + 1 - lo) * P
                dve.wait_ge(s_S, h * NU + (u + 1))
                ins = nc.vector.tensor_tensor(span[:, n - P:n], span[:, n - P:n], cst("causal_ts"), ALU.add)
                if kind == "w":
                    cm = span[:, 5 * P:5 * P + NCMP]
                    ins = nc.vector.tensor_tensor(cm, cm, cst("cmp_add")[:, i * NCMP:(i + 1) * NCMP], ALU.add)
                    if i >= WIN // P:
                        ins = nc.vector.tensor_tensor(span[:, 0:P], span[:, 0:P], cst("window_ts"), ALU.add)
                step(ins)
                if kind == "w":
                    nc.vector.tensor_reduce(nmx[:, 3 * i:3 * i + 1], span[:, 5 * P:5 * P + NCMP], AX.X, ALU.max, negate=True)
                j = 1 if kind == "s" else 2
                nc.vector.tensor_reduce(nmx[:, 3 * i + j:3 * i + j + 1], span[:, 0:n], AX.X, ALU.max, negate=True)\
                  .then_inc(s_max, 1)

            with dve.Fori(0, NH) as h:
                own.loop(h, 3 * NU)
                dve.wait_ge(s_pt[0], h * GA + 1)
                nc.vector.tensor_scalar(qTh[:, 0:512], ps[:, 4, :], HD ** -0.5, None, ALU.mult).then_inc(s_ev[0], 1)
                att_max(0, h)
                att_max(1, h)
                na = 1
                for u in range(NU):
                    kind, i, lo, blocks, gr = units[u]
                    dve.wait_ge(s_exp, h * NU + (u + 1))
                    js = (1,) if kind == "s" else (0, 2)
                    span_j = slice(js[0], js[-1] + 1, 2 if kind == "w" else 1)
                    step(nc.vector.reciprocal(gsc[:, i, span_j], rsum[:, i, span_j]))
                    step(nc.vector.tensor_tensor(gsc[:, i, span_j], gsc[:, i, span_j],
                                                 gts[:, i, bass.ds(h * 3, 3)][:, span_j], ALU.mult))
                    n = (i + 1 - lo) * P
                    pb = pbuf[u % 2]
                    if kind == "w":
                        cm = pb[:, 5 * P:5 * P + NCMP]
                        if i == 0:
                            nc.vector.scalar_tensor_tensor(cm, cm, gsc[:, i, 0:1], cst("cmp_one")[:, 0:NCMP], ALU.mult, ALU.mult)
                        else:
                            nc.vector.tensor_scalar(cm, cm, gsc[:, i, 0:1], None, ALU.mult)
                    nc.vector.tensor_scalar(pb[:, 0:n], pb[:, 0:n], gsc[:, i, js[-1]:js[-1] + 1], None, ALU.mult).then_inc(s_one, 1)
                    for j, (q, g) in enumerate(zip(groups[u], gr)):
                        if q % 2 == 0:
                            na += 1
                            dve.wait_ge(s_pt[0], h * GA + na)
                            if u >= 2:
                                dve.wait_ge(s_pv, h * NU + (u - 1))
                            full = sum(1 for c, w, b in g if w == P)
                            if full:
                                ins = nc.vector.tensor_copy(ptbuf[u % 2][:, j * 512:j * 512 + full * P], ps[:, 4, 0:full * P])
                            if full < len(g):
                                ins = nc.vector.tensor_copy(ptbuf[u % 2][0:NCMP, j * 512 + full * P:j * 512 + (full + 1) * P],
                                                            ps[0:NCMP, 4, full * P:(full + 1) * P])
                            ins.then_inc(s_ev[0], 1)
                    if u + 2 < NU:
                        att_max(u + 2, h)
            own.end(NH)

            dve.wait_ge(s_smp, 16 * 34)
            for x in (sg, hg):
                step(nc.vector.tensor_tensor(x[:, 6:7], x[:, 1:2], x[:, 2:3], ALU.add))
                step(nc.vector.tensor_tensor(x[:, 3:4], x[:, 6:7], x[:, 0:1], ALU.max))
                nc.vector.tensor_tensor(x[:, 4:5], x[:, 0:1], x[:, 3:4], ALU.subtract)
                step(nc.vector.tensor_tensor(x[:, 5:6], x[:, 6:7], x[:, 3:4], ALU.subtract))
                step(nc.vector.memset(x[:, 6:8], 0.0))
            nc.vector.tensor_copy(hg[:, 7:8], hg[:, 3:4]).then_inc(s_cg, 1)
            step(nc.vector.tensor_scalar(sq, sq, DQK ** -0.5, None, ALU.mult))
            step(nc.vector.tensor_tensor(sT_, sC, sq.unsqueeze(2).to_broadcast([P, DQ, DV]), ALU.mult))
            nc.vector.tensor_reduce(sW[:, 0:DV], sT_.rearrange("p a v -> p v a"), AX.X, ALU.add)
            step(nc.vector.tensor_tensor(hsum[:, 0, :], sq, sk, ALU.mult))
            step(nc.vector.tensor_tensor(hsum[:, 1, :], sq, sn, ALU.mult))
            nc.vector.tensor_reduce(sW[:, DV:DV + 2], hsum, AX.X, ALU.add).then_inc(s_sWd, 1)
            dve.wait_ge(s_cge, 1)
            dve.wait_ge(s_sWd, 1)
            step(nc.vector.tensor_scalar(sk, sk, sg[:, 4:5], None, ALU.mult))
            step(nc.vector.tensor_tensor(sT_, sk.unsqueeze(2).to_broadcast([P, DQ, DV]),
                                         sv.unsqueeze(1).to_broadcast([P, DQ, DV]), ALU.mult))
            nc.vector.scalar_tensor_tensor(sC, sC, sg[:, 5:6], sT_, ALU.mult, ALU.add)
            step(nc.vector.scalar_tensor_tensor(sn, sn, sg[:, 5:6], sk, ALU.mult, ALU.add))
            dve.sem_inc(s_sCn, 1)
            dve.wait_ge(s_sWp, 1)
            step(nc.vector.tensor_copy(hs, ps[0:32, 0, 0:DV + 2]))
            step(nc.vector.tensor_tensor(hg[:, 8:9], hs[:, DV:DV + 1], hg[:, 4:5], ALU.mult))
            step(nc.vector.tensor_scalar(hv, hv, hg[:, 8:9], None, ALU.mult))
            step(nc.vector.scalar_tensor_tensor(hv, hs[:, 0:DV], hg[:, 5:6], hv, ALU.mult, ALU.add))
            step(nc.vector.scalar_tensor_tensor(hg[:, 8:9], hs[:, DV + 1:DV + 2], hg[:, 5:6], hg[:, 8:9], ALU.mult, ALU.add))
            step(nc.vector.scalar_tensor_tensor(hg[:, 8:9], hg[:, 8:9], -1.0, hg[:, 8:9], ALU.mult, ALU.max))
            step(nc.vector.tensor_tensor(hg[:, 8:9], hg[:, 8:9], hg[:, 7:8], ALU.max))
            step(nc.vector.reciprocal(hg[:, 8:9], hg[:, 8:9]))
            step(nc.vector.tensor_scalar(hv, hv, hg[:, 8:9], None, ALU.mult))
            step(nc.vector.tensor_tensor(hsq, hv, hv, ALU.mult))
            step(nc.vector.tensor_reduce(hg[:, 9:10], hsq, AX.X, ALU.add))
            nc.vector.tensor_scalar(hg[:, 9:10], hg[:, 9:10], 1.0 / DV, EPS, ALU.mult, ALU.add).then_inc(s_sh2, 1)
            dve.wait_ge(s_shd, 2)
            step(nc.vector.reciprocal(hg[:, 9:10], hg[:, 9:10]))
            step(nc.vector.tensor_scalar(hv, hv, hg[:, 9:10], None, ALU.mult))
            step(nc.vector.tensor_tensor(hv, hv, hw, ALU.mult))
            nc.vector.tensor_tensor(hv, hv, hmo, ALU.mult).then_inc(s_sh2, 1)
            step(nc.vector.memset(Qall, 0.0))
            nc.vector.memset(zrow, 0.0).then_inc(s_zero, 1)
            dve.wait_ge(s_Qps, 1)
            for g in range(NKV):
                nc.vector.tensor_scalar(Qall[g * HD:(g + 1) * HD, :, g * HPG:(g + 1) * HPG].rearrange("p b h -> p h b"),
                                        ps[0:HD, 1, g * HPG * NS:(g + 1) * HPG * NS].rearrange("p (h b) -> p h b", b=NS),
                                        HD ** -0.5, None, ALU.mult)
            step(nc.vector.tensor_copy(knT, ps[:, 1, 64:80].rearrange("p (a b) -> p a b", a=2)))
            dve.sem_inc(s_Qall, 1)
            dve.wait_ge(s_syT, 1)
            nc.vector.tensor_copy(yaT[:, :, SEQ:TOK], ps[:, 2, 0:32].rearrange("p (b h) -> p h b", h=MH)).then_inc(s_sya, 1)
            with dve.Fori(0, NS) as b:
                dve.wait_ge(s_free, b + 2)
                nc.vector.tensor_tensor(Qpad, Qall, cst("onehot")[:, bass.ds(b * NS, NS)].unsqueeze(2).to_broadcast([P, NS, NH]),
                                        ALU.mult).then_inc(s_qp, 1)
                dve.wait_ge(s_pgps, 2 * b + 1)
                nc.vector.tensor_copy(pT[:, 512:1024], ps[:, 5, :])
                dve.wait_ge(s_pgps, 2 * b + 2)
                nc.vector.tensor_copy(ckT, ps[:, 7, 0:NCMP])
                nc.vector.tensor_scalar(vcs[:, bass.ds(b, 1), :].rearrange("p a c -> p (a c)"),
                                        ps[0:NCMP, 7, 64:64 + NKV * HD], 1.0, None, ALU.mult).then_inc(s_pgd, 1)
            dve.wait_ge(s_free, 2 + NS)
            dve.wait_ge(s_soft, 1)
            nc.vector.tensor_copy(Scm, ps[0:SR, 3, 64:64 + NCMP])
            step(nc.vector.tensor_copy(Swn[:, 0:WIN], ps[0:SR, 2, :]))
            nc.vector.tensor_tensor(Swn[:, WIN:], ps[0:SR, 3, 8:16], cst("own_new", SR), ALU.add)
            nc.vector.tensor_tensor(Ssl[:, PAST:], ps[0:SR, 3, 0:8], cst("own_new", SR), ALU.add)
            step(nc.vector.memset(Swn[:, 0:1], NEG))
            nc.vector.tensor_reduce(small[:, 0:1], Scm, AX.X, ALU.max, negate=True).then_inc(s_softm, 1)
            nc.vector.tensor_reduce(small[:, 2:3], Swn, AX.X, ALU.max, negate=True).then_inc(s_softm, 1)
            dve.wait_ge(s_softe, 1)
            step(nc.vector.reciprocal(small[:, 8:9], small[:, 4:5]))
            nc.vector.tensor_scalar(pcm, Scm, small[:, 8:9], None, ALU.mult).then_inc(s_soft, 1)
            dve.wait_ge(s_impps, 1)
            step(nc.vector.tensor_reduce(imp, ps[0:SR, 7, 0:NCMP].rearrange("p (k r) -> p k r", r=2), AX.X, ALU.add))
            step(nc.vector.tensor_reduce(small[:, 9:10], imp[:, 1:16], AX.X, ALU.min))
            step(nc.vector.scalar_tensor_tensor(imp[:, 1:16], imp[:, 1:16], small[:, 9:10], cst("blk", SR)[:, 1:16],
                                                ALU.is_equal, ALU.mult))
            step(nc.vector.tensor_reduce(small[:, 10:11], imp[:, 1:16], AX.X, ALU.max))
            step(nc.vector.tensor_scalar(msk, cst("blk", SR), small[:, 10:11], NEG, ALU.is_equal, ALU.mult))
            for j in range(2):
                ins = nc.vector.tensor_tensor(Ssl[:, j * 512:(j + 1) * 512].rearrange("p (k c) -> p k c", c=SEL),
                                              ps[0:SR, j, :].rearrange("p (k c) -> p k c", c=SEL),
                                              msk[:, j * 8:(j + 1) * 8].unsqueeze(2).to_broadcast([SR, 8, SEL]), ALU.add)
            step(ins)
            nc.vector.tensor_reduce(small[:, 1:2], Ssl, AX.X, ALU.max, negate=True).then_inc(s_softm, 1)
            dve.wait_ge(s_softe, 3)
            step(nc.vector.reciprocal(small[:, 4:7], small[:, 4:7]))
            step(nc.vector.tensor_tensor(small[:, 4:7], small[:, 4:7], sgt, ALU.mult))
            for j, x in ((0, Scm), (1, Ssl), (2, Swn)):
                ins = nc.vector.tensor_scalar(x, x, small[:, 4 + j:5 + j], None, ALU.mult)
            step(ins)
            dve.sem_inc(s_soft, 1)
            dve.wait_ge(s_sPT, 1)
            nc.vector.tensor_copy(PTw[:, 0:256], ps[:, 5, 0:256])
            nc.vector.tensor_copy(PTw[0:NCMP, 256:320], ps[0:NCMP, 5, 256:320])
            nc.vector.tensor_copy(PTw[0:NS, 320:448], ps[0:NS, 5, 320:448]).then_inc(s_sPTe, 1)
            dve.wait_ge(s_Osum, 1)
            for h in range(NH):
                g, odd = h // HPG, h % 2
                ins = nc.vector.tensor_copy(ybT[odd * HD:(odd + 1) * HD, h // 2, SEQ:TOK],
                                            ps[g * HD:(g + 1) * HD, 6, h:SR:NH])
            ins.then_inc(s_yb, 1)

            dve.sem_inc(s_mgdve, 2)
            with dve.Fori(0, 2) as i:
                own.loop(i, 12)
                for s in range(2):
                    for m in range(2):
                        for q in range(3):
                            u = (s * 2 + m) * 3 + q
                            dve.wait_ge(s_mgact, i * 12 + (u + 1))
                            nc.vector.tensor_tensor(sgm[2 * (u % 2)], sgm[2 * (u % 2)], ps[:, 4 * (u % 2) + 2, 0:TG], ALU.mult)
                            step(nc.vector.tensor_tensor(sgm[2 * (u % 2) + 1], sgm[2 * (u % 2) + 1],
                                                         ps[:, 4 * (u % 2) + 3, 0:TG], ALU.mult))
                            nc.vector.tensor_tensor(merT[:, bass.ds(i * 4 + (s * 2 + m), 1), q * TG:(q + 1) * TG]
                                                    .rearrange("p a c -> p (a c)"),
                                                    sgm[2 * (u % 2)], sgm[2 * (u % 2) + 1], ALU.add).then_inc(s_mgdve, 1)
            own.end(2)
            dve.sem_inc(s_wodve, 3)
            with dve.Fori(0, 2) as i:
                for s in range(2):
                    for u in range(1, 6, 2):
                        dve.wait_ge(s_wops, i * 12 + (s * 6 + u + 1))
                        nc.vector.tensor_scalar(yT1[:, bass.ds(i * 4 + (s * 2 + u // 3), 1), (u % 3) * TG:(u % 3 + 1) * TG]
                                                .rearrange("p a c -> p (a c)"), ps[:, u, 0:TG], 1.0, None, ALU.mult)\
                          .then_inc(s_wodve, 1)

            def post_dve(rnd, gg, Gp, Gsm):
                for k in range(KD):
                    ins = nc.vector.tensor_scalar(diag[rnd][:, k * P:(k + 1) * P], ident, gg[:, k, 0:1], None, ALU.mult)
                ins.then_inc(s_diag, 1)
                dve.wait_ge(s_Gps, rnd + 1)
                nc.vector.tensor_copy(Gp, ps[:, 4:6, :].rearrange("p b c -> p (b c)"))
                step(nc.vector.tensor_copy(Gsm, ps[0:NS, 6:8, :].rearrange("p b c -> p (b c)")))
                for n in range(NT + 1):
                    r, dst, g = (P, yt[:, n, :], Gp) if n < NT else (NS, yts, Gsm)
                    b = 2 * (n % 2)
                    dve.wait_ge(s_ytsq, (NT + 1) * rnd + n + 1)
                    nc.vector.tensor_tensor(dst, ps[0:r, b:b + 2, :].rearrange("p b c -> p (b c)"), g, ALU.mult).then_inc(s_ytdve, 1)
                nc.vector.tensor_scalar(rstd[:, :], ss[:, :], 1.0 / D, EPS, ALU.mult, ALU.add).then_inc(s_ms, 1)
                dve.wait_ge(s_ytdve, (NT + 1) * (rnd + 1))
                dve.wait_ge(s_sd, 2 * rnd + 2)
                step(nc.vector.reciprocal(rstd[:, :], rstd[:, :]))
                dve.wait_ge(s_x1in, 32)
                for n in range(NT + 1):
                    r, dst, y = (P, xres[:, n, :], yt[:, n, :]) if n < NT else (NS, xress, yts)
                    nc.vector.scalar_tensor_tensor(dst, y, rstd[0:r, n:n + 1], dst, ALU.mult, ALU.add)\
                      .then_inc(s_out if rnd else s_out2, 1)
            dve.wait_ge(s_mgdve, 26)
            post_dve(0, gg1, G, Gs)
            dve.wait_ge(s_ss2, NT + 1)
            nc.vector.tensor_scalar(rstd[:, :], ss[:, :], 1.0 / D, EPS, ALU.mult, ALU.add).then_inc(s_ms, 1)
            dve.wait_ge(s_sd, 3)
            step(nc.vector.reciprocal(rstd[:, :], rstd[:, :]))
            h_dve(1, xres, xress)
            dve.sem_inc(s_updve, 2)
            with dve.Fori(0, KF // 2) as i:
                for s in range(2):
                    for q in range(3):
                        u = s * 3 + q
                        dve.wait_ge(s_upact, i * 6 + (u + 1))
                        nc.vector.tensor_tensor(aT[:, bass.ds(i * 2 + s, 1), q * TG:(q + 1) * TG].rearrange("p a c -> p (a c)"),
                                                sil[u % 2], ps[:, 2 * q + 1, 0:TG], ALU.mult).then_inc(s_updve, 1)
            with dve.Fori(0, KD // 2) as i:
                for u in range(1, 6, 2):
                    dve.wait_ge(s_wops, i * 6 + (24 + u + 1))
                    nc.vector.tensor_scalar(hT[:, bass.ds(i * 2 + u // 3, 1), (u % 3) * TG:(u % 3 + 1) * TG]
                                            .rearrange("p a c -> p (a c)"), ps[:, u, 0:TG], 1.0, None, ALU.mult)\
                      .then_inc(s_wodve, 1)
            dve.wait_ge(s_woused, 4 + KD)
            post_dve(1, gg2, G2, G2s)

        @block.tensor
        def _(pe):
            pe.wait_ge(s_const, 32)
            pe.wait_ge(s_c, 32)
            for k in range(KD):
                ins = nc.tensor.transpose(ps[:, 7, k * 9:(k + 1) * 9], cin[:, k * P:(k + 1) * P], ident[0:9, 0:9])
            ins.then_inc(s_cT, 1)
            pe.wait_ge(s_vrow, 96)
            nc.tensor.transpose(ps[:, 6, 0:96], vrows, ident[0:96, 0:96]).then_inc(s_vT, 1)
            pe.wait_ge(s_cS, 1)
            with pe.Fori(0, 4) as i:
                for s in range(3):
                    pe.wait_ge(s_ada[s], i * 16 + 16)
                    for m in range(4):
                        for k in range(KD):
                            ins = nc.tensor.matmul(ps[:, 0, bass.ds(i * 108 + (s * 4 + m) * 9, 9)],
                                                   wada[s][:, k, m * P:(m + 1) * P], cT[:, k, :],
                                                   start=(k == 0), stop=(k == KD - 1))
                    ins.then_inc(s_ada_used, 1)
            pe.wait_ge(s_ada_used, 12)
            pe.sem_inc(s_modps, 1)
            pe.wait_ge(s_mod, 1)
            def h_pe(rnd):
                with pe.Fori(0, NT // 2) as i:
                    for s in range(2):
                        pe.wait_ge(s_xn, 2 * i + ((NT + 1) * rnd + s + 1))
                        pe.wait_ge(s_xT_act, 2 * i + (NT * rnd + s + 1))
                        for k in range(KD):
                            ins = nc.tensor.transpose(ps[:, 2 * s + k // 4, (k % 4) * P:(k % 4 + 1) * P],
                                                      xn[:, s, k * P:(k + 1) * P], ident)
                        ins.then_inc(s_xT, 1)
                pe.wait_ge(s_xn, (NT + 1) * (rnd + 1))
                for k in range(KD):
                    ins = nc.tensor.transpose(ps[:, 4, k * NS:(k + 1) * NS], xn[0:NS, 0, k * P:(k + 1) * P],
                                              ident[0:NS, 0:NS])
                ins.then_inc(s_sT, 1)
                pe.wait_ge(s_xT_act, NT * rnd + NT + 2)
                pe.wait_ge(s_xT_dve, NT * rnd + NT + 2)
                pe.wait_ge(s_sh, rnd + 1)
            h_pe(0)
            with pe.Fori(0, MIX // PB // 2) as i:
                for s in range(2):
                    pe.wait_ge(s_wmix[s], i * 16 + 16)
                    for n in range(9):
                        pe.wait_ge(s_mix, i * 18 + (s * 9 + n + 1))
                        rows = P if n < NT else NS
                        for k in range(KD):
                            ins = nc.tensor.matmul(ps[0:rows, n % 4 if n < NT else 4, 0:PB],
                                                   hT[:, k, n * P:n * P + rows], wmix[s][:, k, :],
                                                   start=(k == 0), stop=(k == KD - 1))
                        ins.then_inc(s_mixps, 1)
                    pe.wait_ge(s_mixps, i * 18 + (s * 9 + 9))
                    pe.sem_inc(s_wmix_used, 1)
            pe.wait_ge(s_mix, 4 + 72)
            pe.wait_ge(s_gate, 2)
            nc.tensor.transpose(ps[0:32, 5, 0:P], gi[:, 0:32], ident)
            nc.tensor.transpose(ps[0:32, 5, P:2 * P], lf[:, 0:32], ident).then_inc(s_gRps, 1)
            pe.wait_ge(s_gR, 1)
            nc.tensor.transpose(ps[0:1, 5, 0:32], AR[:, P - 1:P], ident[0:32, 0:32])
            nc.tensor.transpose(ps[0:1, 5, 32:64], bR[:, P - 1:P], ident[0:32, 0:32]).then_inc(s_rowps, 1)
            pe.wait_ge(s_rowsb, 1)
            nc.tensor.transpose(ps[0:32, 6, 0:1], row[:, 3, :], ident[0:1, 0:1])
            nc.tensor.transpose(ps[0:32, 6, 1:2], row[:, 4, :], ident[0:1, 0:1]).then_inc(s_colps, 1)
            pe.wait_ge(s_gexp, 1)
            for j, r in enumerate((aR, eiR, emR, ainR)):
                nc.tensor.transpose(ps[:, 5, j * 32:(j + 1) * 32], r, ident[0:32, 0:32])
            nc.tensor.matmul(ps[:, 5, P:P + 32], ones[0:1, :], row[:, 5, :], start=True, stop=True).then_inc(s_tokps, 1)
            pe.wait_ge(s_tok, 1)
            pe.sem_inc(s_st, 1)
            with pe.Fori(0, NT) as c:
                pe.wait_ge(s_stage, 2 * c + 1)
                pe.wait_ge(s_C, c + 1)
                nc.tensor.matmul(ps[:, 3, :], ones[0:32, :], nmxM.rearrange("p h t -> p (h t)"), start=True, stop=True)\
                  .then_inc(s_zps, 1)
                for h in range(MH):
                    nc.tensor.transpose(ps[0:DQK, 0, h * P:(h + 1) * P], qk[:, h, :], ident)
                    nc.tensor.transpose(ps[0:DQK, 2, h * P:(h + 1) * P], qe[:, h, :], ident)
                    ins = nc.tensor.transpose(ps[0:DQK, 1, h * P:(h + 1) * P], qk[:, MH + h, :], ident)
                ins.then_inc(s_qkps, 1)
                pe.wait_ge(s_qTs, c + 1)
                pe.wait_ge(s_kTs, c + 1)
                for h in range(MH):
                    ins = nc.tensor.matmul(ps[:, 4, h * P:(h + 1) * P], kT[:, h, :], qT[:, h, :], start=True, stop=True)
                ins.then_inc(s_Sps, 1)
                pe.wait_ge(s_stage, 2 * c + 2)
                pe.wait_ge(s_w, c + 1)
                pe.wait_ge(s_h, c + 1)
                for h in range(MH):
                    out = ps[:, 5 + h // 2, (h % 2) * (DV + 1):(h % 2 + 1) * (DV + 1)]
                    nc.tensor.matmul(out, wgt[:, h, :], vone[:, h, :], start=True, stop=False)
                    nc.tensor.matmul(out, qeT[:, h, :], Cst[:, h, :], start=False, stop=True)
                for h in range(MH):
                    out = ps[0:DQK, 7 if h < 2 else 0, (h % 2) * (DV + 1):(h % 2 + 1) * (DV + 1)]
                    ins = nc.tensor.matmul(out, ke[:, h, :], vone[:, h, :], start=True, stop=True)
                ins.then_inc(s_st, 1)
            for c in range(NT):
                pe.wait_ge(s_y, c + 1)
                pe.wait_ge(s_C, NT + 1)
                if c >= 4:
                    pe.wait_ge(s_ya, c - 3)
                for h in range(MH):
                    ins = nc.tensor.transpose(ps[:, c % 4, h * P:(h + 1) * P], Pm[:, c, 512 + h * DV:512 + (h + 1) * DV], ident)
                ins.then_inc(s_yT, 1)
            pe.wait_ge(s_ya, NT)
            for j in range(4):
                lo = C_KV + (256, 512)[j // 2]
                for b in range(4):
                    ins = nc.tensor.transpose(ps[:, j, b * P:(b + 1) * P], Pm[:, (j % 2) * 4 + b, lo:lo + P], ident)
                ins.then_inc(s_kvps, 1)
            pe.wait_ge(s_cw, 1)
            pe.wait_ge(s_kvT, 4)
            for tile in range(NT):
                nc.tensor.matmul(ps[:, 0, 4 * tile:4 * tile + 4], kcw[:, tile, :], cst("block")[:, 28:32],
                                 start=True, stop=True)
            for tile in range(NT):
                ins = nc.tensor.matmul(ps[0:NCMP, 0, 64:64 + NKV * HD], cst("block")[:, 28 - 4 * tile:60 - 4 * tile],
                                       vcw[:, tile, :], start=(tile == 0), stop=(tile == NT - 1))
            ins.then_inc(s_cps, 1)
            pe.wait_ge(s_cT2, 2)
            pe.wait_ge(s_gts, 1)
            pe.sem_inc(s_qseen, 1)

            def att_S(u, g):
                kind, i, lo, blocks, _ = units[u]
                n = (i + 1 - lo) * P
                q = qTh[:, i * P:(i + 1) * P]
                kT_ = ksT if kind == "s" else kwT
                for c in range(0, n, 512):
                    w = min(512, n - c)
                    ins = nc.tensor.matmul(ps[:, 2 * (u % 2) + c // 512, 0:w], q, kT_[:, lo * P + c:lo * P + c + w],
                                           start=True, stop=True)
                if kind == "w":
                    ins = nc.tensor.matmul(ps[:, 2 * (u % 2) + 1, P:P + NCMP], q, kcT, start=True, stop=True)
                ins.then_inc(s_S, 1)

            for g in range(NKV):
                with pe.Fori(g * HPG, (g + 1) * HPG) as h:
                    pe.wait_ge(s_qst, h + 1)
                    for j in range(2):
                        pe.wait_ge(s_ev[j], h * (GA, GB)[j] + 1)
                        for b in range(4):
                            ins = nc.tensor.transpose(ps[:, 4 + j, b * P:(b + 1) * P], qst[:, 4 * j + b, :], ident)
                        ins.then_inc(s_pt[j], 1)
                    pe.wait_ge(s_ev[0], h * GA + 2)
                    pe.wait_ge(s_ev[1], h * GB + 2)
                    pe.sem_inc(s_qseen, 1)
                    att_S(0, g)
                    att_S(1, g)
                    cnt = [1, 1]
                    for u in range(NU):
                        kind, i, lo, blocks, gr = units[u]
                        pe.wait_ge(s_one, h * NU + (u + 1))
                        for q, grp in zip(groups[u], gr):
                            b = q % 2
                            pe.wait_ge(s_ev[b], h * (GA, GB)[b] + (cnt[b] + 1))
                            for o, (c, w, _) in enumerate(grp):
                                ins = nc.tensor.transpose(ps[0:w, 4 + b, o * P:(o + 1) * P], pbuf[u % 2][:, c:c + w], ident)
                            ins.then_inc(s_pt[b], 1)
                            cnt[b] += 1
                        if u + 2 < NU:
                            att_S(u + 2, g)
                        for b in range(2):
                            pe.wait_ge(s_ev[b], h * (GA, GB)[b] + (cnt[b] + 1))
                        if kind == "w":
                            pe.wait_ge(s_comb, h * NT + max(i, 1))
                        for o, (c, w, b) in enumerate(blocks):
                            src = ptbuf[u % 2][0:w, o * P:(o + 1) * P]
                            if b is None:
                                v = vc[:, g * HD:(g + 1) * HD]
                            else:
                                vlo = C_KV + (384 if kind == "s" else 640) + g * HD
                                v = Pm[:, b, vlo:vlo + HD]
                            ins = nc.tensor.matmul(ps[0:HD, 6 + i % 2, 0:P], v, src, start=(kind == "w" and o == 0),
                                                   stop=(kind == "s" and b == i))
                        ins.then_inc(s_pv, 1)
            pe.wait_ge(s_sWd, 1)
            pe.wait_ge(s_ybd, 16 * (NH + 1))
            nc.tensor.matmul(ps[0:32, 0, 0:DV + 2], cst("quarter"), sW, start=True, stop=True).then_inc(s_sWp, 1)
            for h in range(NH):
                nc.tensor.transpose(ps[0:HD, 1, h * NS:(h + 1) * NS], Ps[:, C_NQ + h * HD:C_NQ + (h + 1) * HD], ident[0:NS, 0:NS])
            for j in range(2):
                lo = C_KV + 256 * (j + 1)
                ins = nc.tensor.transpose(ps[:, 1, 64 + j * NS:64 + (j + 1) * NS], Ps[:, lo:lo + P], ident[0:NS, 0:NS])
            ins.then_inc(s_Qps, 1)
            pe.wait_ge(s_sh2, 2)
            nc.tensor.transpose(ps[:, 2, 0:32], hv, ident[0:32, 0:32]).then_inc(s_syT, 1)
            pe.wait_ge(s_Qall, 1)
            pe.wait_ge(s_sya, 1)
            pe.wait_ge(s_zero, 1)
            for j in range(2):
                nc.tensor.matmul(ps[0:SR, 3, j * NS:(j + 1) * NS], Qall.rearrange("p b h -> p (b h)"), knT[:, j, :],
                                 start=True, stop=True)
            for bank in range(3):
                nc.tensor.matmul(ps[0:SR, bank, :], ones[0:1, 0:SR], zrow, start=True, stop=False)
            nc.tensor.matmul(ps[0:SR, 3, 64:64 + NCMP], ones[0:1, 0:SR], zrow[:, 0:NCMP], start=True, stop=False)
            pe.sem_inc(s_free, 2)
            with pe.Fori(0, NS // 2) as i:
                for s in range(2):
                    pe.wait_ge(s_ldk[s], i * 272 + 272)
                    for j in range(NPAGE):
                        ins = nc.tensor.transpose(ps[:, 4 + j // 4, (j % 4) * P:(j % 4 + 1) * P], pg_slc[s][:, j, :], ident)
                    ins.then_inc(s_pgps, 1)
                    for j in range(WIN // P):
                        nc.tensor.transpose(ps[:, 6, j * P:(j + 1) * P], pg_win[s][:, j, :], ident)
                    pe.wait_ge(s_cmul, i * 2 + (s + 1))
                    for j in range(NPAGE):
                        nc.tensor.matmul(ps[:, 7, 4 * j:4 * j + 4], pg_cmp[s][:, j, 0:P], cst("block")[:, 28:32],
                                         start=True, stop=True)
                    for j in range(NPAGE):
                        ins = nc.tensor.matmul(ps[0:NCMP, 7, 64:64 + P], cst("block")[:, 28 - 4 * j:60 - 4 * j],
                                               pg_cmp[s][:, j, P:2 * P], start=(j == 0), stop=(j == NPAGE - 1))
                    ins.then_inc(s_pgps, 1)
                    pe.wait_ge(s_pga, i * 2 + (s + 1))
                    pe.wait_ge(s_pgd, i * 2 + (s + 1))
                    pe.wait_ge(s_qp, i * 2 + (s + 1))
                    Q2 = Qpad.rearrange("p b h -> p (b h)")
                    for j in range(2):
                        nc.tensor.matmul(ps[0:SR, j, :], Q2, pT[:, j * 512:(j + 1) * 512], start=False, stop=False)
                    nc.tensor.matmul(ps[0:SR, 2, :], Q2, wT, start=False, stop=False)
                    nc.tensor.matmul(ps[0:SR, 3, 64:64 + NCMP], Q2, ckT, start=False, stop=False).then_inc(s_free, 1)
            for bank in range(3):
                nc.tensor.matmul(ps[0:SR, bank, :], ones[0:1, 0:SR], zrow, start=False, stop=True)
            nc.tensor.matmul(ps[0:SR, 3, 64:64 + NCMP], ones[0:1, 0:SR], zrow[:, 0:NCMP], start=False, stop=True).then_inc(s_soft, 1)
            pe.wait_ge(s_soft, 2)
            nc.tensor.matmul(ps[0:SR, 7, 0:NCMP], cst("same_group", SR), pcm, start=True, stop=True).then_inc(s_impps, 1)
            pe.wait_ge(s_soft, 3)
            for j in range(NPAGE):
                nc.tensor.transpose(ps[:, 4, j * SR:(j + 1) * SR], Ssl[:, j * P:(j + 1) * P], ident[0:SR, 0:SR])
            for j in range(WIN // P):
                nc.tensor.transpose(ps[:, 5, j * SR:(j + 1) * SR], Swn[:, j * P:(j + 1) * P], ident[0:SR, 0:SR])
            nc.tensor.transpose(ps[0:NCMP, 5, 256:320], Scm, ident[0:SR, 0:SR])
            nc.tensor.transpose(ps[0:NS, 5, 320:384], Ssl[:, PAST:], ident[0:SR, 0:SR])
            nc.tensor.transpose(ps[0:NS, 5, 384:448], Swn[:, WIN:], ident[0:SR, 0:SR]).then_inc(s_sPT, 1)
            pe.wait_ge(s_sPTe, 2)
            O = ps[:, 6, 0:SR]
            nc.tensor.matmul(O, Ps[:, C_KV + 384:C_KV + 512], PTw[0:NS, 320:384], start=True, stop=False)
            nc.tensor.matmul(O, Ps[:, C_KV + 640:C_KV + 768], PTw[0:NS, 384:448], start=False, stop=False)
            for b in range(NS):
                nc.tensor.matmul(ps[:, 6, b * NH:(b + 1) * NH], vcs[:, b, :], PTw[0:NCMP, 256 + b * NH:256 + (b + 1) * NH],
                                 start=False, stop=False, skip_group_check=True)
            with pe.Fori(0, NS // 2) as i:
                for s in range(2):
                    pe.wait_ge(s_ldv[s], i * 144 + 144)
                    out = ps[:, 6, bass.ds(i * 16 + s * NH, NH)]
                    for j in range(NPAGE):
                        nc.tensor.matmul(out, pg_slc[s][:, j, :], PTs[:, 0, bass.ds(i * 16 + (j * SR + s * NH), NH)],
                                         start=False, stop=False, skip_group_check=True)
                    for j in range(WIN // P):
                        ins = nc.tensor.matmul(out, pg_win[s][:, j, :], PTw[:, bass.ds(i * 16 + (j * SR + s * NH), NH)],
                                               start=False, stop=False, skip_group_check=True)
                    ins.then_inc(s_free, 1)
            nc.tensor.matmul(O, ones[0:1, :], zrow[:, 0:SR], start=False, stop=True).then_inc(s_Osum, 1)
            pe.wait_ge(s_yb, 1)
            pe.wait_ge(s_Osum, 1)

            def chain(bank, w, k0, kn, src, q):
                for k in range(kn):
                    ins = nc.tensor.matmul(ps[:, bank, 0:TG], w[:, k0 + k, :], src[:, k, q * TG:(q + 1) * TG],
                                           start=(k == 0), stop=(k == kn - 1))
                return ins
            with pe.Fori(0, 2) as i:
                for s in range(2):
                    pe.wait_ge(s_wmg[s], i * 64 + 64)
                    for m in range(2):
                        for q in range(3):
                            u = (s * 2 + m) * 3 + q
                            pe.wait_ge(s_mgdve, i * 12 + (u + 1))
                            w = wmg[s][:, :, m * P:(m + 1) * P]
                            b = 4 * (u % 2)
                            chain(b, w, 0, 8, hT, q)
                            chain(b + 1, w, 8, 8, hT, q)
                            chain(b + 2, w, 16, 4, yaT, q)
                            ins = chain(b + 3, w, 20, 4, ybT, q)
                            ins.then_inc(s_mgps, 1)
                    pe.wait_ge(s_mgps, i * 12 + (s * 6 + 6))
                    pe.sem_inc(s_mgused, 1)
            pe.wait_ge(s_mgdve, 26)
            with pe.Fori(0, 2) as i:
                for s in range(2):
                    pe.wait_ge(s_wl[s], i * 16 + 16)
                    for u in range(6):
                        pe.wait_ge((s_woact, s_wodve)[u % 2], i * 6 + (s * 3 + u // 2 + 1))
                        chain(u, wot[s][:, :, (u // 3) * P:(u // 3 + 1) * P], 0, 8, merT, u % 3).then_inc(s_wops, 1)
                    pe.wait_ge(s_wops, i * 12 + (s * 6 + 6))
                    pe.sem_inc(s_woused, 1)

            def post_pe(rnd, gg, src):
                pe.wait_ge(s_diag, rnd + 1)
                for j in range(2):
                    nc.tensor.matmul(ps[:, 4 + j, :], ones[:, :], diag[rnd][:, j * 512:(j + 1) * 512], start=True, stop=True)
                for k in range(KD):
                    ins = nc.tensor.transpose(ps[0:NS, 6 + k // 4, (k % 4) * P:(k % 4 + 1) * P], gg[:, k, 1:9], ident)
                ins.then_inc(s_Gps, 1)
                for n in range(NT + 1):
                    r = P if n < NT else NS
                    if n >= 2:
                        pe.wait_ge(s_ytdve, (NT + 1) * rnd + n - 1)
                    for k in range(KD):
                        ins = nc.tensor.transpose(ps[0:r, 2 * (n % 2) + k // 4, (k % 4) * P:(k % 4 + 1) * P],
                                                  src[:, k, n * P:n * P + r], ident)
                    ins.then_inc(s_ytps, 1)
            pe.wait_ge(s_woact, 15)
            pe.wait_ge(s_wodve, 15)
            post_pe(0, gg1, yT1)
            pe.wait_ge(s_ytdve, NT + 1)
            h_pe(1)
            with pe.Fori(0, KF // 2) as i:
                for s in range(2):
                    pe.wait_ge(s_wl[s], i * 32 + (UP0 + 32))
                    for q in range(3):
                        u = s * 3 + q
                        pe.wait_ge(s_updve, i * 6 + (u + 1))
                        chain(2 * q, wup[s], 0, 8, hT, q)
                        chain(2 * q + 1, wup[s], 8, 8, hT, q).then_inc(s_upps, 1)
                    pe.wait_ge(s_upps, i * 6 + (s * 3 + 3))
                    pe.sem_inc(s_upused, 1)
            pe.wait_ge(s_updve, 3 * KF + 2)
            with pe.Fori(0, KD // 2) as i:
                for s in range(2):
                    pe.wait_ge(s_wl[s], i * 16 + (DN0 + 16))
                    for q in range(3):
                        u = s * 3 + q
                        pe.wait_ge((s_woact, s_wodve)[u % 2], i * 3 + (12 + u // 2 + 1))
                        chain(u, wdn[s], 0, KF, aT, q).then_inc(s_wops, 1)
                    pe.wait_ge(s_wops, i * 6 + (24 + s * 3 + 3))
                    pe.sem_inc(s_woused, 1)
            pe.wait_ge(s_woact, 27)
            pe.wait_ge(s_wodve, 27)
            post_pe(1, gg2, hT)


_INS = ["x_prompt", "x_sample", "c_prompt", "c_sample", "cache_cmp_kv", "cache_slc_kv", "cache_win_kv",
        "state_mlstm_C", "state_mlstm_n", "state_mlstm_m", "page_table", "g_pre_mix", "g_post_mix", "g_pre_ffn",
        "g_post_ffn", "w_ada", "b_ada", "w_in", "b_in", "mlstm_norm_w", "w_cmp_k", "w_cmp_v", "w_proj_a", "w_proj_b",
        "w_out", "w_up", "w_down"]
_KV = (2, NKV, HD)
_OUTS = [(1, SEQ, D), (NS, 1, D), (1, 1, SEQ) + _KV, (1, 1, SEQ) + _KV, (1, 1, WIN) + _KV,
         (1, 1, MH, DQK, DV), (1, 1, MH, DQK), (1, 1, MH),
         (1, NS, 1) + _KV, (1, NS, 1) + _KV, (1, NS, WIN) + _KV,
         (1, NS, MH, DQK, DV), (1, NS, MH, DQK), (1, NS, MH)]


def kernel(**inputs):
    import concourse.bacc as _bacc
    from concourse.bass_utils import run_bass_kernel_spmd as _run

    nc = _bacc.Bacc("TRN2", target_bir_lowering=False, num_devices=1)
    arrays, args = {}, {}
    for name in _INS + ["const"]:
        a = CONST if name == "const" else np.ascontiguousarray(inputs[name])
        arrays[f"in_{name}"] = a
        args[name] = nc.dram_tensor(f"in_{name}", a.shape, mybir.dt.from_np(a.dtype), kind="ExternalInput").ap()
    outs = [nc.dram_tensor(f"out_{i}", shape, F32, kind="ExternalOutput").ap() for i, shape in enumerate(_OUTS)]
    build(nc, args, outs)
    r = _run(nc, [arrays], core_ids=[0])
    return tuple(r.results[0][f"out_{i}"] for i in range(len(_OUTS)))
```

```python
from contextlib import ExitStack

import numpy as np
import concourse.bass as bass
from concourse import mybir

ALU = mybir.AluOpType
ACT = mybir.ActivationFunctionType
AX = mybir.AxisListType
F32 = mybir.dt.float32
FR = mybir.dt.float32r
I32 = mybir.dt.int32

P = 128
D = 1024
KD = D // P
SEQ = 1024
NT = SEQ // P
NS = 8
TOK = SEQ + NS
TG = TOK // 3
MH, DQK, DV = 4, 64, 128
NH, NKV, HD = 8, 2, 64
HPG = NH // NKV
CAP = 15.0
CMP, SEL, WIN = 32, 64, 512
PAST, PAGE = 1024, 128
NPAGE = PAST // PAGE
NCMP = SEQ // CMP
DFF = 2816
KF = DFF // P
EPS = 1e-6
NEG = -1e30

C_MQ, C_MK, C_MV, C_MO, C_MI, C_MF = 0, 256, 512, 1024, 1536, 1540
C_NQ, C_KV, C_NG, C_GA, C_GB, D_IN = 1544, 2056, 2824, 2848, 3872, 4896
MIX = C_GA
PB = 356
NPB = MIX // PB
ARENA = 38500


def constants():
    p = np.arange(P)
    parts = {}
    parts["ident"] = np.eye(P)
    parts["causal_st"] = np.where(p[:, None] <= p[None, :], 0.0, NEG)
    parts["causal_ts"] = np.where(p[None, :] <= p[:, None], 0.0, NEG)
    parts["window_ts"] = np.where(p[None, :] > p[:, None], 0.0, NEG)
    pos = (np.arange(NT)[None, :, None] * P + p[:, None, None])
    ends = (np.arange(NCMP) + 1)[None, None, :] * CMP - 1
    parts["cmp_add"] = np.where(ends <= pos, 0.0, NEG).reshape(P, NT * NCMP)
    parts["cmp_one"] = np.where(ends <= pos, 1.0, 0.0).reshape(P, NT * NCMP)
    parts["block"] = (np.arange(60)[None, :] - 28 == p[:, None] // CMP) * 1.0
    half = HD // 8
    inv = (np.float32(500000.0) ** (-np.arange(half, dtype=np.float32) * np.float32(2.0) / np.float32(HD // 4)))
    ang = (pos.astype(np.float32) * inv.astype(np.float32)[None, None, :]).astype(np.float32)
    parts["cos"] = np.cos(ang.astype(np.float64)).reshape(P, NT * half)
    parts["sin"] = np.sin(ang.astype(np.float64)).reshape(P, NT * half)
    sang = (np.float32(PAST) * inv).astype(np.float32).astype(np.float64)
    parts["scos"] = np.broadcast_to(np.cos(sang), (P, half))
    parts["ssin"] = np.broadcast_to(np.sin(sang), (P, half))
    r = np.arange(P)
    parts["own_new"] = np.where((r[:, None] // NH) == np.arange(NS)[None, :], 0.0, NEG)
    parts["same_group"] = ((r[:, None] // HPG) == (r[None, :] // HPG))[:, :64] * 1.0
    parts["blk"] = np.broadcast_to(np.arange(16.0), (P, 16))
    parts["quarter"] = ((r[:, None] // 4) == np.arange(32)[None, :]) * 1.0
    parts["onehot"] = np.broadcast_to(np.eye(NS).reshape(1, NS * NS), (P, NS * NS))
    at, n = {}, 0
    for k, v in parts.items():
        at[k] = (n, n + v.shape[1])
        n += v.shape[1]
    return np.concatenate([v.astype(np.float32) for v in parts.values()], axis=1), at


CONST, CAT = constants()


class Tally:

    def __init__(self, sem):
        self.sem, self.base, self.n, self.trip, self.per = sem, 0, 0, None, 0

    def loop(self, trip, per):
        self.base += self.n
        self.n, self.trip, self.per = 0, trip, per

    def end(self, trips):
        assert self.n == self.per, f"{self.sem.name}: per trip {self.n}, not {self.per}"
        self.base += trips * self.per
        self.n, self.trip, self.per = 0, None, 0

    def value(self, back=0):
        v = self.base + self.n - back
        return v if self.trip is None else self.trip * self.per + v


def build(nc, t, outs):
    (y_prompt, y_sample, cmp_prompt, slc_prompt, win_prompt, C_prompt, n_prompt, m_prompt,
     cmp_sample, slc_sample, win_sample, C_sample, n_sample, m_sample) = outs
    with ExitStack() as ctx:
        def sb(name, shape, dt=F32):
            return ctx.enter_context(nc.sbuf_tensor(name, shape, dt))

        def sem(name):
            return ctx.enter_context(nc.semaphore(name))

        ps = ctx.enter_context(nc.psum_tensor("ps", [P, 8, 512], F32))

        const = sb("const", [P, CONST.shape[1]])

        def cst(name, rows=P):
            return const[0:rows, CAT[name][0]:CAT[name][1]]

        ident = cst("ident")
        vecT = sb("vecT", [P, 96])
        modT = sb("modT", [P, 48, 9])
        sc1 = sb("sc1", [P, KD, 9])
        sc2 = sb("sc2", [P, KD, 9])
        gg1 = sb("gg1", [P, KD, 9])
        gg2 = sb("gg2", [P, KD, 9])
        ones = sb("ones", [P, P])
        mnormB = sb("mnormB", [P, MH * DV])
        ss = sb("ss", [P, 9])
        rstd = sb("rstd", [P, 9])
        cT = sb("cT", [P, KD, 9])
        place = {}
        for name, shape in (("xn", [P, 2, D]), ("hT", [P, KD, TOK]), ("arena", [P, ARENA])):
            place[name] = nc.sbuf_base
            place[name + "_"] = sb(name, shape)
        xn, hT, arena = (place[n] for n in ("xn_", "hT_", "arena_"))

        def fr(name, within, at, *shape):
            return nc.alloc_sbuf_tensor_at(name, [P, *shape], FR, offset=place[within] + 4 * at)

        def room(at, *shape, rows=P):
            n = int(np.prod(shape))
            assert at + n <= ARENA, (at, shape)
            v = arena[0:rows, at:at + n]
            if len(shape) == 2:
                v = v.rearrange("p (a b) -> p a b", a=shape[0])
            if len(shape) == 3:
                v = v.rearrange("p (a b c) -> p a b c", a=shape[0], b=shape[1])
            return v

        xin = room(0, NT, D)
        xs = room(NT * D, D, rows=NS)
        cin = room(NT * D + D, D, rows=9)
        vrows = room(NT * D + 2 * D, P, rows=96)
        wada = [room(NT * D + 2 * D + P + s * KD * 512, KD, 512) for s in range(3)]
        modrow = room(NT * D + 2 * D + P + 3 * KD * 512, 6 * D, rows=9)
        Pm = room(0, NT, MIX)
        Ps = room(NT * MIX, MIX, rows=NS)
        bmix = room(NT * MIX + MIX, MIX)
        wmix = [room(NT * MIX + 2 * MIX + s * KD * PB, KD, PB) for s in range(2)]

        at = NT * MIX + MIX
        yaT = room(at, MH, TOK)
        at += MH * TOK
        ybT = room(at, NH * HD // P, TOK)
        at_nsa = at + NH * HD // P * TOK

        def take(rows, *shape):
            nonlocal at
            v = room(at, *shape, rows=rows)
            at += int(np.prod(shape))
            return v
        gate = take(P, 9, 8)
        gi, lf, gtmp = take(P, 36), take(P, 36), take(P, 36)
        iR, fR, bR, aR, AR, nmxR, eiR, emR, ainR = (take(32, P) for _ in range(9))
        row = sb("row", [1, 6, 32])
        colR = take(32, 4)
        tok = take(P, 4, 32)
        astB = take(P, 32)
        nmxM = take(32, MH, P)
        qk, vone, qe, ke = ([take(P, *shape) for _ in range(2)]
                            for shape in ((2 * MH, DQK), (MH, DV + 1), (MH, DQK), (MH, DQK)))
        qT, qeT, kT = ([take(DQK, MH, P), xn[0:DQK, j // 2, (j % 2) * 512:(j % 2 + 1) * 512].rearrange("p (h t) -> p h t", h=MH)]
                       for j in range(3))
        wexp, wgt = take(P, MH, P), [take(P, MH, P) for _ in range(2)]
        Cst = sb("Cst", [DQK, MH, DV + 1])
        dn = take(P, MH)
        hn = take(P, 32)

        at = at_nsa
        ksT, kwT = take(P, SEQ), take(P, SEQ)
        kcT = take(P, NCMP)
        vc = take(NCMP, NKV * HD)
        gts = take(P, NT, 3 * NH)
        wck, wcv = take(P, HD), take(P, HD)
        qst = Pm[:, 5, 0:SEQ].rearrange("p (t c) -> p t c", c=P)
        ost = take(HD, SEQ)
        nmx = take(P, 3 * NT)
        rsum = take(P, NT, 3)
        gsc = take(P, NT, 3)
        pbuf = [Pm[:, u, 0:SEQ] for u in range(2)]
        ptbuf = [Pm[:, 2 + u, 0:SEQ] for u in range(2)]
        qTh = Pm[:, 4, 0:SEQ]
        kcw, vcw = (Pm[:, 6 + j, 0:SEQ].rearrange("p (t c) -> p t c", t=NT) for j in range(2))
        units = []
        for i in range(NT):
            for kind in "ws":
                lo = max(0, i - WIN // P) if kind == "w" else 0
                blocks = [((b - lo) * P, P, b) for b in range(lo, i + 1)]
                if kind == "w":
                    blocks.append((5 * P, NCMP, None))
                units.append((kind, i, lo, blocks, [blocks[j:j + 4] for j in range(0, len(blocks), 4)]))
        NU = len(units)
        groups, turns = [], []
        used = [0, 0]
        for u, (_, _, _, _, gr) in enumerate(units):
            if u == NU - 1:
                q_turn = list(used)
                used = [n + 1 for n in used]
            first = int(used[0] > used[1])
            mine = []
            for j in range(len(gr)):
                b = (first + j) % 2
                mine.append((b, used[b]))
                used[b] += 1
            groups.append(mine)
            turns.append(tuple(used))
        GN = tuple(used)

        at = 0
        CB, SB_, WB = NPAGE * 2 * NKV * HD, NPAGE * NKV * HD, WIN // P * NKV * HD
        slot_at = [at, at + CB + SB_ + WB]
        pg_cmp = [room(x, NPAGE, 2 * NKV * HD) for x in slot_at]
        pg_slc = [room(x + CB, NPAGE, NKV * HD) for x in slot_at]
        pg_win = [room(x + CB + SB_, WIN // P, NKV * HD) for x in slot_at]
        at = slot_at[1] + CB + SB_ + WB
        pT, wT = take(P, PAST), take(P, WIN)
        ckT = take(P, NCMP)
        vcs = take(NCMP, NS, NKV * HD)
        Qall, Qpad = take(P, NS, NH), take(P, NS, NH)
        knT = take(P, 2, NS)
        SR = NS * NH
        Ssl, Swn, Scm = take(SR, PAST + NS), take(SR, WIN + NS), take(SR, NCMP)
        pcm = take(SR, NCMP)
        imp, msk, small, sgt = take(SR, 16), take(SR, 16), take(SR, 16), take(SR, 3)
        zrow = take(1, 512)
        PTs = take(P, 1, 512)
        PTw = take(P, 512)
        DQ = DQK // 4
        sC, sT_ = take(P, DQ, DV), take(P, DQ, DV)
        sv = take(P, DV)
        sq, sk, sn = take(P, DQ), take(P, DQ), take(P, DQ)
        sW = take(P, DV + 2)
        hsum = take(P, 2, DQ)
        sg = take(P, 8)
        hv, hmo, hw = take(32, DV), take(32, DV), take(32, DV)
        hg = take(32, 10)
        hs = take(32, DV + 2)
        hsq = take(32, DV)
        assert at <= NT * MIX, at
        x1_dram = nc.dram_tensor("x1", [SEQ, D], F32, kind="Internal").ap()
        x1s_dram = nc.dram_tensor("x1_samples", [NS, D], F32, kind="Internal").ap()
        scr = {n: nc.dram_tensor(f"scratch_{n}", [NS, w], F32, kind="Internal").ap()
               for n, w in (("q", 256), ("k", 256), ("v", 512), ("o", 512), ("i", MH), ("f", MH), ("g", 3 * NH))}
        ptab = sb("ptab", [1, NS * NPAGE], I32)

        merT = room(0, KD, TOK)
        wmg = [room(8256 + s * 6144, 24, 256) for s in range(2)]
        wot = [room(20608 + s * 2048, KD, 256) for s in range(2)]
        yT1 = room(9216, KD, TOK)
        yt, yts = room(0, NT, D), room(NT * D, D, rows=NS)
        xres, xress = room(25632, NT, D), room(25632 + NT * D, D, rows=NS)
        G, Gs = room(34848, D), room(35872, D, rows=NS)
        sgm = [room(36896 + j * TG, TG) for j in range(4)]
        aT = room(0, KF, TOK)
        h_hi, h_lo = fr("h_hi", "hT", 0, KD, TOK), fr("h_lo", "arena", 22704, KD, TOK)
        wup = [room(30960, 2 * KD, P), room(33008, 2 * KD, P)]
        wup_lo = [fr("wup_lo0", "arena", 30960, 2 * KD, P), fr("wup_lo1", "arena", 33008, 2 * KD, P)]
        wup_hi = [fr("wup_hi0", "arena", 35056, 2 * KD, P), fr("wup_hi1", "xn", 0, 2 * KD, P)]
        sil = [room(37104, TG), room(37104 + TG, TG)]
        hraw = [room(35056 + s * D, KD, P) for s in range(2)]
        hraw_s = room(37104, KD, NS)
        wdn = [room(22704, KF, P), room(34848, KF, P)]
        G2, G2s = xn[:, 0, :], xn[0:NS, 1, :]
        bnow = room(38300, 8)

        def flat(x):
            return x[:, :, :].rearrange("p a b -> p (a b)")
        junk = room(9216 + KD * TOK + D, D)
        diag = [room(9216 + KD * TOK, D), room(9216, D)]

        s_const, s_c, s_vrow, s_x, s_bmix = (sem(n) for n in ("const", "c", "vrow", "x", "bmix"))
        s_ada = [sem(f"ada{s}") for s in range(3)]
        s_ada_used = sem("ada_used")
        s_cT, s_vT, s_cS = sem("cT_ps"), sem("vT_ps"), sem("cT_silu")
        s_modps, s_mod, s_ss, s_ms, s_sd = (
            sem(n) for n in ("mod_ps", "mod", "ss", "meansq", "std"))
        s_xn, s_xT, s_xT_act, s_xT_dve = (sem(n) for n in ("xn", "xT", "xT_act", "xT_dve"))
        s_sT, s_sh = sem("sampleT"), sem("sample_h")
        s_wmix = [sem(f"wmix{s}") for s in range(2)]
        s_wmix_used, s_mixps, s_mix = sem("wmix_used"), sem("mix_ps"), sem("mix")
        s_rope, s_rows = sem("rope"), sem("rows_out")
        s_gate, s_tanh, s_gabs, s_gln, s_gRps, s_gR, s_rowps, s_rowsb, s_colps, s_bR = (
            sem(n) for n in ("gate", "tanh", "gabs", "gln", "gR_ps", "gR", "row_ps", "row_sb", "col_ps", "bR"))
        s_gexp, s_tokps, s_tok = sem("gexp"), sem("tok_ps"), sem("tok")
        s_ones, s_stage, s_qkps, s_qTs, s_kTs, s_zps, s_arg, s_we, s_Sps, s_w, s_st, s_h, s_C = (
            sem(n) for n in ("ones", "stage", "qk_ps", "qT", "kT", "z_ps", "w_arg", "w_exp", "S_ps", "w", "state_ps", "h", "C"))
        s_kvps, s_kvT, s_wc, s_cw, s_cps, s_cT2, s_gts = (
            sem(n) for n in ("kv_ps", "kvT", "w_cmp", "cmp_weighted", "cmp_ps", "cmpT", "gates"))
        s_qst, s_qseen, s_S, s_max, s_exp, s_scaled, s_pv, s_comb = (
            sem(n) for n in ("q_staged", "q_seen", "att_S", "att_max", "att_exp", "att_scaled", "att_pv", "att_O_taken"))
        s_pt, s_ev = [sem("pt_A"), sem("pt_B")], [sem("ev_A"), sem("ev_B")]
        s_yb, s_ybd = sem("ybT_sample"), sem("ybT_rows")
        s_scr, s_scrg, s_smp, s_pt64, s_newwin = sem("scratch"), sem("scratch_gates"), sem("sample_in"), sem("page_table"), sem("new_win")
        s_ldk, s_ldv = [sem("pages_k0"), sem("pages_k1")], [sem("pages_v0"), sem("pages_v1")]
        s_free, s_cmul, s_pgps, s_pga, s_pgd, s_qp = (
            sem(n) for n in ("pages_used", "pages_weighted", "pages_T", "pages_act", "pages_dve", "q_padded"))
        s_Qps, s_Qall, s_zero, s_soft, s_softm, s_softe, s_impps, s_sPT, s_sPTe, s_Osum = (
            sem(n) for n in ("Q_ps", "Q_all", "zero", "soft", "soft_max", "soft_exp", "imp_ps", "sPT_ps", "sPT", "sample_O"))
        s_cg, s_cge, s_sWd, s_sWp, s_sh2, s_shd, s_sCn, s_syT, s_sya = (
            sem(n) for n in ("sm_gate", "sm_exp", "sm_W", "sm_W_ps", "sm_h", "sm_std", "sm_C", "sm_yT", "sm_ya"))
        s_wmg, s_wl = ([sem(f"{n}{j}") for j in range(2)] for n in ("wmerge", "wlate"))
        UP0, DN0 = 2 * 16, 2 * 16 + KF // 2 * 32
        s_mgps, s_mgact, s_mgdve, s_mgused, s_mgadd = sem("merge_ps"), sem("merge_sig"), sem("merge_dve"), sem("merge_used"), sem("merge_add")
        s_wops, s_woact, s_wodve, s_woused = sem("wout_ps"), sem("wout_act"), sem("wout_dve"), sem("wout_used")
        s_upps, s_upact, s_updve, s_upused = sem("up_ps"), sem("up_act"), sem("up_dve"), sem("up_used")
        s_out2, s_ss2 = sem("x1_ready"), sem("ss_x1")
        s_x1in, s_diag, s_Gps, s_ytps, s_ytsq, s_ytdve, s_out = (
            sem(n) for n in ("x_again", "diag", "G_ps", "yt_ps", "yt_sq", "yt_dve", "y_out"))
        s_mo, s_y, s_yT, s_ya, s_hsd = sem("mo_sig"), sem("y"), sem("yT_ps"), sem("yaT"), sem("h_std")
        s_dve, s_act, s_pool = sem("dve_steps"), sem("act_steps"), sem("pool_steps")

        block = ctx.enter_context(nc.Block())

        s_modrow = sem("mod_row")
        s_x1out, s_hsplit, s_whi, s_wlo = sem("x1_out"), sem("h_split"), sem("w_hi"), sem("w_lo")

        @block.sync
        def _(sp):
            sp.dma_start(ptab[:, :], t["page_table"].rearrange("b j -> (b j)").unsqueeze(0)).then_inc(s_pt64, 16)
            sp.dma_start(const[:, :], t["const"]).then_inc(s_const, 16)
            sp.dma_start(mnormB[:, :], t["mlstm_norm_w"].partition_broadcast(P)).then_inc(s_const, 16)
            sp.dma_start(cin[0:1, :], t["c_prompt"]).then_inc(s_c, 16)
            sp.dma_start(cin[1:9, :], t["c_sample"]).then_inc(s_c, 16)
            line = 0
            for name, lo, n in (("b_ada", 0, 48), ("b_in", C_GA, 16), ("g_pre_mix", 0, 8), ("g_pre_ffn", 0, 8),
                                ("g_post_mix", 0, 8), ("g_post_ffn", 0, 8)):
                sp.dma_start(vrows[line:line + n, :], t[name][0, lo:lo + n * P].rearrange("(r f) -> r f", f=P))\
                  .then_inc(s_vrow, 16)
                line += n
            w_ada = t["w_ada"][0].rearrange("(k p) n -> p k n", p=P)
            for s in range(3):
                sp.dma_start(wada[s], w_ada[:, :, s * 512:(s + 1) * 512]).then_inc(s_ada[s], 16)
            with sp.Fori(1, 4) as i:
                for s in range(3):
                    sp.wait_ge(s_ada_used, i * 3 + (s - 2))
                    sp.dma_start(wada[s], w_ada[:, :, bass.ds(i * 1536 + s * 512, 512)]).then_inc(s_ada[s], 16)
            w_in = t["w_in"][0].rearrange("(k p) n -> p k n", p=P)
            sp.wait_ge(s_modps, 1)
            sp.wait_ge(s_sh, 1)
            sp.wait_ge(s_xn, 8)
            sp.dma_start(bmix, t["b_in"][:, 0:MIX].partition_broadcast(P)).then_inc(s_bmix, 16)
            for s in range(2):
                sp.dma_start(wmix[s], w_in[:, :, s * PB:(s + 1) * PB]).then_inc(s_wmix[s], 16)
            with sp.Fori(1, MIX // PB // 2) as i:
                for s in range(2):
                    sp.wait_ge(s_wmix_used, i * 2 + (s - 1))
                    sp.dma_start(wmix[s], w_in[:, :, bass.ds(i * 2 * PB + s * PB, PB)]).then_inc(s_wmix[s], 16)
            sp.wait_ge(s_rope, 1)
            for n, lo, w in (("q", C_MQ, 256), ("k", C_MK, 256), ("v", C_MV, 512), ("o", C_MO, 512), ("g", C_NG, 24)):
                sp.dma_start(scr[n], Ps[:, lo:lo + w]).then_inc(s_scr, 16)
            sp.wait_ge(s_gate, 2)
            sp.dma_start(scr["i"], gi[0:NS, 32:36]).then_inc(s_scrg, 16)
            sp.dma_start(scr["f"], lf[0:NS, 32:36]).then_inc(s_scrg, 16)
            sp.dma_start(win_sample[0, :, 0:WIN - 1].rearrange("b r a g d -> b (r a g d)"),
                         t["cache_win_kv"][0, :, 1:WIN].rearrange("b r a g d -> b (r a g d)")).then_inc(s_newwin, 16)
            sp.wait_ge(s_ya, NT)
            for r in range(4):
                sp.dma_start(wck[r * CMP:(r + 1) * CMP, :], t["w_cmp_k"][0]).then_inc(s_wc, 16)
                sp.dma_start(wcv[r * CMP:(r + 1) * CMP, :], t["w_cmp_v"][0]).then_inc(s_wc, 16)
            with sp.Fori(0, NH // 2) as j:
                for odd in range(2):
                    sp.wait_ge(s_comb, j * 2 * NT + (odd * NT + NT + 1))
                    sp.dma_start(ybT[odd * HD:(odd + 1) * HD, bass.ds(j, 1), 0:SEQ], ost.unsqueeze(1)).then_inc(s_ybd, 16)
            sp.wait_ge(s_rope, 1)

            def rows(dst, src, slow=False):
                sp.dma_start(dst, src, allow_slow_non_contiguous=slow).then_inc(s_rows, 16)
            rows(cmp_prompt[0, 0].rearrange("(t p) a g d -> p t (a g d)", p=P), Pm[:, :, C_KV:C_KV + 256])
            rows(slc_prompt[0, 0].rearrange("(t p) a g d -> p t (a g d)", p=P), Pm[:, :, C_KV + 256:C_KV + 512])
            rows(win_prompt[0, 0].rearrange("(t p) a g d -> p t (a g d)", p=P), Pm[:, NT - WIN // P:, C_KV + 512:C_KV + 768])
            rows(cmp_sample[0, :, 0].rearrange("b a g d -> b (a g d)"), Ps[:, C_KV:C_KV + 256])
            rows(slc_sample[0, :, 0].rearrange("b a g d -> b (a g d)"), Ps[:, C_KV + 256:C_KV + 512])
            sp.wait_ge(s_C, NT + 1)
            rows(C_prompt[0, 0].rearrange("h d v -> d h v"), Cst[:, :, 0:DV])
            rows(n_prompt[0, 0].rearrange("h d -> d h").unsqueeze(2), Cst[:, :, DV:DV + 1], True)
            rows(m_prompt[0], row[:, 2, 32 - MH:32])
            rows(win_sample[0, :, WIN - 1].rearrange("b a g d -> b (a g d)"), Ps[:, C_KV + 512:C_KV + 768])
            sp.wait_ge(s_scr, 80)
            sp.wait_ge(s_scrg, 32)
            sp.wait_ge(s_ybd, 16 * (NH + 1))

            def give(dst, src, slow=False):
                sp.dma_start(dst, src, allow_slow_non_contiguous=slow).then_inc(s_smp, 16)

            def flat_rows(x, w):
                names = "abcdef"[:len(x.shape)]
                return x.rearrange(f"{' '.join(names)} -> ({' '.join(names)})").rearrange("(r w) -> r w", w=w)
            sC2 = sC.rearrange("p a b -> p (a b)")
            give(sC2, flat_rows(t["state_mlstm_C"], DQ * DV))
            give(sn, flat_rows(t["state_mlstm_n"], DQ))
            give(sq, flat_rows(scr["q"], DQ))
            give(sk, flat_rows(scr["k"], DQ))
            for j in range(4):
                give(sv[j::4, :], flat_rows(scr["v"], DV))
                give(sg[j::4, 0:1], flat_rows(scr["i"], 1))
                give(sg[j::4, 1:2], flat_rows(scr["f"], 1))
                give(sg[j::4, 2:3], flat_rows(t["state_mlstm_m"], 1))
            give(hv, flat_rows(scr["v"], DV))
            give(hmo, flat_rows(scr["o"], DV))
            give(hg[:, 0:1], flat_rows(scr["i"], 1))
            give(hg[:, 1:2], flat_rows(scr["f"], 1))
            give(hg[:, 2:3], flat_rows(t["state_mlstm_m"], 1))
            for b in range(NS):
                give(hw[b * MH:(b + 1) * MH, :], flat_rows(t["mlstm_norm_w"], DV))
            give(sgt, flat_rows(scr["g"], 3))
            sp.wait_ge(s_pt64, 16)

            def win_rows(b, a):
                return t["cache_win_kv"][0, bass.ds(b, 1), :, a].rearrange("o (q p) g d -> p (o q) (g d)", p=P)

            def load_keys(b, s):
                for j in range(NPAGE):
                    page = sp.value_load(ptab[0:1, bass.ds(b * NPAGE + j, 1)], min_val=0,
                                         max_val=t["cache_cmp_kv"].shape[1] - 1)
                    sp.dma_start(pg_cmp[s][:, j:j + 1, :],
                                 t["cache_cmp_kv"][0, bass.ds(page, 1)].rearrange("o p a g d -> p o (a g d)")).then_inc(s_ldk[s], 16)
                    sp.dma_start(pg_slc[s][:, j:j + 1, :],
                                 t["cache_slc_kv"][0, bass.ds(page, 1), :, 0].rearrange("o p g d -> p o (g d)")).then_inc(s_ldk[s], 16)
                sp.dma_start(pg_win[s], win_rows(b, 0)).then_inc(s_ldk[s], 16)

            def load_values(b, s):
                for j in range(NPAGE):
                    page = sp.value_load(ptab[0:1, bass.ds(b * NPAGE + j, 1)], min_val=0,
                                         max_val=t["cache_slc_kv"].shape[1] - 1)
                    sp.dma_start(pg_slc[s][:, j:j + 1, :],
                                 t["cache_slc_kv"][0, bass.ds(page, 1), :, 1].rearrange("o p g d -> p o (g d)")).then_inc(s_ldv[s], 16)
                sp.dma_start(pg_win[s], win_rows(b, 1)).then_inc(s_ldv[s], 16)
            with sp.Fori(0, NS // 2) as i:
                for s in range(2):
                    sp.wait_ge(s_free, i * 2 + (s + 1))
                    load_keys(i * 2 + s, s)
            with sp.Fori(0, NS // 2) as i:
                for s in range(2):
                    sp.wait_ge(s_free, i * 2 + (NS + s + 1))
                    load_values(i * 2 + s, s)
            sp.wait_ge(s_sCn, 1)
            rows(flat_rows(C_sample, DQ * DV), sC2)
            rows(flat_rows(n_sample, DQ), sn)
            rows(flat_rows(m_sample, 1), hg[:, 3:4])
            sp.wait_ge(s_newwin, 16)
            sp.wait_ge(s_rows, 16 * 12)

            sp.wait_ge(s_yb, 1)
            wpa = t["w_proj_a"][0].rearrange("(k p) n -> p k n", p=P)
            wpb = t["w_proj_b"][0].rearrange("(k p) n -> p k n", p=P)
            w_out = t["w_out"][0].rearrange("(k p) n -> p k n", p=P)
            w_up = t["w_up"][0].rearrange("(k p) n -> p k n", p=P)
            w_down = t["w_down"][0].rearrange("(k p) n -> p k n", p=P)

            def load_merge(col, s):
                sp.dma_start(wmg[s][:, 0:8, :], w_in[:, :, bass.ds(col + C_GA, 256)]).then_inc(s_wmg[s], 16)
                sp.dma_start(wmg[s][:, 8:16, :], w_in[:, :, bass.ds(col + C_GB, 256)]).then_inc(s_wmg[s], 16)
                sp.dma_start(wmg[s][:, 16:20, :], wpa[:, :, bass.ds(col, 256)]).then_inc(s_wmg[s], 16)
                sp.dma_start(wmg[s][:, 20:24, :], wpb[:, :, bass.ds(col, 256)]).then_inc(s_wmg[s], 16)
            for s in range(2):
                load_merge(s * 256, s)
            for s in range(2):
                sp.dma_start(wot[s], w_out[:, :, s * 256:(s + 1) * 256]).then_inc(s_wl[s], 16)
            for s in range(2):
                sp.wait_ge(s_mgused, s + 1)
                load_merge(512 + s * 256, s)
            sp.wait_ge(s_mgused, 4)
            sp.dma_start(xres, t["x_prompt"][0].rearrange("(t p) d -> p t d", p=P)).then_inc(s_x1in, 16)
            sp.dma_start(xress, t["x_sample"][:, 0, :]).then_inc(s_x1in, 16)
            for s in range(2):
                sp.wait_ge(s_woused, s + 1)
                sp.dma_start(wot[s], w_out[:, :, 512 + s * 256:768 + s * 256]).then_inc(s_wl[s], 16)

            def load_up(col, s):
                sp.dma_start(wup[s][:, 0:8, :], w_up[:, :, bass.ds(col, P)]).then_inc(s_wl[s], 16)
                sp.dma_start(wup[s][:, 8:16, :], w_up[:, :, bass.ds(col + DFF, P)]).then_inc(s_wl[s], 16)
            for n in range(NT):
                sp.wait_ge(s_out2, n + 1)
                sp.dma_start(x1_dram[n * P:(n + 1) * P, :], yt[:, n, :]).then_inc(s_x1out, 16)
            sp.wait_ge(s_out2, NT + 1)
            sp.dma_start(x1s_dram, yts).then_inc(s_x1out, 16)
            load_up(0, 0)
            load_up(P, 1)
            with sp.Fori(1, KF // 2) as i:
                for s in range(2):
                    sp.wait_ge(s_upused, i * 2 + (s - 1))
                    load_up(i * 2 * P + s * P, s)
            sp.wait_ge(s_upused, KF)
            sp.wait_ge(s_updve, 3 * KF + 2)
            for s in range(2):
                sp.dma_start(wdn[s], w_down[:, :, s * P:(s + 1) * P]).then_inc(s_wl[s], 16)
            sp.wait_ge(s_x1out, 16 * (NT + 1))
            sp.dma_start(xres, x1_dram.rearrange("(t p) d -> p t d", p=P)).then_inc(s_x1in, 16)
            sp.dma_start(xress, x1s_dram).then_inc(s_x1in, 16)
            with sp.Fori(1, KD // 2) as i:
                for s in range(2):
                    sp.wait_ge(s_woused, i * 2 + (4 + s - 1))
                    sp.dma_start(wdn[s], w_down[:, :, bass.ds(i * 2 * P + s * P, P)]).then_inc(s_wl[s], 16)
            for n in range(NT):
                sp.wait_ge(s_out, n + 1)
                sp.dma_start(y_prompt[0, n * P:(n + 1) * P, :], xres[:, n, :]).then_inc(s_rows, 16)
            sp.wait_ge(s_out, NT + 1)
            sp.dma_start(y_sample[:, 0, :], xress).then_inc(s_rows, 16)
            sp.wait_ge(s_rows, 16 * 21)

        @block.gpsimd
        def _(pool):
            nc.gpsimd.memset(ones[:, :], 1.0).then_inc(s_ones, 1)
            pool.wait_ge(s_ones, 1)
            pool.wait_ge(s_mix, 4 + 72)
            for s in range(2):
                ins = nc.gpsimd.memset(vone[s], 1.0)
            ins.then_inc(s_ones, 1)
            pool.wait_ge(s_ones, 2)
            pool.wait_ge(s_tok, 1)
            with pool.Fori(0, NT // 2) as i:
                for s in range(2):
                    pm = Pm[:, bass.ds(i * 2 + s, 1), :]
                    q3 = pm[:, :, 0:256].rearrange("p a (h d) -> p (a h) d", d=DQK)
                    k3 = pm[:, :, 256:512].rearrange("p a (h d) -> p (a h) d", d=DQK)

                    def per_head(j):
                        return tok[:, j, bass.ds(i * 2 * MH + s * MH, MH)].unsqueeze(2).to_broadcast([P, MH, DQK])
                    pool.wait_ge(s_zps, i * 2 + (s + 1))
                    nc.gpsimd.tensor_copy(qk[s], pm[:, :, 0:512].rearrange("p a (h d) -> p (a h) d", d=DQK))
                    nc.gpsimd.tensor_tensor(qe[s], q3, per_head(1), ALU.mult)
                    nc.gpsimd.tensor_tensor(nmxM, nmxR.unsqueeze(1).to_broadcast([32, MH, P]),
                                            ident[0:32, bass.ds(i * 2 * MH + s * MH, MH)].unsqueeze(2).to_broadcast([32, MH, P]),
                                            ALU.mult).then_inc(s_stage, 1)
                    pool.wait_ge(s_st, i * 2 + (s + 1))
                    nc.gpsimd.tensor_tensor(ke[s], k3, per_head(3), ALU.mult)
                    nc.gpsimd.tensor_copy(vone[s][:, :, 0:DV], pm[:, :, 512:1024].rearrange("p a (h v) -> p (a h) v", v=DV))\
                      .then_inc(s_stage, 1)

            pool.wait_ge(s_wc, 128)
            for src, w, lo in ((kcw, wck, C_KV), (vcw, wcv, C_KV + 128)):
                for g in range(NKV):
                    ins = nc.gpsimd.tensor_tensor(src[:, :, g * HD:(g + 1) * HD], Pm[:, :, lo + g * HD:lo + (g + 1) * HD],
                                                  w.unsqueeze(1).to_broadcast([P, NT, HD]), ALU.mult)
            ins.then_inc(s_cw, 1)
            for g in range(NKV):
                pool.wait_ge(s_qseen, g * HPG + 1)
                nc.gpsimd.memset(qst, 0.0).then_inc(s_pool, 1)
                pool.wait_ge(s_pool, g + 1)
                with pool.Fori(g * HPG, (g + 1) * HPG + g) as h:
                    pool.wait_ge(s_qseen, h + 1)
                    nc.gpsimd.tensor_copy(qst[:, :, g * HD:(g + 1) * HD], Pm[:, :, bass.ds(h * HD + C_NQ, HD)]).then_inc(s_qst, 1)

            with pool.Fori(0, NS // 2) as i:
                for s in range(2):
                    pool.wait_ge(s_ldk[s], i * 272 + 272)
                    for a, w in ((0, wck), (1, wcv)):
                        v = pg_cmp[s][:, :, a * NKV * HD:(a + 1) * NKV * HD].rearrange("p j (g d) -> p j g d", g=NKV)
                        ins = nc.gpsimd.tensor_tensor(v, v, w.unsqueeze(1).unsqueeze(1).to_broadcast([P, NPAGE, NKV, HD]), ALU.mult)
                    ins.then_inc(s_cmul, 1)

            pool.sem_inc(s_hsplit, 2)
            with pool.Fori(0, NT // 2) as i:
                for s in range(2):
                    pool.wait_ge(s_xT_act, 2 * i + (NT + 2 + s + 1))
                    pool.wait_ge(s_xT_dve, 2 * i + (NT + 2 + s + 1))
                    cols = bass.ds(i * 256 + s * P, P)
                    nc.gpsimd.tensor_copy(h_hi[:, :, cols], hraw[s]).then_inc(s_pool, 1)
                    pool.wait_ge(s_pool, 2 * i + (NKV + s + 1))
                    nc.gpsimd.tensor_tensor(h_lo[:, :, cols], hraw[s], h_hi[:, :, cols], ALU.subtract).then_inc(s_hsplit, 1)
            pool.wait_ge(s_sh, 2)
            nc.gpsimd.tensor_copy(h_hi[:, :, SEQ:TOK], hraw_s).then_inc(s_pool, 1)
            pool.wait_ge(s_pool, NKV + NT + 1)
            nc.gpsimd.tensor_tensor(h_lo[:, :, SEQ:TOK], hraw_s, h_hi[:, :, SEQ:TOK], ALU.subtract).then_inc(s_hsplit, 1)

        @block.scalar
        def _(act):
            act.dma_start(xin, t["x_prompt"][0].rearrange("(t p) d -> p t d", p=P)).then_inc(s_x, 16)
            act.dma_start(xs, t["x_sample"][:, 0, :]).then_inc(s_x, 16)
            act.sem_inc(s_xT_act, 2)
            act.wait_ge(s_cT, 1)
            nc.scalar.activation(cT[:, :, :], ps[:, 7, 0:72].rearrange("p (k c) -> p k c", c=9), ACT.Silu).then_inc(s_cS, 1)
            act.wait_ge(s_x, 32)
            act.wait_ge(s_ss, 1)
            with act.Fori(0, NT) as i:
                nc.scalar.activation(hT[:, 0, 0:D], xin[:, bass.ds(i, 1), :].rearrange("p a b -> p (a b)"), ACT.Square,
                                     accum_out=ss[:, bass.ds(i, 1)]).then_inc(s_ss, 1)
                act.wait_ge(s_ss, i + 2)
            nc.scalar.activation(hT[0:NS, 0, 0:D], xs, ACT.Square, accum_out=ss[0:NS, 8:9]).then_inc(s_ss, 1)
            act.wait_ge(s_ms, 1)
            nc.scalar.activation(rstd[:, :], rstd[:, :], ACT.Sqrt).then_inc(s_sd, 1)
            act.wait_ge(s_mod, 1)

            def h_act(rnd):
                sc, sh = (sc1, sc2)[rnd], 24 * rnd
                with act.Fori(0, NT // 2) as i:
                    for s in range(2):
                        act.wait_ge(s_xT, 2 * i + (NT * rnd + s + 1))
                        if rnd:
                            act.wait_ge(s_hsplit, 2 * i + (s + 1))
                        for k in range(KD // 2):
                            ins = nc.scalar.activation(hraw[s][:, k, :] if rnd else hT[:, k, bass.ds(i * 256 + s * P, P)],
                                                       ps[:, 2 * s + k // 4, (k % 4) * P:(k % 4 + 1) * P], ACT.Identity,
                                                       scale=sc[:, k, 0:1], bias=modT[:, sh + k, 0:1])
                        ins.then_inc(s_xT_act, 1)
            h_act(0)

            act.wait_ge(s_gate, 1)
            nc.scalar.activation(gate, gate, ACT.Tanh, scale=1.0 / CAP).then_inc(s_tanh, 1)
            act.wait_ge(s_gabs, 1)
            nc.scalar.activation(gtmp, gtmp, ACT.Exp, scale=-1.0).then_inc(s_gln, 1)
            act.wait_ge(s_gln, 1)
            nc.scalar.activation(gtmp, gtmp, ACT.Ln, bias=1.0).then_inc(s_gln, 1)
            act.wait_ge(s_bR, 1)
            nc.scalar.activation(eiR, nmxR, ACT.Exp, bias=colR[:, 0:1])
            nc.scalar.activation(emR, emR, ACT.Exp, scale=-1.0)
            nc.scalar.activation(ainR, aR, ACT.Exp, bias=colR[:, 2:3])
            nc.scalar.activation(row[:, 5, :], row[:, 5, :], ACT.Exp).then_inc(s_gexp, 1)
            with act.Fori(0, NT // 2) as i:
                for s in range(2):
                    act.wait_ge(s_qkps, i * 2 + (s + 1))
                    act.wait_ge(s_st, i * 2 + (s + 1))
                    nc.scalar.activation(qT[s], ps[0:DQK, 0, :].rearrange("p (h t) -> p h t", h=MH), ACT.Copy, scale=DQK ** -0.5)
                    nc.scalar.activation(qeT[s], ps[0:DQK, 2, :].rearrange("p (h t) -> p h t", h=MH), ACT.Copy, scale=DQK ** -0.5)\
                      .then_inc(s_qTs, 1)
                    act.wait_ge(s_arg, i * 2 + (s + 2))
                    nc.scalar.activation(wexp, wexp, ACT.Exp).then_inc(s_we, 1)
            for c in range(NT):
                ins = nc.scalar.activation(Pm[:, c, C_MO:C_MO + 512], Pm[:, c, C_MO:C_MO + 512], ACT.Sigmoid)
            ins.then_inc(s_mo, 1)
            act.wait_ge(s_h, NT + 2)
            nc.scalar.activation(hn, hn, ACT.Sqrt).then_inc(s_hsd, 1)

            act.wait_ge(s_ya, NT)
            nc.scalar.activation(gts, Pm[:, :, C_NG:C_NG + 24], ACT.Sigmoid).then_inc(s_gts, 1)
            for j in range(1, 4, 2):
                act.wait_ge(s_kvps, j + 1)
                nc.scalar.activation((ksT, kwT)[j // 2][:, 512:1024], ps[:, j, :], ACT.Copy).then_inc(s_kvT, 1)
            act.sem_inc(s_ev[1], 1)
            act.sem_inc(s_comb, 1)
            act.sem_inc(s_ybd, 16)

            def att_exp(u, h):
                kind, i, lo, blocks, _ = units[u]
                act.wait_ge(s_max, h * NU + (u + 1))
                for b in range(2):
                    n = turns[u - 2][b] if u >= 2 else 0
                    act.wait_ge(s_pt[b], h * GN[b] + (n + 1))
                span = ps[:, 2 * (u % 2):2 * (u % 2) + 2, :].rearrange("p b c -> p (b c)")
                n = (i + 1 - lo) * P
                j = 1 if kind == "s" else 2
                ins = nc.scalar.activation(pbuf[u % 2][:, 0:n], span[:, 0:n], ACT.Exp, bias=nmx[:, 3 * i + j:3 * i + j + 1],
                                           accum_out=rsum[:, i, j:j + 1])
                if kind == "w":
                    ins = nc.scalar.activation(pbuf[u % 2][:, 5 * P:5 * P + NCMP], span[:, 5 * P:5 * P + NCMP], ACT.Exp,
                                               bias=nmx[:, 3 * i:3 * i + 1], accum_out=rsum[:, i, 0:1])
                ins.then_inc(s_exp, 1)

            def att_out(i, h):
                act.wait_ge(s_pv, h * NU + (2 * i + 2))
                if i == 0:
                    act.wait_ge(s_ybd, h * 16 + 16)
                nc.scalar.activation(ost[:, i * P:(i + 1) * P], ps[0:HD, 6 + i % 2, 0:P], ACT.Copy).then_inc(s_comb, 1)

            act.wait_ge(s_pt[1], 1)
            nc.scalar.activation(qTh[:, 512:1024], ps[:, 5, :], ACT.Copy, scale=HD ** -0.5).then_inc(s_ev[1], 1)
            with act.Fori(0, NH) as h:
                att_exp(0, h)
                att_exp(1, h)
                for u in range(NU):
                    for j, ((b, turn), g) in enumerate(zip(groups[u], units[u][4])):
                        if b == 1:
                            act.wait_ge(s_pt[1], h * GN[1] + (turn + 2))
                            if u >= 2:
                                act.wait_ge(s_pv, h * NU + (u - 1))
                            full = sum(1 for c, w, _ in g if w == P)
                            if full:
                                ins = nc.scalar.activation(ptbuf[u % 2][:, j * 512:j * 512 + full * P], ps[:, 5, 0:full * P], ACT.Copy)
                            if full < len(g):
                                ins = nc.scalar.activation(ptbuf[u % 2][0:NCMP, j * 512 + full * P:j * 512 + (full + 1) * P],
                                                           ps[0:NCMP, 5, full * P:(full + 1) * P], ACT.Copy)
                            ins.then_inc(s_ev[1], 1)
                    if u + 2 < NU:
                        att_exp(u + 2, h)
                    if u == NU - 2:
                        act.wait_ge(s_pt[1], h * GN[1] + (q_turn[1] + 2))
                        nc.scalar.activation(qTh[:, 512:1024], ps[:, 5, :], ACT.Copy, scale=HD ** -0.5).then_inc(s_ev[1], 1)
                    if u % 2 == 0 and u:
                        att_out(u // 2 - 1, h)
                att_out(NT - 1, h)

            act.wait_ge(s_cg, 1)
            for x in (sg, hg):
                nc.scalar.activation(x[:, 4:7], x[:, 4:7], ACT.Exp)
            act.wait_ge(s_smp, 16 * 34)
            nc.scalar.activation(hg[:, 7:8], hg[:, 7:8], ACT.Exp, scale=-1.0).then_inc(s_cge, 1)
            act.wait_ge(s_sh2, 1)
            nc.scalar.activation(hg[:, 9:10], hg[:, 9:10], ACT.Sqrt).then_inc(s_shd, 1)
            nc.scalar.activation(hmo, hmo, ACT.Sigmoid)
            nc.scalar.activation(sgt, sgt, ACT.Sigmoid).then_inc(s_shd, 1)
            with act.Fori(0, NS) as b:
                act.wait_ge(s_pgps, 2 * b + 1)
                nc.scalar.activation(pT[:, 0:512], ps[:, 4, :], ACT.Copy)
                act.wait_ge(s_pgps, 2 * b + 2)
                nc.scalar.activation(wT, ps[:, 6, :], ACT.Copy).then_inc(s_pga, 1)
            for n, x, j in ((1, Scm, 0), (2, Swn, 2), (3, Ssl, 1)):
                act.wait_ge(s_softm, n)
                nc.scalar.activation(x, x, ACT.Exp, bias=small[:, j:j + 1], accum_out=small[:, 4 + j:5 + j]).then_inc(s_softe, 1)
            act.wait_ge(s_sPT, 1)
            nc.scalar.activation(PTs[:, 0, :], ps[:, 4, :], ACT.Copy).then_inc(s_sPTe, 1)

            with act.Fori(0, 2) as i:
                for j in range(2):
                    ins = nc.scalar.activation(bnow[:, 4 * j:4 * j + 4], vecT[:, bass.ds(i * 4 + (48 + 8 * j), 4)], ACT.Copy)
                ins.then_inc(s_act, 1)
                act.wait_ge(s_act, i + 1)
                for s in range(2):
                    for m in range(2):
                        for q in range(3):
                            u = (s * 2 + m) * 3 + q
                            act.wait_ge(s_mgps, i * 12 + (u + 1))
                            act.wait_ge(s_mgdve, i * 12 + (u + 1))
                            for j in range(2):
                                ins = nc.scalar.activation(sgm[2 * (u % 2) + j], ps[:, 4 * (u % 2) + j, 0:TG], ACT.Sigmoid,
                                                           bias=bnow[:, 4 * j + 2 * s + m:4 * j + 2 * s + m + 1])
                            ins.then_inc(s_mgact, 1)
                act.wait_ge(s_mgact, i * 12 + 12)

            act.sem_inc(s_woact, 3)
            with act.Fori(0, 2) as i:
                for s in range(2):
                    for u in range(0, 6, 2):
                        act.wait_ge(s_wops, i * 12 + (s * 6 + u + 1))
                        nc.scalar.activation(flat(yT1)[:, bass.ds(i * 4 * TOK + (s * 6 + u) * TG, TG)], ps[:, u, 0:TG], ACT.Copy).then_inc(s_woact, 1)
            def post_act(rnd):
                for n in range(NT + 1):
                    r = P if n < NT else NS
                    act.wait_ge(s_ytps, (NT + 1) * rnd + n + 1)
                    b = 2 * (n % 2)
                    nc.scalar.activation(junk[0:r, :], ps[0:r, b:b + 2, :].rearrange("p b c -> p (b c)"), ACT.Square,
                                         accum_out=ss[0:r, n:n + 1]).then_inc(s_ytsq, 1)
                    act.wait_ge(s_ytsq, (NT + 1) * rnd + n + 1)
                act.wait_ge(s_ms, 2 * rnd + 2)
                nc.scalar.activation(rstd[:, :], rstd[:, :], ACT.Sqrt).then_inc(s_sd, 1)
            post_act(0)
            for n in range(NT + 1):
                act.wait_ge(s_out2, n + 1)
                r, src = (P, yt[:, n, :]) if n < NT else (NS, yts)
                nc.scalar.activation(junk[0:r, :], src, ACT.Square, accum_out=ss[0:r, n:n + 1]).then_inc(s_ss2, 1)
                act.wait_ge(s_ss2, n + 1)
            act.wait_ge(s_ms, 3)
            nc.scalar.activation(rstd[:, :], rstd[:, :], ACT.Sqrt).then_inc(s_sd, 1)
            h_act(1)
            act.wait_ge(s_hsplit, NT + 3)

            def w_hi(s, count):
                act.wait_ge(s_wl[s], count)
                nc.scalar.activation(wup_hi[s][:, :, :], wup[s], ACT.Copy).then_inc(s_whi, 1)

            def up_act(i, last=False):
                for s in range(2):
                    for q in range(3):
                        u = s * 3 + q
                        if q == 2 and not (last and s):
                            w_hi(1 - s, i * 32 + (UP0 + 32 + 32 * s))
                        act.wait_ge(s_upps, i * 6 + (u + 1))
                        act.wait_ge(s_updve, i * 6 + (u + 1))
                        nc.scalar.activation(sil[u % 2], ps[:, 2 * q, 0:TG], ACT.Silu).then_inc(s_upact, 1)
            w_hi(0, UP0 + 32)
            with act.Fori(0, KF // 2 - 1) as i:
                up_act(i)
            up_act(KF // 2 - 1, last=True)
            with act.Fori(0, KD // 2) as i:
                for u in range(0, 6, 2):
                    act.wait_ge(s_wops, i * 6 + (24 + u + 1))
                    nc.scalar.activation(flat(hT)[:, bass.ds(i * 2 * TOK + u * TG, TG)], ps[:, u, 0:TG], ACT.Copy).then_inc(s_woact, 1)
            post_act(1)

        @block.vector
        def _(dve):
            own = Tally(s_dve)

            def step(ins):
                ins.then_inc(s_dve, 1)
                own.n += 1
                dve.wait_ge(s_dve, own.value())

            nc.vector.memset(ss[:, :], 1.0).then_inc(s_ss, 1)
            dve.sem_inc(s_xT_dve, 2)
            dve.wait_ge(s_vT, 1)
            step(nc.vector.tensor_copy(vecT[:, :], ps[:, 6, 0:96]))
            dve.wait_ge(s_ss, 10)
            nc.vector.tensor_scalar(rstd[:, :], ss[:, :], 1.0 / D, EPS, ALU.mult, ALU.add).then_inc(s_ms, 1)
            dve.wait_ge(s_sd, 1)
            step(nc.vector.reciprocal(rstd[:, :], rstd[:, :]))
            dve.sem_inc(s_modrow, 3)
            with dve.Fori(0, 4) as i:
                for s in range(3):
                    dve.wait_ge(s_ada_used, i * 3 + (s + 1))
                    nc.vector.tensor_scalar(modrow[:, bass.ds(i * 1536 + s * 512, 512)], ps[0:9, 1 + s, :], 1.0, None, ALU.mult)\
                      .then_inc(s_modrow, 1)
            dve.wait_ge(s_modps, 1)
            step(nc.vector.tensor_tensor(modT[:, :, :], ps[:, 0, 0:432].rearrange("p (m c) -> p m c", c=9),
                                         vecT[:, 0:48].unsqueeze(2).to_broadcast([P, 48, 9]), ALU.add))

            def feat(lo):
                return vecT[:, lo:lo + 8].unsqueeze(2).to_broadcast([P, KD, 9])
            nc.vector.scalar_tensor_tensor(sc1[:, :, :], modT[:, 8:16, :], 1.0, feat(64), ALU.add, ALU.mult)
            nc.vector.scalar_tensor_tensor(sc2[:, :, :], modT[:, 32:40, :], 1.0, feat(72), ALU.add, ALU.mult)
            nc.vector.tensor_tensor(gg1[:, :, :], modT[:, 16:24, :], feat(80), ALU.mult)
            step(nc.vector.tensor_tensor(gg2[:, :, :], modT[:, 40:48, :], feat(88), ALU.mult))
            dve.sem_inc(s_mod, 1)
            def h_dve(rnd, rows_p, rows_s):
                sc, sh = (sc1, sc2)[rnd], 24 * rnd
                with dve.Fori(0, NT // 2) as i:
                    for s in range(2):
                        dve.wait_ge(s_xT_dve, 2 * i + (NT * rnd + s + 1))
                        tile = i * 2 + s
                        nc.vector.tensor_scalar(xn[:, s, :], rows_p[:, bass.ds(tile, 1), :].rearrange("p a b -> p (a b)"),
                                                rstd[:, bass.ds(tile, 1)], None, ALU.mult).then_inc(s_xn, 1)
                        dve.wait_ge(s_xT, 2 * i + (NT * rnd + s + 1))
                        if rnd:
                            dve.wait_ge(s_hsplit, 2 * i + (s + 1))
                        for k in range(KD // 2, KD):
                            ins = nc.vector.tensor_scalar(hraw[s][:, k, :] if rnd else hT[:, k, bass.ds(i * 256 + s * P, P)],
                                                          ps[:, 2 * s + k // 4, (k % 4) * P:(k % 4 + 1) * P],
                                                          sc[:, k, 0:1], modT[:, sh + k, 0:1], ALU.mult, ALU.add)
                        ins.then_inc(s_xT_dve, 1)
                dve.wait_ge(s_xT_dve, NT * rnd + NT + 2)
                nc.vector.tensor_scalar(xn[0:NS, 0, :], rows_s, rstd[0:NS, 8:9], None, ALU.mult).then_inc(s_xn, 1)
                dve.wait_ge(s_sT, rnd + 1)
                sT = ps[:, 4, 0:64].rearrange("p (k c) -> p k c", c=NS)
                hs_ = hraw_s if rnd else hT[:, :, SEQ:TOK]
                step(nc.vector.tensor_tensor(hs_, sT, sc[:, :, 1:9], ALU.mult))
                nc.vector.tensor_tensor(hs_, hs_, modT[:, sh:sh + 8, 1:9], ALU.add).then_inc(s_sh, 1)
            h_dve(0, xin, xs)

            dve.sem_inc(s_mix, 4)
            dve.wait_ge(s_bmix, 16)
            with dve.Fori(0, MIX // PB // 2) as i:
                for s in range(2):
                    for n in range(9):
                        dve.wait_ge(s_mixps, i * 18 + (s * 9 + n + 1))
                        cols = bass.ds(i * 2 * PB + s * PB, PB)
                        rows, dst = (P, Pm[:, n, cols]) if n < NT else (NS, Ps[:, cols])
                        nc.vector.tensor_tensor(dst, ps[0:rows, n % 4 if n < NT else 4, 0:PB], bmix[0:rows, cols],
                                                ALU.add).then_inc(s_mix, 1)
            dve.wait_ge(s_mix, 4 + 72)
            for rows, pm, lead in ((P, Pm, [NT]), (NS, Ps, [])):
                for lo, heads in ((C_NQ, NH), (C_KV, NKV), (C_KV + 256, NKV), (C_KV + 512, NKV)):
                    h8 = heads * 8
                    if lead:
                        v = pm[:, :, lo:lo + heads * HD].rearrange("p t (h d) -> p t h d", d=HD)
                        x1, x2 = v[:, :, :, 0:8], v[:, :, :, 8:16]
                        tmp = [xn[:, j // 2, (j % 2) * 512:(j % 2) * 512 + NT * h8].rearrange("p (t h d) -> p t h d", t=NT, d=8)
                               for j in range(4)]
                        co, si = (cst(c).rearrange("p (t d) -> p t d", t=NT).unsqueeze(2).to_broadcast([P, NT, heads, 8])
                                  for c in ("cos", "sin"))
                    else:
                        v = pm[:, lo:lo + heads * HD].rearrange("p (h d) -> p h d", d=HD)
                        x1, x2 = v[:, :, 0:8], v[:, :, 8:16]
                        tmp = [xn[0:NS, j // 2, (j % 2) * 512:(j % 2) * 512 + h8].rearrange("p (h d) -> p h d", d=8)
                               for j in range(4)]
                        co, si = (cst(c, NS).unsqueeze(1).to_broadcast([NS, heads, 8]) for c in ("scos", "ssin"))
                    nc.vector.tensor_tensor(tmp[0], x1, co, ALU.mult)
                    nc.vector.tensor_tensor(tmp[1], x2, si, ALU.mult)
                    nc.vector.tensor_tensor(tmp[2], x2, co, ALU.mult)
                    step(nc.vector.tensor_tensor(tmp[3], x1, si, ALU.mult))
                    nc.vector.tensor_tensor(x1, tmp[0], tmp[1], ALU.subtract)
                    step(nc.vector.tensor_tensor(x2, tmp[2], tmp[3], ALU.add))
            dve.sem_inc(s_rope, 1)

            step(nc.vector.memset(gate, 0.0))
            dve.wait_ge(s_rope, 1)
            step(nc.vector.tensor_copy(gate[:, 0:NT, :], Pm[:, :, C_MI:C_MI + 8]))
            nc.vector.tensor_copy(gate[0:NS, NT, :], Ps[:, C_MI:C_MI + 8]).then_inc(s_gate, 1)
            dve.wait_ge(s_tanh, 1)
            g4 = gate.rearrange("p t (a h) -> p t a h", a=2)
            lf3, gi3, gt3 = (x.rearrange("p (t h) -> p t h", h=MH) for x in (lf, gi, gtmp))
            nc.vector.tensor_scalar(gi3, g4[:, :, 0, :], CAP, None, ALU.mult)
            step(nc.vector.tensor_scalar(lf3, g4[:, :, 1, :], CAP, None, ALU.mult))
            nc.vector.scalar_tensor_tensor(gtmp, lf, -1.0, lf, ALU.mult, ALU.max).then_inc(s_gabs, 1)
            dve.wait_ge(s_gln, 2)
            nc.vector.scalar_tensor_tensor(lf, lf, 0.0, gtmp, ALU.min, ALU.subtract).then_inc(s_gate, 1)
            dve.wait_ge(s_gRps, 1)
            nc.vector.tensor_copy(iR, ps[0:32, 5, 0:P])
            step(nc.vector.tensor_copy(fR, ps[0:32, 5, P:2 * P]))
            dve.wait_ge(s_ones, 1)
            step(nc.vector.tensor_tensor_scan(bR, ones[0:32, :], fR, 0.0, ALU.mult, ALU.add))
            step(nc.vector.tensor_tensor(aR, iR, bR, ALU.subtract))
            step(nc.vector.tensor_tensor_scan(AR, ones[0:32, :], aR, -3e38, ALU.mult, ALU.max))
            dve.sem_inc(s_gR, 1)
            dve.wait_ge(s_rowps, 1)
            step(nc.vector.tensor_copy(row[:, 0:2, :], ps[0:1, 5, 0:64].rearrange("p (a b) -> p a b", a=2)))
            for h in range(MH):
                ins = nc.vector.tensor_tensor_scan(row[:, 2, h::MH], row[:, 0, h::MH], row[:, 1, h::MH], 0.0, ALU.max, ALU.add)
            nc.vector.memset(row[:, 3, 0:MH], 0.0)
            step(nc.vector.memset(row[:, 4, :], 0.0))
            step(nc.vector.tensor_copy(row[:, 3, MH:32], row[:, 2, 0:32 - MH]))
            step(nc.vector.tensor_tensor(row[:, 4, :], row[:, 0, :], row[:, 3, :], ALU.max))
            nc.vector.tensor_tensor(row[:, 5, :], row[:, 3, :], row[:, 4, :], ALU.subtract).then_inc(s_rowsb, 1)
            dve.wait_ge(s_colps, 1)
            step(nc.vector.tensor_copy(colR[:, 0:2], ps[0:32, 6, 0:2]))
            step(nc.vector.tensor_scalar(colR[:, 2:3], colR[:, 1:2], -1.0, None, ALU.mult))
            step(nc.vector.tensor_scalar(nmxR, AR, colR[:, 0:1], -1.0, ALU.max, ALU.mult))
            nc.vector.tensor_tensor(emR, bR, nmxR, ALU.subtract).then_inc(s_bR, 1)
            dve.wait_ge(s_tokps, 1)
            nc.vector.tensor_copy(tok, ps[:, 5, 0:P].rearrange("p (a b) -> p a b", a=4))
            step(nc.vector.tensor_copy(astB, ps[:, 5, P:P + 32]))
            nc.vector.memset(Cst[:, :, :], 0.0).then_inc(s_tok, 1)
            dve.wait_ge(s_tok, 1)
            for x in (s_C, s_h, s_arg, s_w):
                dve.sem_inc(x, 1)

            def m_front(c, s):
                dve.wait_ge(s_qkps, c + 1)
                nc.vector.tensor_copy(kT[s], ps[0:DQK, 1, :].rearrange("p (h t) -> p h t", h=MH)).then_inc(s_kTs, 1)
                dve.wait_ge(s_zps, c + 2)
                dve.wait_ge(s_w, c + 1)
                for h in range(MH):
                    ins = nc.vector.scalar_tensor_tensor(wexp[:, h, :], ps[:, 3, h * P:(h + 1) * P],
                                                         tok[:, 0, bass.ds(c * MH + h, 1)], cst("causal_st"),
                                                         ALU.add, ALU.min)
                ins.then_inc(s_arg, 1)

            def m_weights(c, s):
                dve.wait_ge(s_we, c + 1)
                dve.wait_ge(s_Sps, c + 1)
                nc.vector.tensor_tensor(wgt[s], wexp, ps[:, 4, :].rearrange("p (h t) -> p h t", h=MH), ALU.mult).then_inc(s_w, 1)

            def m_back(c):
                dve.wait_ge(s_st, c + 3)
                num = ps[:, 5:7, 0:2 * (DV + 1)].rearrange("p b (j e) -> p b j e", e=DV + 1)
                step(nc.vector.tensor_copy(dn.rearrange("p (b j) -> p b j", b=2), num[:, :, :, DV]))
                for h in range(MH):
                    src = ps[0:DQK, 7, h * (DV + 1):(h + 1) * (DV + 1)] if h < 3 else ps[0:DQK, 6, 2 * (DV + 1):3 * (DV + 1)]
                    ins = nc.vector.scalar_tensor_tensor(Cst[:, h, :], Cst[:, h, :], astB[0:DQK, bass.ds(c * MH + h, 1)],
                                                         src, ALU.mult, ALU.add)
                ins.then_inc(s_C, 1)
                step(nc.vector.scalar_tensor_tensor(dn, dn, -1.0, dn, ALU.mult, ALU.max))
                step(nc.vector.tensor_tensor(dn, dn, tok[:, 2, bass.ds(c * MH, MH)], ALU.max))
                step(nc.vector.reciprocal(dn, dn))
                pm = Pm[:, bass.ds(c, 1), 512:1024].rearrange("p a (b j v) -> p (a b) j v", b=2, v=DV)
                for b in range(2):
                    ins = nc.vector.tensor_tensor(pm[:, b, :, :], num[:, b, :, 0:DV],
                                                  dn[:, 2 * b:2 * b + 2].unsqueeze(2).to_broadcast([P, 2, DV]), ALU.mult)
                ins.then_inc(s_h, 1)
            m_front(0, 0)
            m_weights(0, 0)
            with dve.Fori(0, NT // 2 - 1) as i:
                own.loop(i, 8)
                for s in range(2):
                    m_front(i * 2 + (s + 1), 1 - s)
                    m_back(i * 2 + s)
                    m_weights(i * 2 + (s + 1), 1 - s)
            own.end(NT // 2 - 1)
            m_front(NT - 1, 1)
            m_back(NT - 2)
            m_weights(NT - 1, 1)
            m_back(NT - 1)
            dve.wait_ge(s_h, NT + 1)
            H4 = Pm[:, :, 512:1024].rearrange("p t (h v) -> p t h v", v=DV)
            for c in range(NT):
                step(nc.vector.tensor_tensor(wexp, H4[:, c], H4[:, c], ALU.mult))
                step(nc.vector.tensor_reduce(hn[:, c * MH:(c + 1) * MH], wexp, AX.X, ALU.add))
            nc.vector.tensor_scalar(hn, hn, 1.0 / DV, EPS, ALU.mult, ALU.add).then_inc(s_h, 1)
            dve.wait_ge(s_hsd, 1)
            step(nc.vector.reciprocal(hn, hn))
            dve.wait_ge(s_mo, 1)
            for c in range(NT):
                sl = H4[:, c]
                step(nc.vector.tensor_tensor(sl, sl, hn[:, c * MH:(c + 1) * MH].unsqueeze(2).to_broadcast([P, MH, DV]), ALU.mult))
                step(nc.vector.tensor_tensor(Pm[:, c, 512:1024], Pm[:, c, 512:1024], mnormB[:, :], ALU.mult))
                nc.vector.tensor_tensor(Pm[:, c, 512:1024], Pm[:, c, 512:1024], Pm[:, c, C_MO:C_MO + 512], ALU.mult).then_inc(s_y, 1)
            for c in range(NT):
                dve.wait_ge(s_yT, c + 1)
                nc.vector.tensor_copy(yaT[:, :, c * P:(c + 1) * P], ps[:, c % 4, :].rearrange("p (h t) -> p h t", h=MH)).then_inc(s_ya, 1)

            for j in range(0, 4, 2):
                dve.wait_ge(s_kvps, j + 1)
                nc.vector.tensor_copy((ksT, kwT)[j // 2][:, 0:512], ps[:, j, :]).then_inc(s_kvT, 1)
            dve.wait_ge(s_cps, 1)
            nc.vector.tensor_copy(kcT, ps[:, 0, 0:NCMP]).then_inc(s_cT2, 1)
            nc.vector.tensor_copy(vc, ps[0:NCMP, 0, 64:64 + NKV * HD]).then_inc(s_cT2, 1)
            dve.sem_inc(s_ev[0], 1)
            dve.wait_ge(s_gts, 1)

            def att_max(u, h):
                kind, i, lo, blocks, _ = units[u]
                span = ps[:, 2 * (u % 2):2 * (u % 2) + 2, :].rearrange("p b c -> p (b c)")
                n = (i + 1 - lo) * P
                dve.wait_ge(s_S, h * NU + (u + 1))
                ins = nc.vector.tensor_tensor(span[:, n - P:n], span[:, n - P:n], cst("causal_ts"), ALU.add)
                if kind == "w":
                    cm = span[:, 5 * P:5 * P + NCMP]
                    ins = nc.vector.tensor_tensor(cm, cm, cst("cmp_add")[:, i * NCMP:(i + 1) * NCMP], ALU.add)
                    if i >= WIN // P:
                        ins = nc.vector.tensor_tensor(span[:, 0:P], span[:, 0:P], cst("window_ts"), ALU.add)
                step(ins)
                if kind == "w":
                    nc.vector.tensor_reduce(nmx[:, 3 * i:3 * i + 1], span[:, 5 * P:5 * P + NCMP], AX.X, ALU.max, negate=True)
                j = 1 if kind == "s" else 2
                nc.vector.tensor_reduce(nmx[:, 3 * i + j:3 * i + j + 1], span[:, 0:n], AX.X, ALU.max, negate=True)\
                  .then_inc(s_max, 1)

            def att_scale(u, h):
                kind, i, lo, blocks, gr = units[u]
                dve.wait_ge(s_exp, h * NU + (u + 1))
                js = (1,) if kind == "s" else (0, 2)
                span_j = slice(js[0], js[-1] + 1, 2 if kind == "w" else 1)
                step(nc.vector.reciprocal(gsc[:, i, span_j], rsum[:, i, span_j]))
                step(nc.vector.tensor_tensor(gsc[:, i, span_j], gsc[:, i, span_j],
                                             gts[:, i, bass.ds(h * 3, 3)][:, span_j], ALU.mult))
                n = (i + 1 - lo) * P
                pb = pbuf[u % 2]
                if kind == "w":
                    cm = pb[:, 5 * P:5 * P + NCMP]
                    if i == 0:
                        nc.vector.scalar_tensor_tensor(cm, cm, gsc[:, i, 0:1], cst("cmp_one")[:, 0:NCMP], ALU.mult, ALU.mult)
                    else:
                        nc.vector.tensor_scalar(cm, cm, gsc[:, i, 0:1], None, ALU.mult)
                nc.vector.tensor_scalar(pb[:, 0:n], pb[:, 0:n], gsc[:, i, js[-1]:js[-1] + 1], None, ALU.mult).then_inc(s_scaled, 1)

            dve.wait_ge(s_pt[0], 1)
            nc.vector.tensor_scalar(qTh[:, 0:512], ps[:, 4, :], HD ** -0.5, None, ALU.mult).then_inc(s_ev[0], 1)
            with dve.Fori(0, NH) as h:
                own.loop(h, 3 * NU)
                att_max(0, h)
                att_max(1, h)
                att_scale(0, h)
                for u in range(NU):
                    for j, ((b, turn), g) in enumerate(zip(groups[u], units[u][4])):
                        if b == 0:
                            dve.wait_ge(s_pt[0], h * GN[0] + (turn + 2))
                            if u >= 2:
                                dve.wait_ge(s_pv, h * NU + (u - 1))
                            full = sum(1 for c, w, _ in g if w == P)
                            if full:
                                ins = nc.vector.tensor_copy(ptbuf[u % 2][:, j * 512:j * 512 + full * P], ps[:, 4, 0:full * P])
                            if full < len(g):
                                ins = nc.vector.tensor_copy(ptbuf[u % 2][0:NCMP, j * 512 + full * P:j * 512 + (full + 1) * P],
                                                            ps[0:NCMP, 4, full * P:(full + 1) * P])
                            ins.then_inc(s_ev[0], 1)
                    if u + 1 < NU:
                        att_scale(u + 1, h)
                    if u + 2 < NU:
                        att_max(u + 2, h)
                    if u == NU - 2:
                        dve.wait_ge(s_pt[0], h * GN[0] + (q_turn[0] + 2))
                        nc.vector.tensor_scalar(qTh[:, 0:512], ps[:, 4, :], HD ** -0.5, None, ALU.mult).then_inc(s_ev[0], 1)
            own.end(NH)

            dve.wait_ge(s_smp, 16 * 34)
            for x in (sg, hg):
                step(nc.vector.tensor_tensor(x[:, 6:7], x[:, 1:2], x[:, 2:3], ALU.add))
                step(nc.vector.tensor_tensor(x[:, 3:4], x[:, 6:7], x[:, 0:1], ALU.max))
                nc.vector.tensor_tensor(x[:, 4:5], x[:, 0:1], x[:, 3:4], ALU.subtract)
                step(nc.vector.tensor_tensor(x[:, 5:6], x[:, 6:7], x[:, 3:4], ALU.subtract))
                step(nc.vector.memset(x[:, 6:8], 0.0))
            nc.vector.tensor_copy(hg[:, 7:8], hg[:, 3:4]).then_inc(s_cg, 1)
            step(nc.vector.tensor_scalar(sq, sq, DQK ** -0.5, None, ALU.mult))
            step(nc.vector.tensor_tensor(sT_, sC, sq.unsqueeze(2).to_broadcast([P, DQ, DV]), ALU.mult))
            nc.vector.tensor_reduce(sW[:, 0:DV], sT_.rearrange("p a v -> p v a"), AX.X, ALU.add)
            step(nc.vector.tensor_tensor(hsum[:, 0, :], sq, sk, ALU.mult))
            step(nc.vector.tensor_tensor(hsum[:, 1, :], sq, sn, ALU.mult))
            nc.vector.tensor_reduce(sW[:, DV:DV + 2], hsum, AX.X, ALU.add).then_inc(s_sWd, 1)
            dve.wait_ge(s_cge, 1)
            dve.wait_ge(s_sWd, 1)
            step(nc.vector.tensor_scalar(sk, sk, sg[:, 4:5], None, ALU.mult))
            step(nc.vector.tensor_tensor(sT_, sk.unsqueeze(2).to_broadcast([P, DQ, DV]),
                                         sv.unsqueeze(1).to_broadcast([P, DQ, DV]), ALU.mult))
            nc.vector.scalar_tensor_tensor(sC, sC, sg[:, 5:6], sT_, ALU.mult, ALU.add)
            step(nc.vector.scalar_tensor_tensor(sn, sn, sg[:, 5:6], sk, ALU.mult, ALU.add))
            dve.sem_inc(s_sCn, 1)
            dve.wait_ge(s_sWp, 1)
            step(nc.vector.tensor_copy(hs, ps[0:32, 0, 0:DV + 2]))
            step(nc.vector.tensor_tensor(hg[:, 8:9], hs[:, DV:DV + 1], hg[:, 4:5], ALU.mult))
            step(nc.vector.tensor_scalar(hv, hv, hg[:, 8:9], None, ALU.mult))
            step(nc.vector.scalar_tensor_tensor(hv, hs[:, 0:DV], hg[:, 5:6], hv, ALU.mult, ALU.add))
            step(nc.vector.scalar_tensor_tensor(hg[:, 8:9], hs[:, DV + 1:DV + 2], hg[:, 5:6], hg[:, 8:9], ALU.mult, ALU.add))
            step(nc.vector.scalar_tensor_tensor(hg[:, 8:9], hg[:, 8:9], -1.0, hg[:, 8:9], ALU.mult, ALU.max))
            step(nc.vector.tensor_tensor(hg[:, 8:9], hg[:, 8:9], hg[:, 7:8], ALU.max))
            step(nc.vector.reciprocal(hg[:, 8:9], hg[:, 8:9]))
            step(nc.vector.tensor_scalar(hv, hv, hg[:, 8:9], None, ALU.mult))
            step(nc.vector.tensor_tensor(hsq, hv, hv, ALU.mult))
            step(nc.vector.tensor_reduce(hg[:, 9:10], hsq, AX.X, ALU.add))
            nc.vector.tensor_scalar(hg[:, 9:10], hg[:, 9:10], 1.0 / DV, EPS, ALU.mult, ALU.add).then_inc(s_sh2, 1)
            dve.wait_ge(s_shd, 2)
            step(nc.vector.reciprocal(hg[:, 9:10], hg[:, 9:10]))
            step(nc.vector.tensor_scalar(hv, hv, hg[:, 9:10], None, ALU.mult))
            step(nc.vector.tensor_tensor(hv, hv, hw, ALU.mult))
            nc.vector.tensor_tensor(hv, hv, hmo, ALU.mult).then_inc(s_sh2, 1)
            step(nc.vector.memset(Qall, 0.0))
            nc.vector.memset(zrow, 0.0).then_inc(s_zero, 1)
            dve.wait_ge(s_Qps, 1)
            for g in range(NKV):
                nc.vector.tensor_scalar(Qall[g * HD:(g + 1) * HD, :, g * HPG:(g + 1) * HPG].rearrange("p b h -> p h b"),
                                        ps[0:HD, 1, g * HPG * NS:(g + 1) * HPG * NS].rearrange("p (h b) -> p h b", b=NS),
                                        HD ** -0.5, None, ALU.mult)
            step(nc.vector.tensor_copy(knT, ps[:, 1, 64:80].rearrange("p (a b) -> p a b", a=2)))
            dve.sem_inc(s_Qall, 1)
            dve.wait_ge(s_syT, 1)
            nc.vector.tensor_copy(yaT[:, :, SEQ:TOK], ps[:, 2, 0:32].rearrange("p (b h) -> p h b", h=MH)).then_inc(s_sya, 1)
            with dve.Fori(0, NS) as b:
                dve.wait_ge(s_free, b + 2)
                nc.vector.tensor_tensor(Qpad, Qall, cst("onehot")[:, bass.ds(b * NS, NS)].unsqueeze(2).to_broadcast([P, NS, NH]),
                                        ALU.mult).then_inc(s_qp, 1)
                dve.wait_ge(s_pgps, 2 * b + 1)
                nc.vector.tensor_copy(pT[:, 512:1024], ps[:, 5, :])
                dve.wait_ge(s_pgps, 2 * b + 2)
                nc.vector.tensor_copy(ckT, ps[:, 7, 0:NCMP])
                nc.vector.tensor_scalar(vcs[:, bass.ds(b, 1), :].rearrange("p a c -> p (a c)"),
                                        ps[0:NCMP, 7, 64:64 + NKV * HD], 1.0, None, ALU.mult).then_inc(s_pgd, 1)
            dve.wait_ge(s_free, 2 + NS)
            dve.wait_ge(s_soft, 1)
            nc.vector.tensor_copy(Scm, ps[0:SR, 3, 64:64 + NCMP])
            step(nc.vector.tensor_copy(Swn[:, 0:WIN], ps[0:SR, 2, :]))
            nc.vector.tensor_tensor(Swn[:, WIN:], ps[0:SR, 3, 8:16], cst("own_new", SR), ALU.add)
            nc.vector.tensor_tensor(Ssl[:, PAST:], ps[0:SR, 3, 0:8], cst("own_new", SR), ALU.add)
            step(nc.vector.memset(Swn[:, 0:1], NEG))
            nc.vector.tensor_reduce(small[:, 0:1], Scm, AX.X, ALU.max, negate=True).then_inc(s_softm, 1)
            nc.vector.tensor_reduce(small[:, 2:3], Swn, AX.X, ALU.max, negate=True).then_inc(s_softm, 1)
            dve.wait_ge(s_softe, 1)
            step(nc.vector.reciprocal(small[:, 8:9], small[:, 4:5]))
            nc.vector.tensor_scalar(pcm, Scm, small[:, 8:9], None, ALU.mult).then_inc(s_soft, 1)
            dve.wait_ge(s_impps, 1)
            step(nc.vector.tensor_reduce(imp, ps[0:SR, 7, 0:NCMP].rearrange("p (k r) -> p k r", r=2), AX.X, ALU.add))
            step(nc.vector.tensor_reduce(small[:, 9:10], imp[:, 1:16], AX.X, ALU.min))
            step(nc.vector.scalar_tensor_tensor(imp[:, 1:16], imp[:, 1:16], small[:, 9:10], cst("blk", SR)[:, 1:16],
                                                ALU.is_equal, ALU.mult))
            step(nc.vector.tensor_reduce(small[:, 10:11], imp[:, 1:16], AX.X, ALU.max))
            step(nc.vector.tensor_scalar(msk, cst("blk", SR), small[:, 10:11], NEG, ALU.is_equal, ALU.mult))
            for j in range(2):
                ins = nc.vector.tensor_tensor(Ssl[:, j * 512:(j + 1) * 512].rearrange("p (k c) -> p k c", c=SEL),
                                              ps[0:SR, j, :].rearrange("p (k c) -> p k c", c=SEL),
                                              msk[:, j * 8:(j + 1) * 8].unsqueeze(2).to_broadcast([SR, 8, SEL]), ALU.add)
            step(ins)
            nc.vector.tensor_reduce(small[:, 1:2], Ssl, AX.X, ALU.max, negate=True).then_inc(s_softm, 1)
            dve.wait_ge(s_softe, 3)
            step(nc.vector.reciprocal(small[:, 4:7], small[:, 4:7]))
            step(nc.vector.tensor_tensor(small[:, 4:7], small[:, 4:7], sgt, ALU.mult))
            for j, x in ((0, Scm), (1, Ssl), (2, Swn)):
                ins = nc.vector.tensor_scalar(x, x, small[:, 4 + j:5 + j], None, ALU.mult)
            step(ins)
            dve.sem_inc(s_soft, 1)
            dve.wait_ge(s_sPT, 1)
            nc.vector.tensor_copy(PTw[:, 0:256], ps[:, 5, 0:256])
            nc.vector.tensor_copy(PTw[0:NCMP, 256:320], ps[0:NCMP, 5, 256:320])
            nc.vector.tensor_copy(PTw[0:NS, 320:448], ps[0:NS, 5, 320:448]).then_inc(s_sPTe, 1)
            dve.wait_ge(s_Osum, 1)
            for h in range(NH):
                g, odd = h // HPG, h % 2
                ins = nc.vector.tensor_copy(ybT[odd * HD:(odd + 1) * HD, h // 2, SEQ:TOK],
                                            ps[g * HD:(g + 1) * HD, 6, h:SR:NH])
            ins.then_inc(s_yb, 1)

            dve.sem_inc(s_mgdve, 2)
            with dve.Fori(0, 2) as i:
                own.loop(i, 12)
                for s in range(2):
                    for m in range(2):
                        for q in range(3):
                            u = (s * 2 + m) * 3 + q
                            dve.wait_ge(s_mgact, i * 12 + (u + 1))
                            nc.vector.tensor_tensor(sgm[2 * (u % 2)], sgm[2 * (u % 2)], ps[:, 4 * (u % 2) + 2, 0:TG], ALU.mult)
                            step(nc.vector.tensor_tensor(sgm[2 * (u % 2) + 1], sgm[2 * (u % 2) + 1],
                                                         ps[:, 4 * (u % 2) + 3, 0:TG], ALU.mult))
                            nc.vector.tensor_tensor(merT[:, bass.ds(i * 4 + (s * 2 + m), 1), q * TG:(q + 1) * TG]
                                                    .rearrange("p a c -> p (a c)"),
                                                    sgm[2 * (u % 2)], sgm[2 * (u % 2) + 1], ALU.add).then_inc(s_mgdve, 1)
            own.end(2)
            dve.sem_inc(s_wodve, 3)
            with dve.Fori(0, 2) as i:
                for s in range(2):
                    for u in range(1, 6, 2):
                        dve.wait_ge(s_wops, i * 12 + (s * 6 + u + 1))
                        nc.vector.tensor_scalar(yT1[:, bass.ds(i * 4 + (s * 2 + u // 3), 1), (u % 3) * TG:(u % 3 + 1) * TG]
                                                .rearrange("p a c -> p (a c)"), ps[:, u, 0:TG], 1.0, None, ALU.mult)\
                          .then_inc(s_wodve, 1)

            def post_dve(rnd, gg, Gp, Gsm):
                for k in range(KD):
                    ins = nc.vector.tensor_scalar(diag[rnd][:, k * P:(k + 1) * P], ident, gg[:, k, 0:1], None, ALU.mult)
                ins.then_inc(s_diag, 1)
                dve.wait_ge(s_Gps, rnd + 1)
                nc.vector.tensor_copy(Gp, ps[:, 4:6, :].rearrange("p b c -> p (b c)"))
                step(nc.vector.tensor_copy(Gsm, ps[0:NS, 6:8, :].rearrange("p b c -> p (b c)")))
                for n in range(NT + 1):
                    r, dst, g = (P, yt[:, n, :], Gp) if n < NT else (NS, yts, Gsm)
                    b = 2 * (n % 2)
                    dve.wait_ge(s_ytsq, (NT + 1) * rnd + n + 1)
                    nc.vector.tensor_tensor(dst, ps[0:r, b:b + 2, :].rearrange("p b c -> p (b c)"), g, ALU.mult).then_inc(s_ytdve, 1)
                nc.vector.tensor_scalar(rstd[:, :], ss[:, :], 1.0 / D, EPS, ALU.mult, ALU.add).then_inc(s_ms, 1)
                dve.wait_ge(s_ytdve, (NT + 1) * (rnd + 1))
                dve.wait_ge(s_sd, 2 * rnd + 2)
                step(nc.vector.reciprocal(rstd[:, :], rstd[:, :]))
                dve.wait_ge(s_x1in, 32 * (rnd + 1))
                for n in range(NT + 1):
                    r, x, y = (P, xres[:, n, :], yt[:, n, :]) if n < NT else (NS, xress, yts)
                    nc.vector.scalar_tensor_tensor(x if rnd else y, y, rstd[0:r, n:n + 1], x, ALU.mult, ALU.add)\
                      .then_inc(s_out if rnd else s_out2, 1)
            dve.wait_ge(s_mgdve, 26)
            post_dve(0, gg1, G, Gs)
            dve.wait_ge(s_ss2, NT + 1)
            nc.vector.tensor_scalar(rstd[:, :], ss[:, :], 1.0 / D, EPS, ALU.mult, ALU.add).then_inc(s_ms, 1)
            dve.wait_ge(s_sd, 3)
            step(nc.vector.reciprocal(rstd[:, :], rstd[:, :]))
            h_dve(1, yt, yts)
            def w_lo(s, count):
                dve.wait_ge(s_whi, count)
                nc.vector.tensor_tensor(wup_lo[s][:, :, :], wup[s], wup_hi[s][:, :, :], ALU.subtract).then_inc(s_wlo, 1)

            def up_dve(i, last=False):
                for s in range(2):
                    for q in range(3):
                        u = s * 3 + q
                        if q == 2 and not (last and s):
                            w_lo(1 - s, i * 2 + (s + 2))
                        dve.wait_ge(s_upact, i * 6 + (u + 1))
                        nc.vector.tensor_tensor(aT[:, bass.ds(i * 2 + s, 1), q * TG:(q + 1) * TG].rearrange("p a c -> p (a c)"),
                                                sil[u % 2], ps[:, 2 * q + 1, 0:TG], ALU.mult).then_inc(s_updve, 1)
            w_lo(0, 1)
            dve.wait_ge(s_x1out, 16 * (NT + 1))
            dve.sem_inc(s_updve, 2)
            with dve.Fori(0, KF // 2 - 1) as i:
                up_dve(i)
            up_dve(KF // 2 - 1, last=True)
            with dve.Fori(0, KD // 2) as i:
                for u in range(1, 6, 2):
                    dve.wait_ge(s_wops, i * 6 + (24 + u + 1))
                    nc.vector.tensor_scalar(hT[:, bass.ds(i * 2 + u // 3, 1), (u % 3) * TG:(u % 3 + 1) * TG]
                                            .rearrange("p a c -> p (a c)"), ps[:, u, 0:TG], 1.0, None, ALU.mult)\
                      .then_inc(s_wodve, 1)
            dve.wait_ge(s_woused, 4 + KD)
            post_dve(1, gg2, G2, G2s)

        @block.tensor
        def _(pe):
            pe.wait_ge(s_const, 32)
            pe.wait_ge(s_c, 32)
            for k in range(KD):
                ins = nc.tensor.transpose(ps[:, 7, k * 9:(k + 1) * 9], cin[:, k * P:(k + 1) * P], ident[0:9, 0:9])
            ins.then_inc(s_cT, 1)
            pe.wait_ge(s_vrow, 96)
            nc.tensor.transpose(ps[:, 6, 0:96], vrows, ident[0:96, 0:96]).then_inc(s_vT, 1)
            pe.wait_ge(s_cS, 1)
            with pe.Fori(0, 4) as i:
                for s in range(3):
                    pe.wait_ge(s_ada[s], i * 16 + 16)
                    pe.wait_ge(s_modrow, i * 3 + (s + 1))
                    for k in range(KD):
                        ins = nc.tensor.matmul(ps[0:9, 1 + s, :], cT[:, k, :], wada[s][:, k, :],
                                               start=(k == 0), stop=(k == KD - 1))
                    ins.then_inc(s_ada_used, 1)
            pe.wait_ge(s_modrow, 3 + 12)
            for m in range(48):
                ins = nc.tensor.transpose(ps[:, 0, m * 9:(m + 1) * 9], modrow[:, m * P:(m + 1) * P], ident[0:9, 0:9])
            ins.then_inc(s_modps, 1)
            pe.wait_ge(s_mod, 1)
            def h_pe(rnd):
                with pe.Fori(0, NT // 2) as i:
                    for s in range(2):
                        pe.wait_ge(s_xn, 2 * i + ((NT + 1) * rnd + s + 1))
                        pe.wait_ge(s_xT_act, 2 * i + (NT * rnd + s + 1))
                        for k in range(KD):
                            ins = nc.tensor.transpose(ps[:, 2 * s + k // 4, (k % 4) * P:(k % 4 + 1) * P],
                                                      xn[:, s, k * P:(k + 1) * P], ident)
                        ins.then_inc(s_xT, 1)
                pe.wait_ge(s_xn, (NT + 1) * (rnd + 1))
                for k in range(KD):
                    ins = nc.tensor.transpose(ps[:, 4, k * NS:(k + 1) * NS], xn[0:NS, 0, k * P:(k + 1) * P],
                                              ident[0:NS, 0:NS])
                ins.then_inc(s_sT, 1)
                pe.wait_ge(s_xT_act, NT * rnd + NT + 2)
                pe.wait_ge(s_xT_dve, NT * rnd + NT + 2)
                pe.wait_ge(s_sh, rnd + 1)
            h_pe(0)
            with pe.Fori(0, MIX // PB // 2) as i:
                for s in range(2):
                    pe.wait_ge(s_wmix[s], i * 16 + 16)
                    for n in range(9):
                        pe.wait_ge(s_mix, i * 18 + (s * 9 + n + 1))
                        rows = P if n < NT else NS
                        for k in range(KD):
                            ins = nc.tensor.matmul(ps[0:rows, n % 4 if n < NT else 4, 0:PB],
                                                   hT[:, k, n * P:n * P + rows], wmix[s][:, k, :],
                                                   start=(k == 0), stop=(k == KD - 1))
                        ins.then_inc(s_mixps, 1)
                    pe.wait_ge(s_mixps, i * 18 + (s * 9 + 9))
                    pe.sem_inc(s_wmix_used, 1)
            pe.wait_ge(s_mix, 4 + 72)
            pe.wait_ge(s_gate, 2)
            nc.tensor.transpose(ps[0:32, 5, 0:P], gi[:, 0:32], ident)
            nc.tensor.transpose(ps[0:32, 5, P:2 * P], lf[:, 0:32], ident).then_inc(s_gRps, 1)
            pe.wait_ge(s_gR, 1)
            nc.tensor.transpose(ps[0:1, 5, 0:32], AR[:, P - 1:P], ident[0:32, 0:32])
            nc.tensor.transpose(ps[0:1, 5, 32:64], bR[:, P - 1:P], ident[0:32, 0:32]).then_inc(s_rowps, 1)
            pe.wait_ge(s_rowsb, 1)
            nc.tensor.transpose(ps[0:32, 6, 0:1], row[:, 3, :], ident[0:1, 0:1])
            nc.tensor.transpose(ps[0:32, 6, 1:2], row[:, 4, :], ident[0:1, 0:1]).then_inc(s_colps, 1)
            pe.wait_ge(s_gexp, 1)
            for j, r in enumerate((aR, eiR, emR, ainR)):
                nc.tensor.transpose(ps[:, 5, j * 32:(j + 1) * 32], r, ident[0:32, 0:32])
            nc.tensor.matmul(ps[:, 5, P:P + 32], ones[0:1, :], row[:, 5, :], start=True, stop=True).then_inc(s_tokps, 1)
            pe.wait_ge(s_tok, 1)
            pe.sem_inc(s_st, 2)
            pe.sem_inc(s_zps, 1)

            def m_front(c, s):
                pe.wait_ge(s_stage, c * 2 + 1)
                pe.wait_ge(s_arg, c + 1)
                nc.tensor.matmul(ps[:, 3, :], ones[0:32, :], nmxM.rearrange("p h t -> p (h t)"), start=True, stop=True)\
                  .then_inc(s_zps, 1)
                for h in range(MH):
                    nc.tensor.transpose(ps[0:DQK, 0, h * P:(h + 1) * P], qk[s][:, h, :], ident)
                    nc.tensor.transpose(ps[0:DQK, 2, h * P:(h + 1) * P], qe[s][:, h, :], ident)
                    ins = nc.tensor.transpose(ps[0:DQK, 1, h * P:(h + 1) * P], qk[s][:, MH + h, :], ident)
                ins.then_inc(s_qkps, 1)

            def m_scores(c, s):
                pe.wait_ge(s_qTs, c + 1)
                pe.wait_ge(s_kTs, c + 1)
                for h in range(MH):
                    ins = nc.tensor.matmul(ps[:, 4, h * P:(h + 1) * P], kT[s][:, h, :], qT[s][:, h, :], start=True, stop=True)
                ins.then_inc(s_Sps, 1)

            def m_back(c, s):
                pe.wait_ge(s_stage, c * 2 + 2)
                pe.wait_ge(s_w, c + 2)
                pe.wait_ge(s_h, c + 1)
                pe.wait_ge(s_C, c + 1)
                for h in range(MH):
                    out = ps[:, 5 + h // 2, (h % 2) * (DV + 1):(h % 2 + 1) * (DV + 1)]
                    nc.tensor.matmul(out, wgt[s][:, h, :], vone[s][:, h, :], start=True, stop=False)
                    nc.tensor.matmul(out, qeT[s][:, h, :], Cst[:, h, :], start=False, stop=True)
                for h in range(MH):
                    out = ps[0:DQK, 7, h * (DV + 1):(h + 1) * (DV + 1)] if h < 3 else ps[0:DQK, 6, 2 * (DV + 1):3 * (DV + 1)]
                    ins = nc.tensor.matmul(out, ke[s][:, h, :], vone[s][:, h, :], start=True, stop=True)
                ins.then_inc(s_st, 1)
            m_front(0, 0)
            m_scores(0, 0)
            with pe.Fori(0, NT // 2 - 1) as i:
                for s in range(2):
                    m_front(i * 2 + (s + 1), 1 - s)
                    m_back(i * 2 + s, s)
                    m_scores(i * 2 + (s + 1), 1 - s)
            m_front(NT - 1, 1)
            m_back(NT - 2, 0)
            m_scores(NT - 1, 1)
            m_back(NT - 1, 1)
            for c in range(NT):
                pe.wait_ge(s_y, c + 1)
                pe.wait_ge(s_C, NT + 1)
                if c >= 4:
                    pe.wait_ge(s_ya, c - 3)
                for h in range(MH):
                    ins = nc.tensor.transpose(ps[:, c % 4, h * P:(h + 1) * P], Pm[:, c, 512 + h * DV:512 + (h + 1) * DV], ident)
                ins.then_inc(s_yT, 1)
            pe.wait_ge(s_ya, NT)
            for j in range(4):
                lo = C_KV + (256, 512)[j // 2]
                for b in range(4):
                    ins = nc.tensor.transpose(ps[:, j, b * P:(b + 1) * P], Pm[:, (j % 2) * 4 + b, lo:lo + P], ident)
                ins.then_inc(s_kvps, 1)
            pe.wait_ge(s_cw, 1)
            pe.wait_ge(s_kvT, 4)
            for tile in range(NT):
                nc.tensor.matmul(ps[:, 0, 4 * tile:4 * tile + 4], kcw[:, tile, :], cst("block")[:, 28:32],
                                 start=True, stop=True)
            for tile in range(NT):
                ins = nc.tensor.matmul(ps[0:NCMP, 0, 64:64 + NKV * HD], cst("block")[:, 28 - 4 * tile:60 - 4 * tile],
                                       vcw[:, tile, :], start=(tile == 0), stop=(tile == NT - 1))
            ins.then_inc(s_cps, 1)
            pe.wait_ge(s_cT2, 2)
            pe.wait_ge(s_gts, 1)
            pe.sem_inc(s_qseen, 1)

            def att_S(u):
                kind, i, lo, blocks, _ = units[u]
                n = (i + 1 - lo) * P
                q = qTh[:, i * P:(i + 1) * P]
                kT_ = ksT if kind == "s" else kwT
                for c in range(0, n, 512):
                    w = min(512, n - c)
                    ins = nc.tensor.matmul(ps[:, 2 * (u % 2) + c // 512, 0:w], q, kT_[:, lo * P + c:lo * P + c + w],
                                           start=True, stop=True)
                if kind == "w":
                    ins = nc.tensor.matmul(ps[:, 2 * (u % 2) + 1, P:P + NCMP], q, kcT, start=True, stop=True)
                ins.then_inc(s_S, 1)

            def att_q(h, turn):
                pe.wait_ge(s_qst, h + 1)
                for j in range(2):
                    pe.wait_ge(s_ev[j], turn[j])
                    for b in range(4):
                        ins = nc.tensor.transpose(ps[:, 4 + j, b * P:(b + 1) * P], qst[:, 4 * j + b, :], ident)
                    ins.then_inc(s_pt[j], 1)
                pe.wait_ge(s_pt[0], turn[0])
                pe.wait_ge(s_pt[1], turn[1])

            def att_T(u, h):
                pe.wait_ge(s_scaled, h * NU + (u + 1))
                for (b, turn), grp in zip(groups[u], units[u][4]):
                    pe.wait_ge(s_ev[b], h * GN[b] + (turn + 2))
                    for o, (c, w, _) in enumerate(grp):
                        ins = nc.tensor.transpose(ps[0:w, 4 + b, o * P:(o + 1) * P], pbuf[u % 2][:, c:c + w], ident)
                    ins.then_inc(s_pt[b], 1)

            def att_PV(u, h, g):
                kind, i, lo, blocks, _ = units[u]
                for b, turn in groups[u]:
                    pe.wait_ge(s_ev[b], h * GN[b] + (turn + 3))
                if kind == "w":
                    pe.wait_ge(s_comb, h * NT + max(i, 1))
                for o, (c, w, b) in enumerate(blocks):
                    src = ptbuf[u % 2][0:w, o * P:(o + 1) * P]
                    if b is None:
                        v = vc[:, g * HD:(g + 1) * HD]
                    else:
                        vlo = C_KV + (384 if kind == "s" else 640) + g * HD
                        v = Pm[:, b, vlo:vlo + HD]
                    ins = nc.tensor.matmul(ps[0:HD, 6 + i % 2, 0:P], v, src, start=(kind == "w" and o == 0),
                                           stop=(kind == "s" and b == i))
                ins.then_inc(s_pv, 1)

            att_q(0, (1, 1))
            pe.wait_ge(s_ev[0], 2)
            pe.wait_ge(s_ev[1], 2)
            pe.sem_inc(s_qseen, 1)
            att_S(0)
            att_S(1)
            for g in range(NKV):
                with pe.Fori(g * HPG, (g + 1) * HPG) as h:
                    for u in range(NU):
                        if u == NU - 1:
                            att_q(h + 1, [h * GN[b] + (q_turn[b] + 2) for b in range(2)])
                        att_T(u, h)
                        if u + 2 < NU:
                            att_S(u + 2)
                        if u:
                            att_PV(u - 1, h, g)
                        if u == NU - 1:
                            for b in range(2):
                                pe.wait_ge(s_ev[b], h * GN[b] + (q_turn[b] + 3))
                            pe.sem_inc(s_qseen, 1)
                            att_S(0)
                            att_PV(u, h, g)
                            att_S(1)
            pe.wait_ge(s_sWd, 1)
            pe.wait_ge(s_ybd, 16 * (NH + 1))
            nc.tensor.matmul(ps[0:32, 0, 0:DV + 2], cst("quarter"), sW, start=True, stop=True).then_inc(s_sWp, 1)
            for h in range(NH):
                nc.tensor.transpose(ps[0:HD, 1, h * NS:(h + 1) * NS], Ps[:, C_NQ + h * HD:C_NQ + (h + 1) * HD], ident[0:NS, 0:NS])
            for j in range(2):
                lo = C_KV + 256 * (j + 1)
                ins = nc.tensor.transpose(ps[:, 1, 64 + j * NS:64 + (j + 1) * NS], Ps[:, lo:lo + P], ident[0:NS, 0:NS])
            ins.then_inc(s_Qps, 1)
            pe.wait_ge(s_sh2, 2)
            nc.tensor.transpose(ps[:, 2, 0:32], hv, ident[0:32, 0:32]).then_inc(s_syT, 1)
            pe.wait_ge(s_Qall, 1)
            pe.wait_ge(s_sya, 1)
            pe.wait_ge(s_zero, 1)
            for j in range(2):
                nc.tensor.matmul(ps[0:SR, 3, j * NS:(j + 1) * NS], Qall.rearrange("p b h -> p (b h)"), knT[:, j, :],
                                 start=True, stop=True)
            for bank in range(3):
                nc.tensor.matmul(ps[0:SR, bank, :], ones[0:1, 0:SR], zrow, start=True, stop=False)
            nc.tensor.matmul(ps[0:SR, 3, 64:64 + NCMP], ones[0:1, 0:SR], zrow[:, 0:NCMP], start=True, stop=False)
            pe.sem_inc(s_free, 2)
            with pe.Fori(0, NS // 2) as i:
                for s in range(2):
                    pe.wait_ge(s_ldk[s], i * 272 + 272)
                    for j in range(NPAGE):
                        ins = nc.tensor.transpose(ps[:, 4 + j // 4, (j % 4) * P:(j % 4 + 1) * P], pg_slc[s][:, j, :], ident)
                    ins.then_inc(s_pgps, 1)
                    for j in range(WIN // P):
                        nc.tensor.transpose(ps[:, 6, j * P:(j + 1) * P], pg_win[s][:, j, :], ident)
                    pe.wait_ge(s_cmul, i * 2 + (s + 1))
                    for j in range(NPAGE):
                        nc.tensor.matmul(ps[:, 7, 4 * j:4 * j + 4], pg_cmp[s][:, j, 0:P], cst("block")[:, 28:32],
                                         start=True, stop=True)
                    for j in range(NPAGE):
                        ins = nc.tensor.matmul(ps[0:NCMP, 7, 64:64 + P], cst("block")[:, 28 - 4 * j:60 - 4 * j],
                                               pg_cmp[s][:, j, P:2 * P], start=(j == 0), stop=(j == NPAGE - 1))
                    ins.then_inc(s_pgps, 1)
                    pe.wait_ge(s_pga, i * 2 + (s + 1))
                    pe.wait_ge(s_pgd, i * 2 + (s + 1))
                    pe.wait_ge(s_qp, i * 2 + (s + 1))
                    Q2 = Qpad.rearrange("p b h -> p (b h)")
                    for j in range(2):
                        nc.tensor.matmul(ps[0:SR, j, :], Q2, pT[:, j * 512:(j + 1) * 512], start=False, stop=False)
                    nc.tensor.matmul(ps[0:SR, 2, :], Q2, wT, start=False, stop=False)
                    nc.tensor.matmul(ps[0:SR, 3, 64:64 + NCMP], Q2, ckT, start=False, stop=False).then_inc(s_free, 1)
            for bank in range(3):
                nc.tensor.matmul(ps[0:SR, bank, :], ones[0:1, 0:SR], zrow, start=False, stop=True)
            nc.tensor.matmul(ps[0:SR, 3, 64:64 + NCMP], ones[0:1, 0:SR], zrow[:, 0:NCMP], start=False, stop=True).then_inc(s_soft, 1)
            pe.wait_ge(s_soft, 2)
            nc.tensor.matmul(ps[0:SR, 7, 0:NCMP], cst("same_group", SR), pcm, start=True, stop=True).then_inc(s_impps, 1)
            pe.wait_ge(s_soft, 3)
            for j in range(NPAGE):
                nc.tensor.transpose(ps[:, 4, j * SR:(j + 1) * SR], Ssl[:, j * P:(j + 1) * P], ident[0:SR, 0:SR])
            for j in range(WIN // P):
                nc.tensor.transpose(ps[:, 5, j * SR:(j + 1) * SR], Swn[:, j * P:(j + 1) * P], ident[0:SR, 0:SR])
            nc.tensor.transpose(ps[0:NCMP, 5, 256:320], Scm, ident[0:SR, 0:SR])
            nc.tensor.transpose(ps[0:NS, 5, 320:384], Ssl[:, PAST:], ident[0:SR, 0:SR])
            nc.tensor.transpose(ps[0:NS, 5, 384:448], Swn[:, WIN:], ident[0:SR, 0:SR]).then_inc(s_sPT, 1)
            pe.wait_ge(s_sPTe, 2)
            O = ps[:, 6, 0:SR]
            nc.tensor.matmul(O, Ps[:, C_KV + 384:C_KV + 512], PTw[0:NS, 320:384], start=True, stop=False)
            nc.tensor.matmul(O, Ps[:, C_KV + 640:C_KV + 768], PTw[0:NS, 384:448], start=False, stop=False)
            for b in range(NS):
                nc.tensor.matmul(ps[:, 6, b * NH:(b + 1) * NH], vcs[:, b, :], PTw[0:NCMP, 256 + b * NH:256 + (b + 1) * NH],
                                 start=False, stop=False, skip_group_check=True)
            with pe.Fori(0, NS // 2) as i:
                for s in range(2):
                    pe.wait_ge(s_ldv[s], i * 144 + 144)
                    out = ps[:, 6, bass.ds(i * 16 + s * NH, NH)]
                    for j in range(NPAGE):
                        nc.tensor.matmul(out, pg_slc[s][:, j, :], PTs[:, 0, bass.ds(i * 16 + (j * SR + s * NH), NH)],
                                         start=False, stop=False, skip_group_check=True)
                    for j in range(WIN // P):
                        ins = nc.tensor.matmul(out, pg_win[s][:, j, :], PTw[:, bass.ds(i * 16 + (j * SR + s * NH), NH)],
                                               start=False, stop=False, skip_group_check=True)
                    ins.then_inc(s_free, 1)
            nc.tensor.matmul(O, ones[0:1, :], zrow[:, 0:SR], start=False, stop=True).then_inc(s_Osum, 1)
            pe.wait_ge(s_yb, 1)
            pe.wait_ge(s_Osum, 1)

            def chain(bank, w, k0, kn, src, q):
                for k in range(kn):
                    ins = nc.tensor.matmul(ps[:, bank, 0:TG], w[:, k0 + k, :], src[:, k, q * TG:(q + 1) * TG],
                                           start=(k == 0), stop=(k == kn - 1))
                return ins
            with pe.Fori(0, 2) as i:
                for s in range(2):
                    pe.wait_ge(s_wmg[s], i * 64 + 64)
                    for m in range(2):
                        for q in range(3):
                            u = (s * 2 + m) * 3 + q
                            pe.wait_ge(s_mgdve, i * 12 + (u + 1))
                            w = wmg[s][:, :, m * P:(m + 1) * P]
                            b = 4 * (u % 2)
                            chain(b, w, 0, 8, hT, q)
                            chain(b + 1, w, 8, 8, hT, q)
                            chain(b + 2, w, 16, 4, yaT, q)
                            ins = chain(b + 3, w, 20, 4, ybT, q)
                            ins.then_inc(s_mgps, 1)
                    pe.wait_ge(s_mgps, i * 12 + (s * 6 + 6))
                    pe.sem_inc(s_mgused, 1)
            pe.wait_ge(s_mgdve, 26)
            with pe.Fori(0, 2) as i:
                for s in range(2):
                    pe.wait_ge(s_wl[s], i * 16 + 16)
                    for u in range(6):
                        pe.wait_ge((s_woact, s_wodve)[u % 2], i * 6 + (s * 3 + u // 2 + 1))
                        chain(u, wot[s][:, :, (u // 3) * P:(u // 3 + 1) * P], 0, 8, merT, u % 3).then_inc(s_wops, 1)
                    pe.wait_ge(s_wops, i * 12 + (s * 6 + 6))
                    pe.sem_inc(s_woused, 1)

            def post_pe(rnd, gg, src):
                pe.wait_ge(s_diag, rnd + 1)
                for j in range(2):
                    nc.tensor.matmul(ps[:, 4 + j, :], ones[:, :], diag[rnd][:, j * 512:(j + 1) * 512], start=True, stop=True)
                for k in range(KD):
                    ins = nc.tensor.transpose(ps[0:NS, 6 + k // 4, (k % 4) * P:(k % 4 + 1) * P], gg[:, k, 1:9], ident)
                ins.then_inc(s_Gps, 1)
                for n in range(NT + 1):
                    r = P if n < NT else NS
                    if n >= 2:
                        pe.wait_ge(s_ytdve, (NT + 1) * rnd + n - 1)
                    for k in range(KD):
                        ins = nc.tensor.transpose(ps[0:r, 2 * (n % 2) + k // 4, (k % 4) * P:(k % 4 + 1) * P],
                                                  src[:, k, n * P:n * P + r], ident)
                    ins.then_inc(s_ytps, 1)
            pe.wait_ge(s_woact, 15)
            pe.wait_ge(s_wodve, 15)
            post_pe(0, gg1, yT1)
            pe.wait_ge(s_ytdve, NT + 1)
            h_pe(1)
            def chain3(bank, s, k0, q):
                for k in range(KD):
                    toks = slice(q * TG, (q + 1) * TG)
                    for j, (w, h) in enumerate(((wup_hi[s], h_hi), (wup_hi[s], h_lo), (wup_lo[s], h_hi))):
                        ins = nc.tensor.matmul(ps[:, bank, 0:TG], w[:, k0 + k, :], h[:, k, toks],
                                               start=(k == 0 and j == 0), stop=(k == KD - 1 and j == 2))
                return ins
            pe.wait_ge(s_hsplit, NT + 3)
            with pe.Fori(0, KF // 2) as i:
                for s in range(2):
                    pe.wait_ge(s_wlo, i * 2 + (s + 1))
                    for q in range(3):
                        u = s * 3 + q
                        pe.wait_ge(s_updve, i * 6 + (u + 1))
                        chain3(2 * q, s, 0, q)
                        chain3(2 * q + 1, s, 8, q).then_inc(s_upps, 1)
                    pe.wait_ge(s_upps, i * 6 + (s * 3 + 3))
                    pe.sem_inc(s_upused, 1)
            pe.wait_ge(s_updve, 3 * KF + 2)
            with pe.Fori(0, KD // 2) as i:
                for s in range(2):
                    pe.wait_ge(s_wl[s], i * 16 + (DN0 + 16))
                    for q in range(3):
                        u = s * 3 + q
                        pe.wait_ge((s_woact, s_wodve)[u % 2], i * 3 + (12 + u // 2 + 1))
                        chain(u, wdn[s], 0, KF, aT, q).then_inc(s_wops, 1)
                    pe.wait_ge(s_wops, i * 6 + (24 + s * 3 + 3))
                    pe.sem_inc(s_woused, 1)
            pe.wait_ge(s_woact, 27)
            pe.wait_ge(s_wodve, 27)
            post_pe(1, gg2, hT)


_INS = ["x_prompt", "x_sample", "c_prompt", "c_sample", "cache_cmp_kv", "cache_slc_kv", "cache_win_kv",
        "state_mlstm_C", "state_mlstm_n", "state_mlstm_m", "page_table", "g_pre_mix", "g_post_mix", "g_pre_ffn",
        "g_post_ffn", "w_ada", "b_ada", "w_in", "b_in", "mlstm_norm_w", "w_cmp_k", "w_cmp_v", "w_proj_a", "w_proj_b",
        "w_out", "w_up", "w_down"]
_KV = (2, NKV, HD)
_OUTS = [(1, SEQ, D), (NS, 1, D), (1, 1, SEQ) + _KV, (1, 1, SEQ) + _KV, (1, 1, WIN) + _KV,
         (1, 1, MH, DQK, DV), (1, 1, MH, DQK), (1, 1, MH),
         (1, NS, 1) + _KV, (1, NS, 1) + _KV, (1, NS, WIN) + _KV,
         (1, NS, MH, DQK, DV), (1, NS, MH, DQK), (1, NS, MH)]


def kernel(**inputs):
    import concourse.bacc as _bacc
    from concourse.bass_utils import run_bass_kernel_spmd as _run

    nc = _bacc.Bacc("TRN2", target_bir_lowering=False, num_devices=1)
    arrays, args = {}, {}
    for name in _INS + ["const"]:
        a = CONST if name == "const" else np.ascontiguousarray(inputs[name])
        arrays[f"in_{name}"] = a
        args[name] = nc.dram_tensor(f"in_{name}", a.shape, mybir.dt.from_np(a.dtype), kind="ExternalInput").ap()
    outs = [nc.dram_tensor(f"out_{i}", shape, F32, kind="ExternalOutput").ap() for i, shape in enumerate(_OUTS)]
    build(nc, args, outs)
    r = _run(nc, [arrays], core_ids=[0])
    return tuple(r.results[0][f"out_{i}"] for i in range(len(_OUTS)))
```
